# Optimizing a Trainium2 kernel written in Bass

```python
import jax, jax.numpy as jnp
from jax import lax
import numpy as np

D_MODEL = 1024
BATCH = 1
SEQ = 1024
DEPTH = 1

CHUNK = 64
Q_BLOCK = 128
PLE_DIM = 256
GLA_HEADS = 4
GLA_DK = D_MODEL // 8
GLA_DV = D_MODEL // 4
GLA_LOWRANK = 16
GLA_TAU = 16.0
SB_HEADS = 8
SB_DH = D_MODEL // 8
GLA_QK = GLA_HEADS * GLA_DK
GLA_V = GLA_HEADS * GLA_DV
SB_W = SB_HEADS * SB_DH
EPS = 1e-6

kernel_name = "hybrid_gla_stickbreak_gated_block"

def _split_sizes():
    return [GLA_QK, GLA_QK, GLA_V, GLA_LOWRANK, GLA_V, SB_W, SB_W, SB_W, SB_W, D_MODEL, D_MODEL]

def _d_in():
    return sum(_split_sizes())

def rmsnorm(x, g):
    xf = x.astype(jnp.float32)
    y = xf * lax.rsqrt(jnp.mean(xf * xf, axis=-1, keepdims=True) + EPS)
    return (y * g.astype(jnp.float32)).astype(x.dtype)

def gla_mixer(q, k, v, log_a):
    B, S, H, dk = q.shape
    dv = v.shape[-1]
    n = S // CHUNK

    def to_chunks(t):
        return t.reshape(B, n, CHUNK, H, t.shape[-1]).transpose(1, 0, 3, 2, 4)

    qc = to_chunks(q.astype(jnp.float32) * (dk ** -0.5))
    kc = to_chunks(k.astype(jnp.float32))
    vc = to_chunks(v.astype(jnp.float32))
    bc = jnp.cumsum(to_chunks(log_a.astype(jnp.float32)), axis=3)
    causal = jnp.tril(jnp.ones((CHUNK, CHUNK), dtype=bool))

    def step(state, inp):
        q_, k_, v_, b_ = inp
        eb, enb = jnp.exp(b_), jnp.exp(-b_)
        qd, kd = q_ * eb, k_ * enb
        qi, ki = q_ * enb, k_ * eb
        a_past = jnp.einsum('bhtd,bhsd->bhts', qd, kd)
        a_fut = jnp.einsum('bhtd,bhsd->bhts', qi, ki)
        attn = jnp.where(causal, a_past, a_fut)
        o = jnp.einsum('bhts,bhsv->bhtv', attn, v_) + jnp.einsum('bhtd,bhdv->bhtv', qd, state)
        b_last = b_[:, :, -1:, :]
        k_end = k_ * jnp.exp(b_last - b_)
        state = state * jnp.exp(b_last)[:, :, 0, :, None] + jnp.einsum('bhsd,bhsv->bhdv', k_end, v_)
        return state, o

    state0 = jnp.zeros((B, H, dk, dv), jnp.float32)
    _, o = lax.scan(step, state0, (qc, kc, vc, bc))
    return o.transpose(1, 0, 3, 2, 4).reshape(B, S, H, dv)

def stick_breaking(q, k, v):
    B, S, H, d = q.shape
    nb = S // Q_BLOCK
    qb = q.reshape(B, nb, Q_BLOCK, H, d).transpose(1, 0, 3, 2, 4)
    kt = k.transpose(0, 2, 1, 3)
    vt = v.transpose(0, 2, 1, 3)
    key_pos = jnp.arange(S)
    scale = d ** -0.5

    def block(args):
        qblk, i = args
        z = jnp.einsum('bhtd,bhsd->bhts', qblk, kt).astype(jnp.float32) * scale
        q_pos = i * Q_BLOCK + jnp.arange(Q_BLOCK)
        mask = key_pos[None, :] < q_pos[:, None]
        log_1m = jnp.where(mask, jax.nn.log_sigmoid(-z), 0.0)
        after = lax.cumsum(log_1m, axis=3, reverse=True) - log_1m
        w = jnp.where(mask, jnp.exp(jax.nn.log_sigmoid(z) + after), 0.0)
        return jnp.einsum('bhts,bhsd->bhtd', w.astype(vt.dtype), vt)

    o = lax.map(block, (qb, jnp.arange(nb)))
    return o.transpose(1, 0, 3, 2, 4).reshape(B, S, H, d)

def setup_inputs(seed: int = 0) -> dict:
    key = jax.random.key(seed)
    ks = jax.random.split(key, 16)
    d_in = _d_in()
    f32 = jnp.float32

    def nrm(k, shape, fan_in):
        return jax.random.normal(k, shape, f32) * (fan_in ** -0.5)

    def gain(k, shape):
        return 1.0 + 0.05 * jax.random.normal(k, shape, f32)

    return {
        "x": jax.random.normal(ks[0], (BATCH, SEQ, D_MODEL), f32),
        "p": jax.random.normal(ks[1], (DEPTH, BATCH, SEQ, PLE_DIM), f32),
        "g_mix": gain(ks[2], (DEPTH, D_MODEL)),
        "w_in": nrm(ks[3], (DEPTH, D_MODEL, d_in), D_MODEL),
        "w_alpha": nrm(ks[4], (DEPTH, GLA_LOWRANK, GLA_QK), GLA_LOWRANK),
        "b_alpha": 0.5 + 0.1 * jax.random.normal(ks[5], (DEPTH, GLA_QK), f32),
        "g_gla_out": gain(ks[6], (DEPTH, GLA_HEADS, GLA_DV)),
        "w_out_gla": nrm(ks[7], (DEPTH, GLA_V, D_MODEL), GLA_V),
        "w_out_sb": nrm(ks[8], (DEPTH, SB_W, D_MODEL), SB_W),
        "w_out": nrm(ks[9], (DEPTH, D_MODEL, D_MODEL), D_MODEL),
        "g_ple": gain(ks[10], (DEPTH, D_MODEL)),
        "w_ple_gate": nrm(ks[11], (DEPTH, D_MODEL, D_MODEL), D_MODEL),
        "w_ple": nrm(ks[12], (DEPTH, PLE_DIM, D_MODEL), PLE_DIM),
        "g_final": gain(ks[13], (D_MODEL,)),
    }

def reference(x, p, g_mix, w_in, w_alpha, b_alpha, g_gla_out, w_out_gla, w_out_sb, w_out,
              g_ple, w_ple_gate, w_ple, g_final):
    B, S, _ = x.shape
    sizes = _split_sizes()
    points = []
    acc = 0
    for s_ in sizes[:-1]:
        acc += s_
        points.append(acc)
    for i in range(DEPTH):
        h = rmsnorm(x, g_mix[i])
        z = jnp.einsum('bsd,de->bse', h, w_in[i])
        (q_a, k_a, v_a, lr_a, gate_a, q_b, k_b, v_b, gate_b, m_a, m_b) = jnp.split(z, points, axis=-1)

        log_a = jax.nn.log_sigmoid(
            (jnp.einsum('bsr,re->bse', lr_a, w_alpha[i]) + b_alpha[i]).astype(jnp.float32)) / GLA_TAU
        o_a = gla_mixer(q_a.reshape(B, S, GLA_HEADS, GLA_DK),
                        k_a.reshape(B, S, GLA_HEADS, GLA_DK),
                        v_a.reshape(B, S, GLA_HEADS, GLA_DV),
                        log_a.reshape(B, S, GLA_HEADS, GLA_DK))
        o_a = rmsnorm(o_a, g_gla_out[i]).astype(x.dtype).reshape(B, S, GLA_V)
        y_a = jnp.einsum('bse,ed->bsd', o_a * jax.nn.silu(gate_a), w_out_gla[i])

        o_b = stick_breaking(q_b.reshape(B, S, SB_HEADS, SB_DH),
                             k_b.reshape(B, S, SB_HEADS, SB_DH),
                             v_b.reshape(B, S, SB_HEADS, SB_DH)).reshape(B, S, SB_W)
        y_b = jnp.einsum('bse,ed->bsd', o_b * jax.nn.silu(gate_b), w_out_sb[i])

        merged = jax.nn.sigmoid(m_a) * y_a + jax.nn.sigmoid(m_b) * y_b
        x = x + jnp.einsum('bsd,de->bse', merged, w_out[i])

        u = rmsnorm(x, g_ple[i])
        gate_p = jax.nn.sigmoid(jnp.einsum('bsd,de->bse', u, w_ple_gate[i]))
        x = x + gate_p * jnp.einsum('bsp,pd->bsd', p[i], w_ple[i])
    return rmsnorm(x, g_final)


_drawn_inputs = setup_inputs


def setup_inputs(seed=0):
    import zlib

    import numpy as np

    out = dict(_drawn_inputs(seed))
    spreads = {}
    factors = {'b_alpha': 4.586, 'g_gla_out': 3.976, 'g_ple': 20.903}
    for name, (base, spread) in spreads.items():
        noise = np.random.default_rng([zlib.crc32(name.encode()), seed]).standard_normal(out[name].shape)
        drawn = base * np.exp(spread * noise) if base else spread * noise
        out[name] = __import__('jax').numpy.asarray(drawn.astype(out[name].dtype))
    for name, factor in factors.items():
        out[name] = (out[name] * factor).astype(out[name].dtype)
    return out
```

```python
from contextlib import ExitStack

import concourse.bass as bass
from concourse import mybir

F32 = mybir.dt.float32
F32R = mybir.dt.float32r
U32 = mybir.dt.uint32
ALU = mybir.AluOpType
ACT = mybir.ActivationFunctionType

P = 128
BANK = 512
CHUNK = 64
EPS = 1e-6
TAU = 16.0
EXP_LN = "natural_log_exp_and_others"
SIGMOID = "sigmoid_and_others"

HI, LO = 0, 1
PASSES = ((HI, HI), (HI, LO), (LO, HI))


def hybrid_block(nc, x, p, g_mix, w_in, w_alpha, b_alpha, g_gla_out, w_out_gla, w_out_sb, w_out, g_ple,
                 w_ple_gate, w_ple, g_final, out):
    T, D = x.shape[1], x.shape[2]
    TB, KD = T // P, D // P
    NH = T // BANK
    RANK, QKW = w_alpha.shape[1], w_alpha.shape[2]
    GH, DV = g_gla_out.shape[1], g_gla_out.shape[2]
    DK = QKW // GH
    SH = D // P
    PK = w_ple.shape[1] // P
    CPB = P // CHUNK
    assert DK == P and DV == 2 * P and CPB == 2 and NH == 2 and TB == 8 and KD == 8 and SH == 8
    Q_SCALE = float(P) ** -0.5

    widths = [QKW, QKW, GH * DV, RANK, GH * DV, D, D, D, D, D, D]
    QA, KA, VA, LR, GA, QB, KB, VB, GB, MA, MB = [sum(widths[:i]) for i in range(len(widths))]

    def by_k(w):
        return w.rearrange("(k p) n -> p k n", p=P)

    w_in_k, w_og_k, w_ob_k = by_k(w_in[0]), by_k(w_out_gla[0]), by_k(w_out_sb[0])
    w_out_k, w_pg_k, w_ple_k = by_k(w_out[0]), by_k(w_ple_gate[0]), by_k(w_ple[0])
    x_rows, p_rows, out_rows = x[0], p[0, 0], out[0]

    o_gla_d = nc.dram_tensor("o_gla_scratch", (D, T), F32, kind="Internal").ap()
    o_sb_d = nc.dram_tensor("o_sb_scratch", (D, T), F32, kind="Internal").ap()
    ya_d = nc.dram_tensor("ya_scratch", (D, T), F32, kind="Internal").ap()
    pe_d = nc.dram_tensor("pe_scratch", (T, D), F32, kind="Internal").ap()

    KB_ = 1024
    base = (nc.sbuf_base + 63) // 64 * 64

    def place(name, shape, dt, at):
        return nc.alloc_sbuf_tensor_at(name, shape, dt, offset=base + at)

    HT = place("HT", [P, 2, KD, T], F32R, 0)
    RAW = place("RAW", [P, 2, KD, P], F32, 64 * KB_)
    WS = place("WS", [P, 2, 2, KD, P], F32R, 72 * KB_)
    AREA = 88 * KB_
    MISC = 184 * KB_
    gains = place("gains", [P, 2, D], F32, MISC)
    ident = place("ident", [P, P], F32, MISC + 8192)
    before01 = place("before01", [P, P], F32, MISC + 8704)
    before_cap = place("before_cap", [P, P], F32, MISC + 9216)
    m_past = place("m_past", [P, P], F32, MISC + 9728)
    m_fut = place("m_fut", [P, P], F32, MISC + 10240)
    m_cross = place("m_cross", [P, P], F32, MISC + 10752)
    balp = place("balp", [P, GH], F32, MISC + 11264)
    ggla = place("ggla", [P, 2 * GH], F32, MISC + 11328)
    ssq = place("ssq", [P, TB], F32, MISC + 11392)
    lnm = place("lnm", [P, TB], F32, MISC + 11456)
    rstd = place("rstd", [P, TB], F32, MISC + 11520)
    two_c = place("two_c", [P, TB, 2], F32, MISC + 11584)
    two_k = place("two_k", [P, TB, 2], F32, MISC + 11648)
    dec = place("dec", [P, TB], F32, MISC + 11712)
    epsc = place("epsc", [P, 1], F32, MISC + 11776)
    lrT = place("lrT", [RANK, T], F32, MISC + 12288)
    walp = place("walp", [RANK, QKW], F32, MISC + 16384)
    xin = place("xin", [P, TB, D], F32, AREA)
    pin = place("pin", [P, TB, PK * P], F32, AREA + 32 * KB_)
    wpe_raw = place("wpe_raw", [P, PK, D], F32, AREA + 40 * KB_)
    wpe = place("wpe", [P, 2, PK, D], F32R, AREA + 48 * KB_)
    pT = place("pT", [P, 2, PK, T], F32R, AREA + 64 * KB_)
    pes = place("pes", [P, 2, BANK], F32, AREA + 80 * KB_)
    junk0 = place("junk0", [P, D], F32, AREA + 84 * KB_)
    qkv = place("qkv", [P, 4, T], F32, AREA)
    Y = place("Y", [P, GH, T], F32, AREA + 16 * KB_)
    A_ke = place("A_ke", [P, T], F32, AREA + 32 * KB_)
    A_eb = place("A_eb", [P, T], F32, AREA + 36 * KB_)
    A_enb = place("A_enb", [P, T], F32, AREA + 40 * KB_)
    A_qd = place("A_qd", [P, T], F32, AREA + 44 * KB_)
    A_kd = place("A_kd", [P, T], F32, AREA + 48 * KB_)
    A_qi = place("A_qi", [P, T], F32, AREA + 52 * KB_)
    A_ki = place("A_ki", [P, T], F32, AREA + 56 * KB_)
    VN = place("VN", [P, TB, DV], F32, AREA + 60 * KB_)
    KN = place("KN", [P, TB, DK], F32, AREA + 68 * KB_)
    oT = place("oT", [P, 2, T], F32, AREA + 72 * KB_)
    on = place("on", [P, 2, DV], F32, AREA + 80 * KB_)
    attn = place("attn", [P, 2, P], F32, AREA + 82 * KB_)
    St = place("St", [P, 2, DV], F32, AREA + 83 * KB_)
    junkA = place("junkA", [P, DV], F32, AREA + 85 * KB_)
    newchunk = place("newchunk", [P, T], F32, AREA + 86 * KB_)
    OA = place("OA", [P, 2, KD, T], F32R, AREA)
    SM = place("SM", [P, KD, T], F32, AREA + 64 * KB_)
    sg = place("sg", [P, 2, BANK], F32, AREA + 64 * KB_)
    oin = place("oin", [P, 2, T], F32, AREA + 68 * KB_)
    ys = place("ys", [P, 2, BANK], F32, MISC + 12288)
    yin = place("yin", [P, 2, BANK], F32, MISC + 16384)
    WT = place("WT", [P, 2, TB, BANK], F32R, AREA)
    QK = place("QK", [P, 2, 2, 2, T], F32R, AREA + 32 * KB_)
    VS = place("VS", [P, 2, TB, P], F32R, AREA + 64 * KB_)
    vT = place("vT", [P, T], F32, AREA + 72 * KB_)
    T1 = place("T1", [P, 2, T], F32, AREA + 76 * KB_)
    T2 = place("T2", [P, 2, T], F32, AREA + 84 * KB_)
    oS = place("oS", [P, 2, BANK], F32, AREA + 92 * KB_)
    WD = place("WD", [P, 2, 2, KD, BANK], F32R, AREA)
    x1 = place("x1", [P, TB, D], F32, AREA + 64 * KB_)
    u = place("u", [P, 2, D], F32, 72 * KB_)
    junkD = place("junkD", [P, D], F32, 80 * KB_)
    sgD = place("sgD", [P, 2, BANK], F32, 84 * KB_)
    pin2 = place("pin2", [P, 2, BANK], F32, MISC + 12288)

    with ExitStack() as ctx:
        def sem(name):
            return ctx.enter_context(nc.semaphore(name))

        def bank(name, n=1):
            return ctx.enter_context(nc.psum_tensor(name, [P, n * BANK], F32))

        pj = [bank("pj0"), bank("pj1")]
        z0 = bank("z0", 2)
        z1 = bank("z1", 2)
        trs = [bank("tr0"), bank("tr1")]
        zs = [z0, z1]
        SBK, OBK, UBK = z0[:, 0:BANK], [z0[:, BANK:2 * BANK], z1[:, 0:BANK]], z1[:, BANK:2 * BANK]
        PV = trs[1]

        phase_done = sem("phase_done")
        const_ready = sem("const_ready")
        params_in = sem("params_in")
        waits_passed = sem("waits_passed")
        gain_in, gain2_in, w_ple_in = sem("gain_in"), sem("gain2_in"), sem("w_ple_in")
        p_in, x_in = sem("p_in"), [sem(f"x_in{i}") for i in range(TB)]
        w_in_s = [sem("w_raw0"), sem("w_raw1")]
        w_hi, w_ready = sem("w_hi"), sem("w_ready")
        q_full = sem("q_full")

        def phase_end(eng, k):
            eng.drain().then_inc(phase_done, 1)
            eng.wait_ge(phase_done, 3 * (k + 1))

        def stand_alone(eng):
            eng.sem_inc(waits_passed, 1)

        def product(out_, lhs, rhs, blocks):
            steps = [(k, a, b) for k in range(blocks) for a, b in PASSES]
            for i, (k, a, b) in enumerate(steps):
                mm = nc.tensor.matmul(out_, lhs(a, k), rhs(b, k), start=i == 0, stop=i == len(steps) - 1)
            return mm

        N_A0, N_A = 1, 1 + 4 * GH
        N_FA = N_A + 3 * KD
        N_B = N_FA + 3 * SH
        N_FB = N_B + 3 * KD
        N_D = N_FB + 2 * KD
        GLA_SLICES = [(VA, DV), (VA + P, DV), (QA, P), (KA, P)]
        SB_SLICES = [(QB, P), (KB, P), (VB, P)]

        def col(off, step, i):
            return bass.ds(off + step * i, P)

        p_full, p_hi, p_lo = sem("p_full"), sem("p_hi"), sem("p_lo")
        wpe_hi, wpe_lo = sem("wpe_hi"), sem("wpe_lo")
        pe_full, pe_taken, pe_out = sem("pe_full"), sem("pe_taken"), [sem("pe_out0"), sem("pe_out1")]
        x_sq, x_ln, x_rstd, x_norm = sem("x_sq"), sem("x_ln"), sem("x_rstd"), sem("x_norm")
        xt_full, xt_hi, xt_lo = sem("xt_full"), sem("xt_hi"), sem("xt_lo")
        y_full, y_abs, y_min, y_exp, y_ln, y_ls, y_cum = [sem(n) for n in (
            "y_full", "y_abs", "y_min", "y_exp", "y_ln", "y_ls", "y_cum")]
        a_taken = sem("a_taken")
        chunk_mask = sem("chunk_mask")
        e_done, dd_done, ke_done, dec_part, dec_done, prep, kS_ready, qS_ready = [sem(n) for n in (
            "e_done", "dd_done", "ke_done", "dec_part", "dec_done", "prep", "kS_ready", "qS_ready")]
        g_tr_full, g_tr_taken = sem("g_tr_full"), sem("g_tr_taken")
        s_full, attn_part, attn_ready = sem("s_full"), sem("attn_part"), sem("attn_ready")
        u_full, st_ready = sem("u_full"), sem("st_ready")
        o_full, o_sq, o_ln, o_rstd, on_ready = [sem(n) for n in ("o_full", "o_sq", "o_ln", "o_rstd", "on_ready")]
        oT_out = sem("oT_out")
        b_hi, b_taken = sem("b_hi"), sem("b_taken")
        z_full, z_abs, z_exp, z_ln, sp, spm, cum, y_done, ym, w_done = [sem(n) for n in (
            "z_full", "z_abs", "z_exp", "z_ln", "sp", "spm", "cum", "y_done", "ym", "w_done")]
        b_tr_full, b_tr_hi, b_tr_lo = sem("b_tr_full"), sem("b_tr_hi"), sem("b_tr_lo")
        pv_full, pv_taken, ob_out = sem("pv_full"), sem("pv_taken"), [sem("ob_out0"), sem("ob_out1")]
        fin = {}
        for br in "AB":
            fin[br] = {n: sem(f"f{br}_{n}") for n in (
                "g_taken", "sg_ready", "og", "hi", "oa_ready", "oin0", "oin1", "m_taken", "y_taken", "ysum",
                "yhi", "ylo", "yio0", "yio1")}
        x2_in = [sem(f"x2_in{i}") for i in range(TB)]
        d_full, d1_taken, d3_taken = sem("d_full"), sem("d1_taken"), sem("d3_taken")
        u_sq, u_ln, u_rstd, u_ready = sem("u_sq"), sem("u_ln"), sem("u_rstd"), sem("u_ready")
        ut_full, ut_hi, ut_lo = sem("ut_full"), sem("ut_hi"), sem("ut_lo")
        pe_in, gate_used, x2_ready = [sem("pe_in0"), sem("pe_in1")], sem("gate_used"), sem("x2_ready")
        f_sq, f_ln, f_rstd, f_ready, out_done = sem("f_sq"), sem("f_ln"), sem("f_rstd"), sem("f_ready"), [
            sem("out_done0"), sem("out_done1")]

        def sb_rounds(i):
            if i < 2:
                return [], [("v", i, None, 4 * i, 4)]
            j = i - 2
            if j < 4:
                return [("w", 2 + j, j, 0, j + 1)], []
            return [("w", 6 + 2 * (j - 4), j, 0, 4)], [("w", 7 + 2 * (j - 4), j, 4, j - 3)]

        SB_ROUNDS = 14
        QUANTA_AT = {1: [0], 3: [1], 5: [2], 6: [3], 7: [4], 8: [5]}

        def z_pieces(i):
            w = (i + 1) * P
            first = (0, min(BANK, max(w, 2 * P)))
            return [first] + ([(BANK, max(w, BANK + 2 * P))] if w > BANK else [])

        block = ctx.enter_context(nc.Block())

        @block.sync
        def _(sp_eng):
            sy = sp_eng
            sy.dma_start(pin[:, :, :], p_rows.rearrange("(b t) d -> t b d", t=P)).then_inc(p_in, 16)
            sy.dma_start(wpe_raw[:, :, :], w_ple_k).then_inc(w_ple_in, 16)
            sy.dma_start(gains[:, 0, :], g_mix[0].partition_broadcast(P)).then_inc(gain_in, 16)
            for b in range(TB):
                sy.dma_start(xin[:, b, :], x_rows[b * P:(b + 1) * P, :]).then_inc(x_in[b], 16)

            def load(n, slot, src):
                sy.wait_ge(w_ready, n + 1)
                sy.dma_start(RAW[:, slot, :, :], src).then_inc(w_in_s[slot], 16)

            load(0, 0, w_in_k[:, :, LR:LR + P])
            sy.dma_start(walp[:, :], w_alpha[0]).then_inc(params_in, 16)
            with nc.allow_non_contiguous_dma(reason="two small per-channel vectors"):
                sy.dma_start(balp[:, :], b_alpha[0].rearrange("(h d) -> d h", d=P)).then_inc(params_in, 16)
                sy.dma_start(ggla[:, :], g_gla_out[0].rearrange("h (v d) -> d (h v)", d=P)).then_inc(params_in, 16)
            with sy.Fori(0, GH) as h:
                for c, (off, step) in enumerate(GLA_SLICES):
                    load(N_A0 + c + 4 * h, (N_A0 + c) % 2, w_in_k[:, :, col(off, step, h)])

            def finish(br, n0, gate_off, m_off, wo_k, o_d, stored):
                s = fin[br]
                for e_sem, v in stored:
                    sy.wait_ge(e_sem, v)
                sy.wait_ge(phase_done, 3 * (1 if br == "A" else 5) + 3)
                with sy.Fori(0, KD // 2) as j:
                    for par in range(2):
                        e = 2 * j + par
                        load(n0 + par + 2 * j, (n0 + par) % 2, w_in_k[:, :, col(gate_off, P, e)])
                        sy.wait_ge(s["oa_ready"], 2 * e + 2)
                        sy.dma_start(oin[:, par, :], o_d[bass.ds(P * e, P), :]).then_inc(s[f"oin{par}"], 16)
                with sy.Fori(0, KD // 2) as j:
                    for par in range(2):
                        load(n0 + KD + par + 2 * j, (n0 + par) % 2, w_in_k[:, :, col(m_off, P, 2 * j + par)])
                with sy.Fori(0, KD // 2) as j:
                    for par in range(2):
                        e = 2 * j + par
                        load(n0 + 2 * KD + par + 2 * j, (n0 + par) % 2, wo_k[:, :, col(0, P, e)])
                        if br == "B":
                            for hf in range(NH):
                                sy.wait_ge(s["ysum"], 2 * e + hf + 1)
                                sy.dma_start(yin[:, hf, :], ya_d[bass.ds(P * e, P), hf * BANK:(hf + 1) * BANK]
                                             ).then_inc(s[f"yio{hf}"], 16)

            finish("A", N_A, GA, MA, w_og_k, o_gla_d, [(oT_out, 16 * GH + 1)])
            with sy.Fori(0, SH // 2) as j:
                for par in range(2):
                    for c, (off, step) in enumerate(SB_SLICES):
                        n = N_FA + 3 * par + c
                        load(n + 6 * j, n % 2, w_in_k[:, :, col(off, step, 2 * j + par)])
            finish("B", N_B, GB, MB, w_ob_k, o_sb_d, [(ob_out[0], 16 * SH + 1), (ob_out[1], 16 * SH + 1)])

            sy.dma_start(gains[:, 0, :], g_ple[0].partition_broadcast(P)).then_inc(gain2_in, 16)
            sy.dma_start(gains[:, 1, :], g_final.partition_broadcast(P)).then_inc(gain2_in, 16)
            for m in range(2 * KD):
                w, c = (w_out_k, m) if m < KD else (w_pg_k, m - KD)
                load(N_FB + m, (N_FB + m) % 2, w[:, :, c * P:(c + 1) * P])
                if m == 1:
                    sy.wait_ge(phase_done, 3 * 9)
                    for b in range(TB):
                        sy.dma_start(x1[:, b, :], x_rows[b * P:(b + 1) * P, :]).then_inc(x2_in[b], 16)
            for q in range(2 * TB):
                ch, b = divmod(q, TB)
                if q >= 2:
                    sy.wait_ge(gate_used, q - 1)
                sy.dma_start(pin2[:, q % 2, :], pe_d[b * P:(b + 1) * P, ch * BANK:(ch + 1) * BANK]
                             ).then_inc(pe_in[q % 2], 16)

        @block.gpsimd
        def _(pool):
            g = nc.gpsimd
            g.sem_inc(w_ready, 2)
            steps = []

            def one(ins):
                steps.append(ins)
                ins.then_inc(const_ready, 1)
                pool.wait_ge(const_ready, len(steps))

            one(g.memset(ident[:, :], 0.0))
            one(g.affine_select(out=ident[:, :], in_=ident[:, :], compare_op=ALU.not_equal, fill=1.0, base=0,
                                pattern=[[-1, P]], channel_multiplier=1))
            one(g.memset(before01[:, :], 1.0))
            one(g.affine_select(out=before01[:, :], in_=before01[:, :], compare_op=ALU.is_gt, fill=0.0, base=0,
                                pattern=[[-1, P]], channel_multiplier=1))
            one(g.memset(before_cap[:, :], 3e38))
            one(g.affine_select(out=before_cap[:, :], in_=before_cap[:, :], compare_op=ALU.is_gt, fill=-1e30, base=0,
                                pattern=[[-1, P]], channel_multiplier=1))
            one(g.memset(m_past[:, :], 1.0))
            one(g.affine_select(out=m_past[:, :], in_=m_past[:, :], compare_op=ALU.is_ge, fill=0.0, base=0,
                                pattern=[[1, P]], channel_multiplier=-1))
            one(g.memset(m_past[0:CHUNK, CHUNK:P], 0.0))
            one(g.memset(m_fut[:, :], 1.0))
            one(g.affine_select(out=m_fut[:, :], in_=m_fut[:, :], compare_op=ALU.is_gt, fill=0.0, base=0,
                                pattern=[[-1, P]], channel_multiplier=1))
            one(g.memset(m_fut[CHUNK:P, 0:CHUNK], 0.0))
            one(g.memset(m_cross[:, :], 0.0))
            one(g.memset(m_cross[0:CHUNK, CHUNK:P], 1.0))
            one(g.memset(two_c[:, :, :], 1.0))
            one(g.memset(two_k[:, :, :], 1.0))
            one(g.memset(epsc[:, :], EPS))

            def split(n, half_n, slot, hi, lo):
                pool.wait_ge(w_in_s[slot], 16 * half_n + 16)
                stand_alone(pool)
                g.tensor_scalar(hi, RAW[:, slot, :, :], 1.0, 1.0, ALU.mult, ALU.mult).then_inc(w_hi, 1)
                pool.wait_ge(w_hi, n + 1)
                g.tensor_tensor(lo, RAW[:, slot, :, :], hi.bitcast(F32), ALU.subtract).then_inc(w_ready, 1)

            def split_ring(n, half_n, slot):
                pool.wait_ge(q_full, 2 * n + 2)
                split(n, half_n, slot, WS[:, slot, HI, :, :], WS[:, slot, LO, :, :])

            with pool.Fori(0, N_FB // 2) as j:
                for par in range(2):
                    split_ring(2 * j + par, j, par)
            if N_FB % 2:
                split_ring(N_FB - 1, N_FB // 2, 0)
            pool.wait_ge(phase_done, 3 * 9)
            for m in range(2 * KD):
                n, half = N_FB + m, m // 4
                if half >= 2:
                    pool.wait_ge(d_full, TB * (half - 1))
                c = m % 4
                split(n, n // 2, n % 2, WD[:, half % 2, HI, :, c * P:(c + 1) * P],
                      WD[:, half % 2, LO, :, c * P:(c + 1) * P])

        @block.tensor
        def _(pe):
            t = nc.tensor
            pe.sem_inc(q_full, 4)
            pe.sem_inc(o_full, 2)
            pe.sem_inc(g_tr_full, 2)
            pe.sem_inc(pv_full, 1)

            pe.wait_ge(const_ready, 17)
            pe.wait_ge(p_in, 16)
            for r in range(TB // 2):
                if r >= 2:
                    pe.wait_ge(p_lo, r - 1)
                for j in range(4):
                    k, b = j // 2, 2 * r + j % 2
                    mm = t.transpose(trs[r % 2][:, j * P:(j + 1) * P], pin[:, b, k * P:(k + 1) * P], ident[:, :])
                mm.then_inc(p_full, 1)
            pe.wait_ge(wpe_lo, 1)
            for b in range(TB):
                pe.wait_ge(p_lo, b // 2 + 1)
                for ch in range(NH):
                    q = 2 * b + ch
                    if q >= 2:
                        pe.wait_ge(pe_taken, q - 1)
                    product(pj[q % 2][:, :], lambda a, k: pT[:, a, k, b * P:(b + 1) * P],
                            lambda a, k: wpe[:, a, k, ch * BANK:(ch + 1) * BANK], PK).then_inc(pe_full, 1)
            pe.wait_ge(p_lo, TB // 2)
            for b in range(TB):
                pe.wait_ge(x_norm, b + 1)
                for r2 in range(2):
                    r = 2 * b + r2
                    if r >= 2:
                        pe.wait_ge(xt_lo, r - 1)
                    for j in range(4):
                        k = 4 * r2 + j
                        mm = t.transpose(trs[r % 2][:, j * P:(j + 1) * P], xin[:, b, k * P:(k + 1) * P], ident[:, :])
                    mm.then_inc(xt_full, 1)
            phase_end(pe, 0)

            def quantum(n, slot, hf, rhs, taken, q):
                if hf == 0:
                    pe.wait_ge(w_ready, n + 3)
                pe.wait_ge(taken, q + 1)
                product(pj[hf][:, :], lambda a, k: WS[:, slot, a, k, :],
                        lambda a, k: rhs[:, a, k, hf * BANK:(hf + 1) * BANK], KD).then_inc(q_full, 1)

            pe.sem_inc(a_taken, 2)
            pe.sem_inc(g_tr_taken, 2)
            for hf in range(NH):
                quantum(0, 0, hf, HT, a_taken, hf)
            pe.wait_ge(params_in, 48)
            pe.wait_ge(a_taken, 4)
            for r in range(2 * GH):
                h, hf = divmod(r, 2)
                if r >= 2:
                    pe.wait_ge(y_min, r - 1)
                t.matmul(trs[hf][:, :], walp[:, h * P:(h + 1) * P], lrT[:, hf * BANK:(hf + 1) * BANK],
                         start=True, stop=True).then_inc(y_full, 1)

            def gla_quantum(h, i):
                c, hf = divmod(i, 2)
                quantum(N_A0 + c + 4 * h, (N_A0 + c) % 2, hf, HT, a_taken, 2 + i + 8 * h)

            for i in range(8):
                gla_quantum(0, i)
            pe.wait_ge(y_min, 2 * GH)

            def gla_head(h, last):
                def tr_round(r):
                    pe.wait_ge(g_tr_taken, r + 1 + 14 * h)
                    return trs[r % 2]

                pe.wait_ge(a_taken, 8 + 8 * h)
                for r in range(4):
                    o = tr_round(r)
                    for j in range(4):
                        b, v = 2 * r + j // 2, j % 2
                        mm = t.transpose(o[:, j * P:(j + 1) * P], qkv[:, v, b * P:(b + 1) * P], ident[:, :])
                    mm.then_inc(g_tr_full, 1)
                if not last:
                    for i in range(4):
                        gla_quantum(h + 1, i)
                pe.wait_ge(kS_ready, h + 1)
                for r in range(4, 6):
                    o = tr_round(r)
                    for j in range(4):
                        b = 4 * (r - 4) + j
                        mm = t.transpose(o[:, j * P:(j + 1) * P], A_enb[:, b * P:(b + 1) * P], ident[:, :])
                    mm.then_inc(g_tr_full, 1)
                pe.wait_ge(qS_ready, h + 1)

                def turn(b):
                    o = tr_round(6 + b)
                    pe.wait_ge(on_ready, b + 3 + 8 * h)
                    for v in range(2):
                        mm = t.transpose(o[:, v * P:(v + 1) * P], on[:, b % 2, v * P:(v + 1) * P], ident[:, :])
                    mm.then_inc(g_tr_full, 1)

                for b in range(TB):
                    cols = slice(b * P, (b + 1) * P)
                    pe.wait_ge(attn_ready, b + 1 + 8 * h)
                    t.matmul(SBK[:, 0:P], A_kd[:, cols], A_qd[:, cols], start=True, stop=True)
                    t.matmul(SBK[:, P:2 * P], A_ki[:, cols], A_qi[:, cols], start=True, stop=True)
                    t.matmul(SBK[:, 2 * P:3 * P], A_ke[:, cols], A_qd[:, cols], start=True,
                             stop=True).then_inc(s_full, 1)
                    if b == 0:
                        pe.wait_ge(g_tr_taken, 8 + 14 * h)
                    if b < TB - 1:
                        pe.wait_ge(st_ready, b + 1 + 7 * h)
                        t.matmul(UBK[:, 0:DV], KN[:, b, :], VN[:, b, :], start=True, stop=True).then_inc(u_full, 1)
                    if not last and b % 2 == 1:
                        gla_quantum(h + 1, 4 + b // 2)
                    pe.wait_ge(attn_ready, b + 2 + 8 * h)
                    pe.wait_ge(on_ready, b + 1 + 8 * h)
                    o = OBK[b % 2][:, 0:DV]
                    mm = t.matmul(o, attn[:, b % 2, :], VN[:, b, :], start=True, stop=b == 0)
                    if b > 0:
                        pe.wait_ge(st_ready, b + 1 + 7 * h)
                        mm = t.matmul(o, A_eb[:, cols], St[:, b % 2, :], start=False, stop=True)
                    mm.then_inc(o_full, 1)
                    if b > 0:
                        turn(b - 1)
                turn(TB - 1)

            with pe.Fori(0, GH - 1) as h:
                gla_head(h, False)
            gla_head(GH - 1, True)
            phase_end(pe, 1)

            def finish(br, n0, k0):
                s = fin[br]
                for part, (rhs, taken) in enumerate(((HT, s["g_taken"]), (HT, s["m_taken"]), (OA, s["y_taken"]))):
                    pe.sem_inc(taken, 2)
                    with pe.Fori(0, KD // 2) as j:
                        for par in range(2):
                            n = n0 + part * KD + par
                            for hf in range(NH):
                                quantum(n + 2 * j, n % 2, hf, rhs, taken, 2 * par + hf + 4 * j)
                    phase_end(pe, k0 + part)

            finish("A", N_A, 2)

            pe.sem_inc(b_taken, 2)

            def sb_quantum(h, par, i):
                c, hf = divmod(i, 2)
                n = N_FA + 3 * par + c
                if par == 0:
                    quantum(n + 3 * h, n % 2, hf, HT, b_taken, i + 6 * h)
                else:
                    quantum(n - 3 + 3 * h, n % 2, hf, HT, b_taken, i + 6 * h)

            for i in range(6):
                sb_quantum(0, 0, i)

            def sb_head(h, par, last):
                def rounds(some):
                    for kind, r, j, b0, nb in some:
                        pe.wait_ge(b_tr_lo, r + 1 + SB_ROUNDS * h)
                        if kind == "v":
                            pe.wait_ge(b_taken, 8 + 6 * h)
                        else:
                            pe.wait_ge(w_done, j + 1 + 8 * h)
                        for m in range(nb):
                            src = vT if kind == "v" else T2[:, j % 2, :]
                            mm = t.transpose(trs[0][:, m * P:(m + 1) * P], src[:, (b0 + m) * P:(b0 + m + 1) * P],
                                             ident[:, :])
                        mm.then_inc(b_tr_full, 1)

                def weigh_values(gq):
                    pe.wait_ge(b_tr_lo, (6 if gq == 0 else SB_ROUNDS) + 1 + SB_ROUNDS * h)
                    pe.wait_ge(pv_taken, gq + 1 + 2 * h)
                    steps = [(sb, a, c) for sb in range(4 * gq + 4) for a, c in PASSES]
                    for i, (sb, a, c) in enumerate(steps):
                        lo = max(0, sb - 4 * gq) * P
                        mm = t.matmul(PV[:, lo:BANK], VS[:, a, sb, :], WT[:, c, sb, lo:BANK], start=i == 0,
                                      stop=i == len(steps) - 1)
                    mm.then_inc(pv_full, 1)

                for i in range(TB + 2):
                    before, after = sb_rounds(i)
                    if i == 6:
                        weigh_values(0)
                    rounds(before)
                    if i < TB:
                        if i == 0:
                            pe.wait_ge(b_taken, 6 + 6 * h)
                        pe.wait_ge(y_done, i + 1 + 8 * h)
                        for c0, c1 in z_pieces(i):
                            for n, (a, c) in enumerate(PASSES):
                                mm = t.matmul(zs[i % 2][:, c0:c1], QK[:, par, 0, a, i * P:(i + 1) * P],
                                              QK[:, par, 1, c, c0:c1], start=n == 0, stop=n == 2)
                        mm.then_inc(z_full, 1)
                    rounds(after)
                    if not last:
                        for q in QUANTA_AT.get(i, []):
                            sb_quantum(h + 1, 1 - par, q)
                weigh_values(1)

            with pe.Fori(0, SH // 2 - 1) as j:
                for par in range(2):
                    sb_head(2 * j + par, par, False)
            sb_head(SH - 2, 0, False)
            sb_head(SH - 1, 1, True)
            phase_end(pe, 5)

            finish("B", N_B, 6)

            def wide(q, half):
                b = q % TB
                product(pj[q % 2][:, :], lambda a, k: HT[:, a, k, b * P:(b + 1) * P],
                        lambda a, k: WD[:, half % 2, a, k, :], KD).then_inc(d_full, 1)

            def turn_u(b):
                pe.wait_ge(u_ready, b + 1)
                for r2 in range(2):
                    r = 2 * b + r2
                    if r >= 2:
                        pe.wait_ge(ut_lo, r - 1)
                    for j in range(4):
                        k = 4 * r2 + j
                        mm = t.transpose(trs[r % 2][:, j * P:(j + 1) * P], u[:, b % 2, k * P:(k + 1) * P], ident[:, :])
                    mm.then_inc(ut_full, 1)

            for q in range(2 * TB):
                if q % TB == 0:
                    pe.wait_ge(w_ready, N_FB + 4 * (q // TB + 1) + 2)
                if q >= 2:
                    pe.wait_ge(d1_taken, q - 1)
                wide(q, q // TB)
                if q >= TB + 2:
                    turn_u(q - TB - 2)
            for b in range(TB - 2, TB):
                turn_u(b)
            for q in range(2 * TB, 4 * TB):
                if q % TB == 0:
                    pe.wait_ge(w_ready, N_FB + 4 * (q // TB + 1) + 2)
                if q < 3 * TB:
                    pe.wait_ge(ut_lo, 2 * (q - 2 * TB) + 2)
                if q < 2 * TB + 2:
                    pe.wait_ge(d1_taken, q - 1)
                else:
                    pe.wait_ge(d3_taken, q - 2 * TB - 1)
                wide(q, q // TB)

        @block.scalar
        def _(act):
            s = nc.scalar
            s.preload_act_table_set(EXP_LN)
            s.sem_inc(pv_taken, 1)
            s.sem_inc(oT_out, 1)
            s.sem_inc(ob_out[0], 1)
            s.sem_inc(ob_out[1], 1)

            def copy(out_, in_, scale=1.0):
                return s.activation(out_, in_, ACT.Copy, scale=scale)

            def inverse_rms(src, n, i, width, sq, ln, inv, count, junk):
                s.activation(junk, src, ACT.Square, accum_out=ssq[:, i:i + 1]).then_inc(sq, 1)
                act.wait_ge(sq, count)
                s.activation(lnm[:, i:i + 1], ssq[:, i:i + 1], ACT.Ln, bias=epsc[:, 0:1],
                             scale=1.0 / width).then_inc(ln, 1)
                act.wait_ge(ln, count)
                return s.activation(rstd[:, i:i + 1], lnm[:, i:i + 1], ACT.Exp, scale=-0.5).then_inc(inv, 1)

            act.wait_ge(const_ready, 17)
            for r in range(TB // 2):
                act.wait_ge(p_full, r + 1)
                copy(pT[:, HI, :, 2 * r * P:(2 * r + 2) * P],
                     trs[r % 2][:, :].rearrange("p (k n) -> p k n", k=PK)).then_inc(p_hi, 1)
            for b in range(TB):
                for q in (2 * b, 2 * b + 1):
                    act.wait_ge(pe_full, q + 1)
                    if q >= 2:
                        act.wait_ge(pe_out[q % 2], 16 * (q // 2))
                    copy(pes[:, q % 2, :], pj[q % 2][:, :]).then_inc(pe_taken, 1)
                    act.wait_ge(pe_taken, q + 1)
                    act.dma_start(pe_d[b * P:(b + 1) * P, (q % 2) * BANK:(q % 2 + 1) * BANK],
                                  pes[:, q % 2, :]).then_inc(pe_out[q % 2], 16)
                act.wait_ge(x_in[b], 16)
                if b:
                    act.wait_ge(x_sq, b)
                inverse_rms(xin[:, b, :], T, b, D, x_sq, x_ln, x_rstd, b + 1, junk0[:, :])
            for r in range(2 * TB):
                b, r2 = divmod(r, 2)
                act.wait_ge(xt_full, r + 1)
                copy(HT[:, HI, 4 * r2:4 * r2 + 4, b * P:(b + 1) * P],
                     trs[r % 2][:, :].rearrange("p (k n) -> p k n", k=4)).then_inc(xt_hi, 1)
            act.wait_ge(pe_out[0], 16 * TB)
            act.wait_ge(pe_out[1], 16 * TB)
            phase_end(act, 0)

            def quantum_in(q):
                act.wait_ge(q_full, 5 + q)

            for hf in range(NH):
                quantum_in(hf)
                copy(lrT[:, hf * BANK:(hf + 1) * BANK], pj[hf][0:RANK, :]).then_inc(a_taken, 1)
            act.wait_ge(params_in, 48)
            tmp = [A_ke, A_qd]

            def take_qkv(h, i):
                c, hf = divmod(i, 2)
                quantum_in(2 + i + 8 * h)
                if c >= 2:
                    act.wait_ge(qS_ready, h)
                copy(qkv[:, c, hf * BANK:(hf + 1) * BANK], pj[hf][:, :]).then_inc(a_taken, 1)

            for h in range(GH):
                for hf in range(NH):
                    r = 2 * h + hf
                    act.wait_ge(y_full, r + 1)
                    if h >= 2 and hf == 0:
                        act.wait_ge(y_ls, h - 1)
                    s.activation(tmp[h % 2][:, hf * BANK:(hf + 1) * BANK], trs[hf][:, :], ACT.Abs,
                                 bias=balp[:, h:h + 1]).then_inc(y_abs, 1)
                act.wait_ge(y_abs, 2 * h + 2)
                s.activation(tmp[h % 2][:, :], tmp[h % 2][:, :], ACT.Exp, scale=-1.0).then_inc(y_exp, 1)
                act.wait_ge(y_exp, h + 1)
                s.activation(tmp[h % 2][:, :], tmp[h % 2][:, :], ACT.Ln, bias=1.0).then_inc(y_ln, 1)
            for i in range(8):
                c, hf = divmod(i, 2)
                quantum_in(2 + i)
                copy(qkv[:, c, hf * BANK:(hf + 1) * BANK], pj[hf][:, :]).then_inc(a_taken, 1)
            act.wait_ge(y_cum, GH)

            def gla_head(h, last):
                act.wait_ge(o_full, 2 + 8 * h)
                stand_alone(act)
                yh = Y[:, bass.ds(h, 1), :] if not isinstance(h, int) else Y[:, h:h + 1, :]
                yh = yh.rearrange("p a t -> p (a t)")
                s.activation(A_eb[:, :], yh, ACT.Exp, scale=1.0 / TAU).then_inc(e_done, 1)
                s.activation(A_enb[:, :], yh, ACT.Exp, scale=-1.0 / TAU).then_inc(e_done, 1)
                act.wait_ge(dd_done, h + 1)
                s.activation(A_ke[:, :], A_ke[:, :], ACT.Exp, scale=1.0 / TAU).then_inc(ke_done, 1)

                def take_round(r, out_):
                    act.wait_ge(g_tr_full, r + 3 + 14 * h)
                    return copy(out_, trs[r % 2][:, :]).then_inc(g_tr_taken, 1)

                for r in range(4):
                    take_round(r, VN[:, 2 * r:2 * r + 2, :].rearrange("p b v -> p (b v)"))
                if not last:
                    for i in range(4):
                        take_qkv(h + 1, i)
                for r in range(4, 6):
                    take_round(r, KN[:, 4 * (r - 4):4 * (r - 4) + 4, :].rearrange("p b d -> p (b d)"))

                def take_turned(b):
                    r = 6 + b
                    act.wait_ge(g_tr_full, r + 3 + 14 * h)
                    if b == 0:
                        act.wait_ge(oT_out, 1 + 16 * h)
                    stand_alone(act)
                    for v in range(2):
                        gain = ggla[:, bass.ds(2 * h + v, 1)] if not isinstance(h, int) else \
                            ggla[:, 2 * h + v:2 * h + v + 1]
                        i = copy(oT[:, v, b * P:(b + 1) * P], trs[r % 2][:, v * P:(v + 1) * P], gain)
                    i.then_inc(g_tr_taken, 1)

                for b in range(TB):
                    if not last and b % 2 == 1:
                        take_qkv(h + 1, 4 + b // 2)
                    act.wait_ge(o_full, b + 3 + 8 * h)
                    act.wait_ge(on_ready, b + 1 + 8 * h)
                    i = b % 2
                    c = b + 1 + 8 * h
                    s.activation(junkA[:, :], OBK[i][:, 0:DV], ACT.Square, accum_out=ssq[:, i:i + 1]).then_inc(o_sq, 1)
                    act.wait_ge(o_sq, c)
                    s.activation(lnm[:, i:i + 1], ssq[:, i:i + 1], ACT.Ln, bias=epsc[:, 0:1],
                                 scale=1.0 / DV).then_inc(o_ln, 1)
                    act.wait_ge(o_ln, c)
                    s.activation(rstd[:, i:i + 1], lnm[:, i:i + 1], ACT.Exp, scale=-0.5).then_inc(o_rstd, 1)
                    if b > 0:
                        take_turned(b - 1)
                take_turned(TB - 1)
                act.wait_ge(g_tr_taken, 16 + 14 * h)
                rows = bass.ds(DV * h, DV) if not isinstance(h, int) else slice(DV * h, DV * h + DV)
                act.dma_start(o_gla_d[rows, :].rearrange("(v p) t -> p v t", p=P), oT[:, :, :]).then_inc(oT_out, 16)

            with act.Fori(0, GH - 1) as h:
                gla_head(h, False)
            gla_head(GH - 1, True)
            act.wait_ge(oT_out, 16 * GH + 1)
            phase_end(act, 1)

            def finish(br, n0, k0):
                f = fin[br]
                s.preload_act_table_set(SIGMOID)
                with act.Fori(0, KD // 2) as j:
                    for par in range(2):
                        for hf in range(NH):
                            q = 2 * par + hf
                            act.wait_ge(q_full, 2 * n0 + q + 5 + 4 * j)
                            act.wait_ge(f["oa_ready"], q + 3 + 4 * j)
                            s.activation(sg[:, hf, :], pj[hf][:, :], ACT.Sigmoid).then_inc(f["sg_ready"], 1)
                phase_end(act, k0)
                with act.Fori(0, KD // 2) as j:
                    for par in range(2):
                        for hf in range(NH):
                            q = 2 * par + hf
                            act.wait_ge(q_full, 2 * (n0 + KD) + q + 5 + 4 * j)
                            stand_alone(act)
                            s.activation(SM[:, bass.ds(2 * j + par, 1), hf * BANK:(hf + 1) * BANK].rearrange(
                                "p a t -> p (a t)"), pj[hf][:, :], ACT.Sigmoid).then_inc(f["m_taken"], 1)
                phase_end(act, k0 + 1)
                if br == "A":
                    with act.Fori(0, KD // 2) as j:
                        for par in range(2):
                            for hf in range(NH):
                                e = 2 * j + par
                                act.wait_ge(f["y_taken"], 2 * par + hf + 3 + 4 * j)
                                act.dma_start(ya_d[bass.ds(P * e, P), hf * BANK:(hf + 1) * BANK],
                                              ys[:, hf, :]).then_inc(f[f"yio{hf}"], 16)
                    act.wait_ge(f["yio0"], 16 * KD + 1)
                    act.wait_ge(f["yio1"], 16 * KD + 1)
                s.preload_act_table_set(EXP_LN)
                phase_end(act, k0 + 2)

            finish("A", N_A, 2)

            def take_quantum(h, par, i):
                c, hf = divmod(i, 2)
                if c == 2:
                    return
                act.wait_ge(q_full, 2 * N_FA + 5 + i + 6 * h)
                copy(QK[:, par, c, HI, hf * BANK:(hf + 1) * BANK], pj[hf][:, :],
                     Q_SCALE if c == 0 else 1.0).then_inc(b_hi, 1)

            for i in range(6):
                take_quantum(0, 0, i)

            def sb_head(h, par, last):
                def take_rounds(some):
                    for kind, r, j, b0, nb in some:
                        act.wait_ge(b_tr_full, r + 1 + SB_ROUNDS * h)
                        src = trs[0][:, 0:nb * P].rearrange("p (b t) -> p b t", b=nb)
                        if kind == "v":
                            copy(VS[:, HI, b0:b0 + nb, :], src).then_inc(b_tr_hi, 1)
                        else:
                            act.wait_ge(pv_full, (2 if j >= 4 else 1) + 2 * h)
                            c0 = (j % 4) * P
                            copy(WT[:, HI, b0:b0 + nb, c0:c0 + P], src).then_inc(b_tr_hi, 1)

                def take_outputs(gq):
                    act.wait_ge(pv_full, gq + 2 + 2 * h)
                    act.wait_ge(ob_out[gq], 1 + 16 * h)
                    copy(oS[:, gq, :], PV[:, :]).then_inc(pv_taken, 1)
                    act.wait_ge(pv_taken, gq + 2 + 2 * h)
                    rows = bass.ds(P * h, P) if not isinstance(h, int) else slice(P * h, P * h + P)
                    act.dma_start(o_sb_d[rows, gq * BANK:(gq + 1) * BANK], oS[:, gq, :]).then_inc(ob_out[gq], 16)

                for i in range(TB + 2):
                    before, after = sb_rounds(i)
                    w = (i + 1) * P
                    c = i + 1 + 8 * h
                    a = T1[:, i % 2, 0:w] if i < TB else None
                    take_rounds(before)
                    if i < TB:
                        act.wait_ge(z_full, c)
                        s.activation(a, zs[i % 2][:, 0:w], ACT.Abs).then_inc(z_abs, 1)
                    take_rounds(after)
                    if i < TB:
                        act.wait_ge(z_abs, c)
                        s.activation(a, a, ACT.Exp, scale=-1.0).then_inc(z_exp, 1)
                        act.wait_ge(z_exp, c)
                        s.activation(a, a, ACT.Ln, bias=1.0).then_inc(z_ln, 1)
                    if 1 <= i <= TB:
                        act.wait_ge(ym, i + 8 * h)
                        v = T2[:, (i - 1) % 2, 0:i * P]
                        s.activation(v, v, ACT.Exp).then_inc(w_done, 1)
                    if i == 6:
                        take_outputs(0)
                    if not last:
                        for q in QUANTA_AT.get(i, []):
                            take_quantum(h + 1, 1 - par, q)
                take_outputs(1)

            with act.Fori(0, SH // 2 - 1) as j:
                for par in range(2):
                    sb_head(2 * j + par, par, False)
            sb_head(SH - 2, 0, False)
            sb_head(SH - 1, 1, True)
            for gq in range(2):
                act.wait_ge(ob_out[gq], 16 * SH + 1)
            phase_end(act, 5)

            finish("B", N_B, 6)

            def u_rms(b):
                act.wait_ge(d1_taken, TB + b + 1)
                if b >= 1:
                    act.wait_ge(u_sq, b)
                inverse_rms(x1[:, b, :], D, b, D, u_sq, u_ln, u_rstd, b + 1, junkD[:, :])

            def take_u(b):
                for r in (2 * b, 2 * b + 1):
                    act.wait_ge(ut_full, r + 1)
                    copy(HT[:, HI, 4 * (r % 2):4 * (r % 2) + 4, b * P:(b + 1) * P],
                         trs[r % 2][:, :].rearrange("p (k n) -> p k n", k=4)).then_inc(ut_hi, 1)

            for b in range(TB):
                u_rms(b)
                if b >= 2:
                    take_u(b - 2)
            for b in range(TB - 2, TB):
                take_u(b)

            def final_rms(b):
                act.wait_ge(x2_ready, TB + b + 1)
                if b >= 1:
                    act.wait_ge(f_sq, b)
                inverse_rms(x1[:, b, :], D, b, D, f_sq, f_ln, f_rstd, b + 1, junkD[:, :])

            def store(b):
                act.wait_ge(f_ready, b + 1)
                act.dma_start(out_rows[b * P:(b + 1) * P, :], u[:, b % 2, :]).then_inc(out_done[b % 2], 16)

            for q in range(2 * TB):
                s.preload_act_table_set(SIGMOID) if q == 0 or q > TB + 1 else None
                act.wait_ge(d_full, 2 * TB + q + 1)
                if q >= 2:
                    act.wait_ge(x2_ready, q - 1)
                s.activation(sgD[:, q % 2, :], pj[q % 2][:, :], ACT.Sigmoid).then_inc(d3_taken, 1)
                if q >= TB + 1:
                    s.preload_act_table_set(EXP_LN)
                    final_rms(q - TB - 1)
                    if q >= TB + 2:
                        store(q - TB - 2)
            final_rms(TB - 1)
            store(TB - 2)
            store(TB - 1)
            for i in range(2):
                act.wait_ge(out_done[i], 16 * (TB // 2))

        @block.vector
        def _(dve):
            v = nc.vector
            v.sem_inc(attn_ready, 1)
            v.sem_inc(st_ready, 1)
            v.sem_inc(on_ready, 2)
            v.sem_inc(y_done, 2)
            v.sem_inc(b_tr_lo, 1)
            for br in "AB":
                v.sem_inc(fin[br]["oa_ready"], 4)
                v.sem_inc(fin[br]["ysum"], 2)
            v.sem_inc(fin["A"]["yio0"], 1)
            v.sem_inc(fin["A"]["yio1"], 1)

            def rest(out_, whole, hi):
                return v.tensor_tensor(out_, whole, hi.bitcast(F32), ALU.subtract)

            dve.wait_ge(w_ple_in, 16)
            v.tensor_copy(wpe[:, HI, :, :], wpe_raw[:, :, :]).then_inc(wpe_hi, 1)
            dve.wait_ge(wpe_hi, 1)
            rest(wpe[:, LO, :, :], wpe_raw[:, :, :], wpe[:, HI, :, :]).then_inc(wpe_lo, 1)
            for r in range(TB // 2):
                dve.wait_ge(p_hi, r + 1)
                c = slice(2 * r * P, (2 * r + 2) * P)
                rest(pT[:, LO, :, c], trs[r % 2][:, :].rearrange("p (k n) -> p k n", k=PK),
                     pT[:, HI, :, c]).then_inc(p_lo, 1)
            dve.wait_ge(gain_in, 16)
            for b in range(TB):
                dve.wait_ge(x_rstd, b + 1)
                v.scalar_tensor_tensor(out=xin[:, b, :], in0=xin[:, b, :], scalar=rstd[:, b:b + 1],
                                       in1=gains[:, 0, :], op0=ALU.mult, op1=ALU.mult).then_inc(x_norm, 1)
            for r in range(2 * TB):
                b, r2 = divmod(r, 2)
                dve.wait_ge(xt_hi, r + 1)
                k, c = slice(4 * r2, 4 * r2 + 4), slice(b * P, (b + 1) * P)
                rest(HT[:, LO, k, c], trs[r % 2][:, :].rearrange("p (k n) -> p k n", k=4),
                     HT[:, HI, k, c]).then_inc(xt_lo, 1)
            phase_end(dve, 0)

            v.memset(newchunk[:, :], 1.0).then_inc(chunk_mask, 1)
            v.memset(attn[:, :, :], 0.0).then_inc(chunk_mask, 1)
            dve.wait_ge(chunk_mask, 2)
            v.memset(newchunk[:, :].rearrange("p (c t) -> p c t", t=CHUNK)[:, :, 0:1], 0.0).then_inc(chunk_mask, 1)
            dve.wait_ge(chunk_mask, 3)
            dve.wait_ge(params_in, 48)
            tmp = [A_ke, A_qd]
            for h in range(GH):
                for hf in range(NH):
                    dve.wait_ge(y_abs, 2 * h + hf + 1)
                    v.tensor_scalar(Y[:, h, hf * BANK:(hf + 1) * BANK], trs[hf][:, :], balp[:, h:h + 1], 0.0,
                                    ALU.add, ALU.min).then_inc(y_min, 1)
                dve.wait_ge(y_min, 2 * h + 2)
                dve.wait_ge(y_ln, h + 1)
                v.tensor_tensor(Y[:, h, :], Y[:, h, :], tmp[h % 2][:, :], ALU.subtract).then_inc(y_ls, 1)
                dve.wait_ge(y_ls, h + 1)
                v.tensor_tensor_scan(Y[:, h, :], newchunk[:, :], Y[:, h, :], 0.0, ALU.mult, ALU.add).then_inc(y_cum, 1)
            dve.wait_ge(y_cum, GH)

            def chunks(a):
                return a.rearrange("p (c t) -> p c t", t=CHUNK)

            def gla_head(h, last):
                dve.wait_ge(o_full, 2 + 8 * h)
                yh = Y[:, bass.ds(h, 1), :] if not isinstance(h, int) else Y[:, h:h + 1, :]
                yc = yh.rearrange("p a (c t) -> p (a c) t", t=CHUNK)
                v.tensor_tensor(chunks(A_ke[:, :]), yc[:, :, CHUNK - 1:CHUNK].to_broadcast([P, T // CHUNK, CHUNK]),
                                yc, ALU.subtract).then_inc(dd_done, 1)
                dve.wait_ge(e_done, 1 + 2 * h)
                if isinstance(h, int) and h == 0:
                    pass
                ends = A_eb[:, :].rearrange("p (b c t) -> p b c t", c=2, t=CHUNK)
                e0, e1 = ends[:, :, 0, CHUNK - 1], ends[:, :, 1, CHUNK - 1]
                v.tensor_copy(two_c[:, :, 1], e0).then_inc(dec_part, 1)
                v.tensor_copy(two_k[:, :, 0], e1).then_inc(dec_part, 1)
                v.tensor_tensor(dec[:, :], e0, e1, ALU.mult).then_inc(dec_part, 1)
                dve.wait_ge(a_taken, 12 + 8 * h)
                dve.wait_ge(e_done, 2 + 2 * h)
                q_, k_ = qkv[:, 2, :], qkv[:, 3, :]
                v.scalar_tensor_tensor(out=A_qd[:, :], in0=q_, scalar=Q_SCALE, in1=A_eb[:, :], op0=ALU.mult,
                                       op1=ALU.mult).then_inc(prep, 1)
                v.scalar_tensor_tensor(out=A_qi[:, :], in0=q_, scalar=Q_SCALE, in1=A_enb[:, :], op0=ALU.mult,
                                       op1=ALU.mult).then_inc(prep, 1)
                v.tensor_tensor(A_kd[:, :], k_, A_enb[:, :], ALU.mult).then_inc(prep, 1)
                v.tensor_tensor(A_ki[:, :], k_, A_eb[:, :], ALU.mult).then_inc(prep, 1)
                dve.wait_ge(ke_done, h + 1)
                v.tensor_tensor(A_ke[:, :], k_, A_ke[:, :], ALU.mult).then_inc(prep, 1)
                dve.wait_ge(prep, 5 + 5 * h)
                dve.wait_ge(dec_part, 3 + 3 * h)
                v.tensor_tensor(chunks(A_enb[:, :]), chunks(A_ke[:, :]),
                                two_k[:, :, :].rearrange("p b (c o) -> p (b c) o", o=1).to_broadcast(
                                    [P, T // CHUNK, CHUNK]), ALU.mult).then_inc(kS_ready, 1)
                v.tensor_tensor(chunks(A_eb[:, :]), chunks(A_qd[:, :]),
                                two_c[:, :, :].rearrange("p b (c o) -> p (b c) o", o=1).to_broadcast(
                                    [P, T // CHUNK, CHUNK]), ALU.mult).then_inc(qS_ready, 1)

                def norm(b):
                    dve.wait_ge(o_rstd, b + 1 + 8 * h)
                    dve.wait_ge(g_tr_full, (b + 1 if b < 2 else b + 7) + 14 * h)
                    v.tensor_scalar(on[:, b % 2, :], OBK[b % 2][:, 0:DV], rstd[:, b % 2:b % 2 + 1], None,
                                    ALU.mult).then_inc(on_ready, 1)

                for b in range(TB):
                    dve.wait_ge(s_full, b + 1 + 8 * h)
                    dve.wait_ge(o_full, b + 1 + 8 * h)
                    stand_alone(dve)
                    a = attn[:, b % 2, :]
                    c = 2 * b + 16 * h
                    v.copy_predicated(a, m_past[:, :].bitcast(U32), SBK[:, 0:P]).then_inc(attn_part, 1)
                    dve.wait_ge(attn_part, c + 1)
                    stand_alone(dve)
                    v.copy_predicated(a, m_fut[:, :].bitcast(U32), SBK[:, P:2 * P]).then_inc(attn_part, 1)
                    dve.wait_ge(attn_part, c + 2)
                    stand_alone(dve)
                    v.copy_predicated(a, m_cross[:, :].bitcast(U32), SBK[:, 2 * P:3 * P]).then_inc(attn_ready, 1)
                    if b < TB - 1:
                        dve.wait_ge(u_full, b + 1 + 7 * h)
                        dve.wait_ge(o_full, b + 2 + 8 * h)
                        dve.wait_ge(st_ready, b + 1 + 7 * h)
                        if b == 0:
                            v.tensor_copy(St[:, 1, :], UBK[:, 0:DV]).then_inc(st_ready, 1)
                        else:
                            v.scalar_tensor_tensor(out=St[:, (b + 1) % 2, :], in0=St[:, b % 2, :],
                                                   scalar=dec[:, b:b + 1], in1=UBK[:, 0:DV], op0=ALU.mult,
                                                   op1=ALU.add).then_inc(st_ready, 1)
                    if b > 0:
                        norm(b - 1)
                norm(TB - 1)

            with dve.Fori(0, GH - 1) as h:
                gla_head(h, False)
            gla_head(GH - 1, True)
            phase_end(dve, 1)

            def finish(br, n0, k0):
                f = fin[br]
                with dve.Fori(0, KD // 2) as j:
                    for par in range(2):
                        dve.wait_ge(f[f"oin{par}"], 16 + 16 * j)
                        for hf in range(NH):
                            q = 2 * par + hf
                            c = slice(hf * BANK, (hf + 1) * BANK)
                            dve.wait_ge(f["sg_ready"], q + 1 + 4 * j)
                            g_ = sg[:, hf, :]
                            v.tensor_tensor(g_, pj[hf][:, :], g_, ALU.mult).then_inc(f["g_taken"], 1)
                            dve.wait_ge(f["g_taken"], q + 3 + 4 * j)
                            v.tensor_tensor(g_, g_, oin[:, par, c], ALU.mult).then_inc(f["og"], 1)
                            dve.wait_ge(f["og"], q + 1 + 4 * j)

                            def dst(part):
                                return OA[:, part, bass.ds(2 * j + par, 1), c].rearrange("p a t -> p (a t)")
                            v.tensor_copy(dst(HI), g_).then_inc(f["hi"], 1)
                            dve.wait_ge(f["hi"], q + 1 + 4 * j)
                            rest(dst(LO), g_, dst(HI)).then_inc(f["oa_ready"], 1)
                phase_end(dve, k0)
                phase_end(dve, k0 + 1)
                with dve.Fori(0, KD // 2) as j:
                    for par in range(2):
                        for hf in range(NH):
                            q = 2 * par + hf
                            e = 2 * j + par
                            c = slice(hf * BANK, (hf + 1) * BANK)
                            dve.wait_ge(q_full, 2 * (n0 + 2 * KD) + q + 5 + 4 * j)
                            y_ = ys[:, hf, :]
                            if br == "A":
                                dve.wait_ge(f[f"yio{hf}"], 1 + 16 * e)
                            else:
                                dve.wait_ge(f["ylo"], q + 4 * j - 1) if False else None
                            m = SM[:, bass.ds(e, 1), c].rearrange("p a t -> p (a t)")
                            v.tensor_tensor(y_, pj[hf][:, :], m, ALU.mult).then_inc(f["y_taken"], 1)
                            if br == "A":
                                continue
                            dve.wait_ge(f["y_taken"], q + 3 + 4 * j)
                            dve.wait_ge(f[f"yio{hf}"], 16 + 16 * e)
                            v.tensor_tensor(y_, y_, yin[:, hf, :], ALU.add).then_inc(f["ysum"], 1)
                            dve.wait_ge(f["ysum"], q + 3 + 4 * j)

                            def dst(part):
                                return HT[:, part, bass.ds(e, 1), c].rearrange("p a t -> p (a t)")
                            v.tensor_copy(dst(HI), y_).then_inc(f["yhi"], 1)
                            dve.wait_ge(f["yhi"], q + 1 + 4 * j)
                            rest(dst(LO), y_, dst(HI)).then_inc(f["ylo"], 1)
                            dve.wait_ge(f["ylo"], q + 1 + 4 * j)
                phase_end(dve, k0 + 2)

            finish("A", N_A, 2)

            def take_quantum(h, par, i):
                c, hf = divmod(i, 2)
                cols = slice(hf * BANK, (hf + 1) * BANK)
                if c == 2:
                    dve.wait_ge(q_full, 2 * N_FA + 5 + i + 6 * h)
                    v.tensor_copy(vT[:, cols], pj[hf][:, :]).then_inc(b_taken, 1)
                    return
                dve.wait_ge(b_hi, i + 1 + 4 * h)
                hi, lo = QK[:, par, c, HI, cols], QK[:, par, c, LO, cols]
                v.scalar_tensor_tensor(out=lo, in0=pj[hf][:, :], scalar=Q_SCALE if c == 0 else 1.0,
                                       in1=hi.bitcast(F32), op0=ALU.mult, op1=ALU.subtract).then_inc(b_taken, 1)

            for i in range(6):
                take_quantum(0, 0, i)

            def sb_head(h, par, last):
                def take_rounds(some):
                    for kind, r, j, b0, nb in some:
                        dve.wait_ge(b_tr_hi, r + 1 + SB_ROUNDS * h)
                        src = trs[0][:, 0:nb * P].rearrange("p (b t) -> p b t", b=nb)
                        if kind == "v":
                            rest(VS[:, LO, b0:b0 + nb, :], src, VS[:, HI, b0:b0 + nb, :]).then_inc(b_tr_lo, 1)
                        else:
                            c0 = (j % 4) * P
                            rest(WT[:, LO, b0:b0 + nb, c0:c0 + P], src,
                                 WT[:, HI, b0:b0 + nb, c0:c0 + P]).then_inc(b_tr_lo, 1)

                for i in range(TB + 2):
                    before, after = sb_rounds(i)
                    take_rounds(before)
                    take_rounds(after)
                    if i < TB:
                        w = (i + 1) * P
                        c = i + 1 + 8 * h
                        z, a, y = zs[i % 2][:, 0:w], T1[:, i % 2, 0:w], T2[:, i % 2, 0:w]
                        dve.wait_ge(z_ln, c)
                        v.scalar_tensor_tensor(out=a, in0=z, scalar=0.0, in1=a, op0=ALU.max,
                                               op1=ALU.add).then_inc(sp, 1)
                        dve.wait_ge(sp, c)
                        v.tensor_tensor(T1[:, i % 2, i * P:w], T1[:, i % 2, i * P:w], before01[:, :],
                                        ALU.mult).then_inc(spm, 1)
                        dve.wait_ge(spm, c)
                        v.tensor_tensor_scan(y[:, ::-1], a[:, ::-1], a[:, ::-1], 0.0, ALU.add,
                                             ALU.bypass).then_inc(cum, 1)
                        dve.wait_ge(cum, c)
                        v.tensor_tensor(y, z, y, ALU.subtract).then_inc(y_done, 1)
                        dve.wait_ge(y_done, c + 2)
                        v.tensor_tensor(T2[:, i % 2, i * P:w], T2[:, i % 2, i * P:w], before_cap[:, :],
                                        ALU.min).then_inc(ym, 1)
                    if not last:
                        for q in QUANTA_AT.get(i, []):
                            take_quantum(h + 1, 1 - par, q)

            with dve.Fori(0, SH // 2 - 1) as j:
                for par in range(2):
                    sb_head(2 * j + par, par, False)
            sb_head(SH - 2, 0, False)
            sb_head(SH - 1, 1, True)
            phase_end(dve, 5)

            finish("B", N_B, 6)

            dve.wait_ge(gain2_in, 32)

            def add_x(q):
                ch, b = divmod(q, TB)
                c = slice(ch * BANK, (ch + 1) * BANK)
                dve.wait_ge(d_full, q + 1)
                if ch == 0:
                    dve.wait_ge(x2_in[b], 16)
                v.tensor_tensor(x1[:, b, c], x1[:, b, c], pj[q % 2][:, :], ALU.add).then_inc(d1_taken, 1)

            def norm_u(b):
                dve.wait_ge(u_rstd, b + 1)
                if b >= 2:
                    dve.wait_ge(ut_full, 2 * b - 2)
                v.scalar_tensor_tensor(out=u[:, b % 2, :], in0=x1[:, b, :], scalar=rstd[:, b:b + 1],
                                       in1=gains[:, 0, :], op0=ALU.mult, op1=ALU.mult).then_inc(u_ready, 1)

            def rest_u(b):
                for r in (2 * b, 2 * b + 1):
                    dve.wait_ge(ut_hi, r + 1)
                    k, c = slice(4 * (r % 2), 4 * (r % 2) + 4), slice(b * P, (b + 1) * P)
                    rest(HT[:, LO, k, c], trs[r % 2][:, :].rearrange("p (k n) -> p k n", k=4),
                         HT[:, HI, k, c]).then_inc(ut_lo, 1)

            for q in range(2 * TB):
                add_x(q)
                if q >= TB + 1:
                    norm_u(q - TB - 1)
                if q >= TB + 2:
                    rest_u(q - TB - 2)
            norm_u(TB - 1)
            rest_u(TB - 2)
            rest_u(TB - 1)

            def norm_out(b):
                dve.wait_ge(f_rstd, b + 1)
                if b >= 2:
                    dve.wait_ge(out_done[b % 2], 16 * (b // 2))
                v.scalar_tensor_tensor(out=u[:, b % 2, :], in0=x1[:, b, :], scalar=rstd[:, b:b + 1],
                                       in1=gains[:, 1, :], op0=ALU.mult, op1=ALU.mult).then_inc(f_ready, 1)

            for q in range(2 * TB):
                ch, b = divmod(q, TB)
                c = slice(ch * BANK, (ch + 1) * BANK)
                dve.wait_ge(d3_taken, q + 1)
                dve.wait_ge(pe_in[q % 2], 16 * (q // 2 + 1))
                v.tensor_tensor(sgD[:, q % 2, :], sgD[:, q % 2, :], pin2[:, q % 2, :], ALU.mult).then_inc(gate_used, 1)
                dve.wait_ge(gate_used, q + 1)
                v.tensor_tensor(x1[:, b, c], x1[:, b, c], sgD[:, q % 2, :], ALU.add).then_inc(x2_ready, 1)
                if q >= TB + 2:
                    norm_out(q - TB - 2)
            norm_out(TB - 2)
            norm_out(TB - 1)


_INS = ["x", "p", "g_mix", "w_in", "w_alpha", "b_alpha", "g_gla_out", "w_out_gla", "w_out_sb", "w_out", "g_ple",
        "w_ple_gate", "w_ple", "g_final"]


def kernel(**inputs):
    import numpy as _np
    import concourse.bacc as _bacc
    from concourse import mybir as _mybir
    from concourse.bass_utils import run_bass_kernel_spmd as _run

    nc = _bacc.Bacc("TRN2", target_bir_lowering=False, num_devices=1)
    arrays, args = {}, []
    for name in _INS:
        a = _np.ascontiguousarray(inputs[name])
        arrays[f"in_{name}_dram"] = a
        args.append(nc.dram_tensor(f"in_{name}_dram", a.shape, _mybir.dt.from_np(a.dtype), kind="ExternalInput").ap())
    out = nc.dram_tensor("out_0_dram", inputs["x"].shape, _mybir.dt.from_np(_np.dtype("float32")),
                         kind="ExternalOutput").ap()
    hybrid_block(nc, *args, out)
    r = _run(nc, [arrays], core_ids=[0])
    return r.results[0]["out_0_dram"]
```

```python
from contextlib import ExitStack

import concourse.bass as bass
from concourse import mybir

F32 = mybir.dt.float32
F32R = mybir.dt.float32r
U32 = mybir.dt.uint32
ALU = mybir.AluOpType
ACT = mybir.ActivationFunctionType

P = 128
BANK = 512
CHUNK = 64
EPS = 1e-6
TAU = 16.0
EXP_LN = "natural_log_exp_and_others"
SIGMOID = "sigmoid_and_others"

HI, LO = 0, 1
PASSES = ((HI, HI), (HI, LO), (LO, HI))


def hybrid_block(nc, x, p, g_mix, w_in, w_alpha, b_alpha, g_gla_out, w_out_gla, w_out_sb, w_out, g_ple,
                 w_ple_gate, w_ple, g_final, out):
    T, D = x.shape[1], x.shape[2]
    TB, KD = T // P, D // P
    NH = T // BANK
    RANK, QKW = w_alpha.shape[1], w_alpha.shape[2]
    GH, DV = g_gla_out.shape[1], g_gla_out.shape[2]
    DK = QKW // GH
    SH = D // P
    PK = w_ple.shape[1] // P
    CPB = P // CHUNK
    assert DK == P and DV == 2 * P and CPB == 2 and NH == 2 and TB == 8 and KD == 8 and SH == 8
    Q_SCALE = float(P) ** -0.5

    widths = [QKW, QKW, GH * DV, RANK, GH * DV, D, D, D, D, D, D]
    QA, KA, VA, LR, GA, QB, KB, VB, GB, MA, MB = [sum(widths[:i]) for i in range(len(widths))]

    def by_k(w):
        return w.rearrange("(k p) n -> p k n", p=P)

    w_in_k, w_og_k, w_ob_k = by_k(w_in[0]), by_k(w_out_gla[0]), by_k(w_out_sb[0])
    w_out_k, w_pg_k, w_ple_k = by_k(w_out[0]), by_k(w_ple_gate[0]), by_k(w_ple[0])
    x_rows, p_rows, out_rows = x[0], p[0, 0], out[0]

    o_gla_d = nc.dram_tensor("o_gla_scratch", (D, T), F32, kind="Internal").ap()
    o_sb_d = nc.dram_tensor("o_sb_scratch", (D, T), F32, kind="Internal").ap()
    ya_d = nc.dram_tensor("ya_scratch", (D, T), F32, kind="Internal").ap()
    pe_d = nc.dram_tensor("pe_scratch", (T, D), F32, kind="Internal").ap()

    KB_ = 1024
    base = (nc.sbuf_base + 63) // 64 * 64

    def place(name, shape, dt, at):
        return nc.alloc_sbuf_tensor_at(name, shape, dt, offset=base + at)

    HT = place("HT", [P, 2, KD, T], F32R, 0)
    RAW = place("RAW", [P, 2, KD, P], F32, 64 * KB_)
    WS = place("WS", [P, 2, 2, KD, P], F32R, 72 * KB_)
    AREA = 88 * KB_
    MISC = 184 * KB_
    gains = place("gains", [P, 2, D], F32, MISC)
    ident = place("ident", [P, P], F32, MISC + 8192)
    before01 = place("before01", [P, P], F32, MISC + 8704)
    before_cap = place("before_cap", [P, P], F32, MISC + 9216)
    m_past = place("m_past", [P, P], F32, MISC + 9728)
    m_fut = place("m_fut", [P, P], F32, MISC + 10240)
    m_cross = place("m_cross", [P, P], F32, MISC + 10752)
    balp = place("balp", [P, GH], F32, MISC + 11264)
    ggla = place("ggla", [P, 2 * GH], F32, MISC + 11328)
    ssq = place("ssq", [P, TB], F32, MISC + 11392)
    lnm = place("lnm", [P, TB], F32, MISC + 11456)
    rstd = place("rstd", [P, TB], F32, MISC + 11520)
    two_c = place("two_c", [P, TB, 2], F32, MISC + 11584)
    two_k = place("two_k", [P, TB, 2], F32, MISC + 11648)
    dec = place("dec", [P, TB], F32, MISC + 11712)
    epsc = place("epsc", [P, 1], F32, MISC + 11776)
    lrT = place("lrT", [RANK, T], F32, MISC + 12288)
    walp = place("walp", [RANK, QKW], F32, MISC + 16384)
    xin = place("xin", [P, TB, D], F32, AREA)
    pin = place("pin", [P, TB, PK * P], F32, AREA + 32 * KB_)
    wpe_raw = place("wpe_raw", [P, PK, D], F32, AREA + 40 * KB_)
    wpe = place("wpe", [P, 2, PK, D], F32R, AREA + 48 * KB_)
    pT = place("pT", [P, 2, PK, T], F32R, AREA + 64 * KB_)
    pes = place("pes", [P, 2, BANK], F32, AREA + 80 * KB_)
    junk0 = place("junk0", [P, D], F32, AREA + 84 * KB_)
    qkv = place("qkv", [P, 4, T], F32, AREA)
    Y = place("Y", [P, GH, T], F32, AREA + 16 * KB_)
    A_ke = place("A_ke", [P, T], F32, AREA + 32 * KB_)
    A_eb = place("A_eb", [P, T], F32, AREA + 36 * KB_)
    A_enb = place("A_enb", [P, T], F32, AREA + 40 * KB_)
    A_qd = place("A_qd", [P, T], F32, AREA + 44 * KB_)
    A_kd = place("A_kd", [P, T], F32, AREA + 48 * KB_)
    A_qi = place("A_qi", [P, T], F32, AREA + 52 * KB_)
    A_ki = place("A_ki", [P, T], F32, AREA + 56 * KB_)
    VN = place("VN", [P, TB, DV], F32, AREA + 60 * KB_)
    KN = place("KN", [P, TB, DK], F32, AREA + 68 * KB_)
    oT = place("oT", [P, 2, T], F32, AREA + 72 * KB_)
    on = place("on", [P, 2, DV], F32, AREA + 80 * KB_)
    attn = place("attn", [P, 2, P], F32, AREA + 82 * KB_)
    St = place("St", [P, 2, DV], F32, AREA + 83 * KB_)
    junkA = place("junkA", [P, DV], F32, AREA + 85 * KB_)
    newchunk = place("newchunk", [P, T], F32, AREA + 86 * KB_)
    OA = place("OA", [P, 2, KD, T], F32R, AREA + 32 * KB_)
    SM = place("SM", [P, KD, T], F32, AREA)
    graw = place("graw", [P, 4, T], F32, AREA)
    early = {"A": qkv, "B": graw}
    sg = place("sg", [P, 2, BANK], F32, AREA + 16 * KB_)
    oin = place("oin", [P, 2, T], F32, AREA + 20 * KB_)
    ys = place("ys", [P, 2, BANK], F32, MISC + 12288)
    yin = place("yin", [P, 2, BANK], F32, MISC + 16384)
    QK = place("QK", [P, 2, 2, 2, T], F32R, AREA)
    WT = place("WT", [P, 2, TB, BANK], F32R, AREA + 32 * KB_)
    VS = place("VS", [P, 2, TB, P], F32R, AREA + 64 * KB_)
    vT = place("vT", [P, T], F32, AREA + 72 * KB_)
    T1 = place("T1", [P, 2, T], F32, AREA + 76 * KB_)
    T2 = place("T2", [P, 2, T], F32, AREA + 84 * KB_)
    oS = place("oS", [P, 2, BANK], F32, AREA + 92 * KB_)
    WD = [place("WD0", [P, 4, 2, KD, P], F32R, AREA - 8 * KB_), place("WD1", [P, 4, 2, KD, P], F32R, AREA + 32 * KB_)]
    x1 = place("x1", [P, TB, D], F32, AREA + 64 * KB_)
    u = place("u", [P, 2, D], F32, 72 * KB_)
    junkD = place("junkD", [P, D], F32, AREA + 24 * KB_)
    sgD = place("sgD", [P, 2, BANK], F32, AREA + 28 * KB_)
    pin2 = place("pin2", [P, 2, BANK], F32, MISC + 12288)

    with ExitStack() as ctx:
        def sem(name):
            return ctx.enter_context(nc.semaphore(name))

        def bank(name, n=1):
            return ctx.enter_context(nc.psum_tensor(name, [P, n * BANK], F32))

        pj = [bank("pj0"), bank("pj1")]
        z0 = bank("z0", 2)
        z1 = bank("z1", 2)
        trs = [bank("tr0"), bank("tr1")]
        zs = [z0, z1]
        SBK = [z0[:, 0:BANK], z0[:, BANK:2 * BANK]]
        OBK = [z1[:, 0:BANK], z1[:, BANK:2 * BANK]]
        ring = [trs[0][:, :], trs[1][:, :]] + SBK

        pe_phase, act_phase, dve_phase = sem("pe_phase"), sem("act_phase"), sem("dve_phase")
        pj_taken = sem("pj_taken")
        const_ready = sem("const_ready")
        params_in = sem("params_in")
        waits_passed = sem("waits_passed")
        gain_in, gain2_in, w_ple_in = sem("gain_in"), sem("gain2_in"), sem("w_ple_in")
        p_in, x_in = sem("p_in"), [sem(f"x_in{i}") for i in range(TB)]
        w_in_s = [sem("w_raw0"), sem("w_raw1")]
        w_hi, w_ready = sem("w_hi"), sem("w_ready")
        q_full = sem("q_full")

        def phase_end(eng, own, k):
            eng.drain().then_inc(own, 1)
            if own is not pe_phase:
                area_free(eng, k)

        def area_free(eng, k):
            for s_ in (pe_phase, act_phase, dve_phase):
                eng.wait_ge(s_, k + 1)

        def stand_alone(eng):
            eng.sem_inc(waits_passed, 1)

        def product(out_, lhs, rhs, blocks):
            steps = [(k, a, b) for k in range(blocks) for a, b in PASSES]
            for i, (k, a, b) in enumerate(steps):
                mm = nc.tensor.matmul(out_, lhs(a, k), rhs(b, k), start=i == 0, stop=i == len(steps) - 1)
            return mm

        N_A0, N_A = 1, 1 + 4 * GH
        N_FA = N_A + 3 * KD
        N_B = N_FA + 3 * SH
        N_FB = N_B + 3 * KD
        N_D = N_FB + 2 * KD
        WIDE_ORDER = [1, 2, 3, 0, 4, 5, 6, 7]
        GLA_SLICES = [(VA, DV), (VA + P, DV), (QA, P), (KA, P)]
        SB_SLICES = [(QB, P), (KB, P), (VB, P)]

        J_P = 0
        J_A = 2 * TB
        J_FA = J_A + 2 + 8 * GH + 8
        FIN_USES = 8 + 16 + 16
        J_B = J_FA + FIN_USES
        J_FB = J_B + 6 + 8 * (SH - 1) + 10
        J_D = J_FB + FIN_USES
        SPARE = 2

        def col(off, step, i):
            return bass.ds(off + step * i, P)

        p_full, p_hi, p_lo = sem("p_full"), sem("p_hi"), sem("p_lo")
        wpe_hi, wpe_lo = sem("wpe_hi"), sem("wpe_lo")
        pe_full, pe_out = sem("pe_full"), [sem("pe_out0"), sem("pe_out1")]
        x_sq, x_ln, x_rstd, x_norm = sem("x_sq"), sem("x_ln"), sem("x_rstd"), sem("x_norm")
        xt_full, xt_hi, xt_lo = sem("xt_full"), sem("xt_hi"), sem("xt_lo")
        y_full, y_abs, y_min, y_exp, y_ln, y_ls, y_cum = [sem(n) for n in (
            "y_full", "y_abs", "y_min", "y_exp", "y_ln", "y_ls", "y_cum")]
        chunk_mask = sem("chunk_mask")
        e_done, dd_done, ke_done, dec_part, dec_done, prep, kS_ready, qS_ready = [sem(n) for n in (
            "e_done", "dd_done", "ke_done", "dec_part", "dec_done", "prep", "kS_ready", "qS_ready")]
        g_tr_full, g_tr_taken = sem("g_tr_full"), sem("g_tr_taken")
        s_full, attn_part, attn_ready = sem("s_full"), sem("attn_part"), sem("attn_ready")
        st_ready = sem("st_ready")
        o_full, o_sq, o_ln, o_rstd, on_ready = [sem(n) for n in ("o_full", "o_sq", "o_ln", "o_rstd", "on_ready")]
        oT_out = sem("oT_out")
        b_hi = sem("b_hi")
        z_full, z_abs, z_exp, z_ln, sp, spm, cum, y_done, ym, w_done = [sem(n) for n in (
            "z_full", "z_abs", "z_exp", "z_ln", "sp", "spm", "cum", "y_done", "ym", "w_done")]
        b_tr_full, b_tr_hi, b_tr_lo = sem("b_tr_full"), sem("b_tr_hi"), sem("b_tr_lo")
        pv_full, ob_out = sem("pv_full"), [sem("ob_out0"), sem("ob_out1")]
        fin = {}
        for br in "AB":
            fin[br] = {n: sem(f"f{br}_{n}") for n in (
                "sg_ready", "gated", "og", "hi", "oa_ready", "oin0", "oin1", "ysum",
                "yhi", "ylo", "yio0", "yio1")}
        x2_in = [sem(f"x2_in{i}") for i in range(TB)]
        d_full = sem("d_full")
        u_sq, u_ln, u_rstd, u_ready = sem("u_sq"), sem("u_ln"), sem("u_rstd"), sem("u_ready")
        ut_full, ut_hi, ut_lo = sem("ut_full"), sem("ut_hi"), sem("ut_lo")
        pe_in, gate_used, x2_ready = [sem("pe_in0"), sem("pe_in1")], sem("gate_used"), sem("x2_ready")
        f_sq, f_ln, f_rstd, f_ready, out_done = sem("f_sq"), sem("f_ln"), sem("f_rstd"), sem("f_ready"), [
            sem("out_done0"), sem("out_done1")]

        def sb_rounds(i):
            if i < 2:
                return [], [("v", i, None, 4 * i, 4)]
            j = i - 2
            if j < 4:
                return [("w", 2 + j, j, 0, j + 1)], []
            return [("w", 6 + 2 * (j - 4), j, 0, 4)], [("w", 7 + 2 * (j - 4), j, 4, j - 3)]

        SB_ROUNDS = 14
        EXTRA = {1: [("q", 0, 0)], 2: [("q", 0, 1), ("q", 1, 0)], 3: [("q", 1, 1)], 4: [("q", 2, 0)],
                 5: [("q", 2, 1), ("q", 3, 0)], 6: [("pv", 0), ("q", 3, 1)], 7: [("q", 4, 0), ("q", 4, 1)],
                 8: [("q", 5, 0)], 9: [("q", 5, 1)], 10: [("pv", 1)]}
        EXTRA_LAST = {1: [("q", 0, 0), ("q", 0, 1)], 2: [("q", 1, 0)], 3: [("q", 1, 1), ("q", 2, 0)],
                      4: [("q", 2, 1), ("q", 3, 0)], 5: [("q", 3, 1), ("q", 4, 0)],
                      6: [("pv", 0), ("q", 4, 1)], 7: [("q", 5, 0), ("q", 5, 1)],
                      8: [("q", 6, 0), ("q", 6, 1)], 9: [("q", 7, 0), ("q", 7, 1)], 10: [("pv", 1)]}

        def uses(extra):
            order = []
            for i in sorted(extra):
                for e in extra[i]:
                    if e[:2] not in order:
                        order.append(e[:2])
            return {e: n for n, e in enumerate(order)}

        def finished(extra, i):
            use = uses(extra)
            return sorted((use[e[:2]], e[:2]) for e in extra.get(i, []) if e[0] == "pv" or e[2] == 1)

        def z_pieces(i):
            w = (i + 1) * P
            first = (0, min(BANK, max(w, 2 * P)))
            return [first] + ([(BANK, max(w, BANK + 2 * P))] if w > BANK else [])

        block = ctx.enter_context(nc.Block())

        @block.sync
        def _(sp_eng):
            sy = sp_eng
            sy.dma_start(wpe_raw[:, :, :], w_ple_k).then_inc(w_ple_in, 16)
            sy.dma_start(pin[:, :, :], p_rows.rearrange("(b t) d -> t b d", t=P)).then_inc(p_in, 16)
            sy.dma_start(gains[:, 0, :], g_mix[0].partition_broadcast(P)).then_inc(gain_in, 16)
            for b in range(TB):
                sy.dma_start(xin[:, b, :], x_rows[b * P:(b + 1) * P, :]).then_inc(x_in[b], 16)

            def load(n, slot, src):
                sy.wait_ge(w_ready, n + 1)
                sy.dma_start(RAW[:, slot, :, :], src).then_inc(w_in_s[slot], 16)

            load(0, 0, w_in_k[:, :, LR:LR + P])
            sy.dma_start(walp[:, :], w_alpha[0]).then_inc(params_in, 16)
            with nc.allow_non_contiguous_dma(reason="two small per-channel vectors"):
                sy.dma_start(balp[:, :], b_alpha[0].rearrange("(h d) -> d h", d=P)).then_inc(params_in, 16)
                sy.dma_start(ggla[:, :], g_gla_out[0].rearrange("h (v d) -> d (h v)", d=P)).then_inc(params_in, 16)
            with sy.Fori(0, GH) as h:
                for c, (off, step) in enumerate(GLA_SLICES):
                    load(N_A0 + c + 4 * h, (N_A0 + c) % 2, w_in_k[:, :, col(off, step, h)])

            def finish(br, n0, k0, gate_off, m_off, wo_k, o_d, stored):
                s = fin[br]

                def load_gate(e):
                    load(n0 + e, (n0 + e) % 2, w_in_k[:, :, gate_off + P * e:gate_off + P * e + P])

                for e in range(6):
                    load_gate(e)
                for e_sem, v in stored:
                    sy.wait_ge(e_sem, v)
                area_free(sy, k0 - 1)
                for i in range(4):
                    for slot, e in enumerate((4 + i, i)):
                        sy.wait_ge(s["oa_ready"], 4 * i + 2 + 2 * slot)
                        sy.dma_start(oin[:, slot, :], o_d[P * e:P * e + P, :]).then_inc(s[f"oin{slot}"], 16)
                    if i < 2:
                        load_gate(6 + i)
                with sy.Fori(0, KD // 2) as j:
                    for par in range(2):
                        load(n0 + KD + par + 2 * j, (n0 + par) % 2, w_in_k[:, :, col(m_off, P, 2 * j + par)])
                if br == "B":
                    for hf in range(NH):
                        sy.wait_ge(fin["A"][f"yio{hf}"], 16 * KD + 1)
                with sy.Fori(0, KD // 2) as j:
                    for par in range(2):
                        e = 2 * j + par
                        load(n0 + 2 * KD + par + 2 * j, (n0 + par) % 2, wo_k[:, :, col(0, P, e)])
                        if br == "B":
                            for hf in range(NH):
                                sy.wait_ge(s["ysum"], 2 * e + hf + 1)
                                sy.dma_start(yin[:, hf, :], ya_d[bass.ds(P * e, P), hf * BANK:(hf + 1) * BANK]
                                             ).then_inc(s[f"yio{hf}"], 16)

            finish("A", N_A, 2, GA, MA, w_og_k, o_gla_d, [(oT_out, 16 * GH + 1)])
            with sy.Fori(0, SH // 2) as j:
                for par in range(2):
                    for c, (off, step) in enumerate(SB_SLICES):
                        n = N_FA + 3 * par + c
                        load(n + 6 * j, n % 2, w_in_k[:, :, col(off, step, 2 * j + par)])
            finish("B", N_B, 6, GB, MB, w_ob_k, o_sb_d, [(ob_out[0], 16 * SH + 1), (ob_out[1], 16 * SH + 1)])

            sy.dma_start(gains[:, 0, :], g_ple[0].partition_broadcast(P)).then_inc(gain2_in, 16)
            sy.dma_start(gains[:, 1, :], g_final.partition_broadcast(P)).then_inc(gain2_in, 16)
            for m in range(2 * KD):
                w, c = (w_out_k, WIDE_ORDER[m]) if m < KD else (w_pg_k, m - KD)
                load(N_FB + m, (N_FB + m) % 2, w[:, :, c * P:(c + 1) * P])
                if m == 1:
                    area_free(sy, 8)
                    for b in range(TB):
                        sy.dma_start(x1[:, b, :], x_rows[b * P:(b + 1) * P, :]).then_inc(x2_in[b], 16)
            for q in range(2 * TB):
                ch, b = divmod(q, TB)
                if q >= 2:
                    sy.wait_ge(gate_used, q - 1)
                sy.dma_start(pin2[:, q % 2, :], pe_d[b * P:(b + 1) * P, ch * BANK:(ch + 1) * BANK]
                             ).then_inc(pe_in[q % 2], 16)

        @block.gpsimd
        def _(pool):
            g = nc.gpsimd
            g.sem_inc(w_ready, 2)
            steps = []

            def one(ins):
                steps.append(ins)
                ins.then_inc(const_ready, 1)
                pool.wait_ge(const_ready, len(steps))

            one(g.memset(ident[:, :], 0.0))
            one(g.affine_select(out=ident[:, :], in_=ident[:, :], compare_op=ALU.not_equal, fill=1.0, base=0,
                                pattern=[[-1, P]], channel_multiplier=1))
            one(g.memset(before01[:, :], 1.0))
            one(g.affine_select(out=before01[:, :], in_=before01[:, :], compare_op=ALU.is_gt, fill=0.0, base=0,
                                pattern=[[-1, P]], channel_multiplier=1))
            one(g.memset(before_cap[:, :], 3e38))
            one(g.affine_select(out=before_cap[:, :], in_=before_cap[:, :], compare_op=ALU.is_gt, fill=-1e30, base=0,
                                pattern=[[-1, P]], channel_multiplier=1))
            one(g.memset(m_past[:, :], 1.0))
            one(g.affine_select(out=m_past[:, :], in_=m_past[:, :], compare_op=ALU.is_ge, fill=0.0, base=0,
                                pattern=[[1, P]], channel_multiplier=-1))
            one(g.memset(m_past[0:CHUNK, CHUNK:P], 0.0))
            one(g.memset(m_fut[:, :], 1.0))
            one(g.affine_select(out=m_fut[:, :], in_=m_fut[:, :], compare_op=ALU.is_gt, fill=0.0, base=0,
                                pattern=[[-1, P]], channel_multiplier=1))
            one(g.memset(m_fut[CHUNK:P, 0:CHUNK], 0.0))
            one(g.memset(m_cross[:, :], 0.0))
            one(g.memset(m_cross[0:CHUNK, CHUNK:P], 1.0))
            one(g.memset(two_c[:, :, :], 1.0))
            one(g.memset(two_k[:, :, :], 1.0))
            one(g.memset(epsc[:, :], EPS))

            def split(n, half_n, slot, hi, lo):
                pool.wait_ge(w_in_s[slot], 16 * half_n + 16)
                stand_alone(pool)
                g.tensor_scalar(hi, RAW[:, slot, :, :], 1.0, 1.0, ALU.mult, ALU.mult).then_inc(w_hi, 1)
                pool.wait_ge(w_hi, n + 1)
                g.tensor_tensor(lo, RAW[:, slot, :, :], hi.bitcast(F32), ALU.subtract).then_inc(w_ready, 1)

            def split_ring(n, half_n, slot):
                pool.wait_ge(q_full, 2 * n + 2)
                split(n, half_n, slot, WS[:, slot, HI, :, :], WS[:, slot, LO, :, :])

            with pool.Fori(0, N_FB // 2) as j:
                for par in range(2):
                    split_ring(2 * j + par, j, par)
            if N_FB % 2:
                split_ring(N_FB - 1, N_FB // 2, 0)
            for m in range(2 * KD):
                n, half = N_FB + m, m // 4
                c = (WIDE_ORDER[m] if m < KD else m) % 4
                if half == 0 and c:
                    pool.wait_ge(pj_taken, SPARE + J_FB + 24 + 4 * c)
                elif half == 0:
                    pool.wait_ge(q_full, 4 + 2 * (N_FB - 1))
                elif m == 4:
                    area_free(pool, 8)
                elif half >= 2:
                    pool.wait_ge(d_full, TB * (half - 1))
                split(n, n // 2, n % 2, WD[half % 2][:, c, HI, :, :], WD[half % 2][:, c, LO, :, :])

        @block.tensor
        def _(pe):
            t = nc.tensor
            pe.sem_inc(pj_taken, 2)
            pe.sem_inc(q_full, 4)
            pe.sem_inc(o_full, 2)
            pe.sem_inc(g_tr_full, 2)
            pe.sem_inc(pv_full, 1)

            pe.wait_ge(const_ready, 2)
            pe.wait_ge(p_in, 16)
            for r in range(TB // 2):
                if r >= 2:
                    pe.wait_ge(p_lo, r - 1)
                for j in range(4):
                    k, b = j // 2, 2 * r + j % 2
                    mm = t.transpose(trs[r % 2][:, j * P:(j + 1) * P], pin[:, b, k * P:(k + 1) * P], ident[:, :])
                mm.then_inc(p_full, 1)

            def turn_x(b):
                pe.wait_ge(x_norm, b + 1)
                for r in (2 * b, 2 * b + 1):
                    if r >= 4:
                        pe.wait_ge(xt_lo, r - 3)
                    for j in range(4):
                        k = 4 * (r % 2) + j
                        mm = t.transpose(ring[r % 4][:, j * P:(j + 1) * P], xin[:, b, k * P:(k + 1) * P], ident[:, :])
                    mm.then_inc(xt_full, 1)

            pe.wait_ge(wpe_lo, 1)
            pe.wait_ge(p_lo, TB // 2)
            for b in range(TB):
                for ch in range(NH):
                    pe.wait_ge(pj_taken, J_P + 2 * b + ch + 1)
                    product(pj[ch][:, :], lambda a, k: pT[:, a, k, b * P:(b + 1) * P],
                            lambda a, k: wpe[:, a, k, ch * BANK:(ch + 1) * BANK], PK).then_inc(pe_full, 1)
                if b > 0:
                    turn_x(b - 1)
            turn_x(TB - 1)
            phase_end(pe, pe_phase, 0)

            def quantum(n, slot, hf, rhs, use, bank_=None, part=None):
                if hf == 0 and part != 1:
                    pe.wait_ge(w_ready, n + 3)
                if part != 1:
                    pe.wait_ge(pj_taken, use + 1)
                o = pj[hf if bank_ is None else bank_][:, :]
                steps = [(k, a, b) for k in range(KD) for a, b in PASSES]
                half = len(steps) // 2
                mine = range(len(steps)) if part is None else range(part * half, (part + 1) * half)
                for i in mine:
                    k, a, b = steps[i]
                    mm = t.matmul(o, WS[:, slot, a, k, :], rhs[:, b, k, hf * BANK:(hf + 1) * BANK], start=i == 0,
                                  stop=i == len(steps) - 1)
                if part != 0:
                    mm.then_inc(q_full, 1)

            pe.sem_inc(g_tr_taken, 2)
            pe.wait_ge(xt_lo, 2 * TB)
            for hf in range(NH):
                quantum(0, 0, hf, HT, J_A + hf)
            pe.wait_ge(params_in, 48)
            pe.wait_ge(pj_taken, SPARE + J_A + 2)
            for r in range(2 * GH):
                h, hf = divmod(r, 2)
                if r >= 2:
                    pe.wait_ge(y_min, r - 1)
                t.matmul(trs[hf][:, :], walp[:, h * P:(h + 1) * P], lrT[:, hf * BANK:(hf + 1) * BANK],
                         start=True, stop=True).then_inc(y_full, 1)

            def gla_quantum(h, i, part=None):
                c, hf = divmod(i, 2)
                quantum(N_A0 + c + 4 * h, (N_A0 + c) % 2, hf, HT, J_A + 2 + i + 8 * h, part=part)

            for i in range(8):
                gla_quantum(0, i)
            pe.wait_ge(y_min, 2 * GH)

            with pe.Fori(0, GH) as h:

                def tr_round(r):
                    pe.wait_ge(g_tr_taken, r + 1 + 14 * h)
                    return trs[r % 2]

                pe.wait_ge(pj_taken, SPARE + J_A + 6 + 8 * h)
                for r in range(4):
                    o = tr_round(r)
                    for j in range(4):
                        b, v = 2 * r + j // 2, j % 2
                        mm = t.transpose(o[:, j * P:(j + 1) * P], qkv[:, v, b * P:(b + 1) * P], ident[:, :])
                    mm.then_inc(g_tr_full, 1)
                for i in range(4):
                    gla_quantum(h + 1, i)
                pe.wait_ge(kS_ready, h + 1)
                for r in range(4, 6):
                    o = tr_round(r)
                    for j in range(4):
                        b = 4 * (r - 4) + j
                        mm = t.transpose(o[:, j * P:(j + 1) * P], A_enb[:, b * P:(b + 1) * P], ident[:, :])
                    mm.then_inc(g_tr_full, 1)
                pe.wait_ge(qS_ready, h + 1)

                def scores(b):
                    cols = slice(b * P, (b + 1) * P)
                    pe.wait_ge(attn_ready, b + 1 + 8 * h)
                    o = SBK[b % 2]
                    t.matmul(o[:, 0:P], A_kd[:, cols], A_qd[:, cols], start=True, stop=True)
                    t.matmul(o[:, P:2 * P], A_ki[:, cols], A_qi[:, cols], start=True, stop=True)
                    t.matmul(o[:, 2 * P:3 * P], A_ke[:, cols], A_qd[:, cols], start=True, stop=True).then_inc(s_full, 1)

                def turn(b):
                    o = tr_round(6 + b)
                    pe.wait_ge(on_ready, b + 3 + 8 * h)
                    for v in range(2):
                        mm = t.transpose(o[:, v * P:(v + 1) * P], on[:, b % 2, v * P:(v + 1) * P], ident[:, :])
                    mm.then_inc(g_tr_full, 1)

                scores(0)
                for b in range(TB):
                    cols = slice(b * P, (b + 1) * P)
                    if b < TB - 1:
                        scores(b + 1)
                    gla_quantum(h + 1, 4 + b // 2, part=b % 2)
                    if b == 0:
                        pe.wait_ge(g_tr_taken, 8 + 14 * h)
                    pe.wait_ge(attn_ready, b + 3 + 8 * h)
                    pe.wait_ge(on_ready, b + 1 + 8 * h)
                    o = OBK[b % 2]
                    mm = t.matmul(o[:, 0:DV], attn[:, b % 2, :], VN[:, b, :], start=True, stop=b == 0)
                    if b > 0:
                        pe.wait_ge(st_ready, b + 1 + 7 * h)
                        mm = t.matmul(o[:, 0:DV], A_eb[:, cols], St[:, b % 2, :], start=False, stop=True)
                    if b < TB - 1:
                        mm = t.matmul(o[:, DV:2 * DV], KN[:, b, :], VN[:, b, :], start=True, stop=True)
                    mm.then_inc(o_full, 1)
                    if b > 0:
                        turn(b - 1)
                turn(TB - 1)
            phase_end(pe, pe_phase, 1)

            def finish(br, n0, j0, k0):
                s = fin[br]
                with pe.Fori(0, 2) as j:
                    for par in range(2):
                        for hf in range(NH):
                            quantum(n0 + 4 + par + 2 * j, (n0 + par) % 2, hf, HT, j0 + 2 * par + hf + 4 * j)
                phase_end(pe, pe_phase, k0)
                for part, rhs in ((1, HT), (2, OA)):
                    if part == 2:
                        pe.wait_ge(s["oa_ready"], 4 + 2 * KD)
                    with pe.Fori(0, KD // 2) as j:
                        for par in range(2):
                            n = n0 + part * KD + par
                            for hf in range(NH):
                                quantum(n + 2 * j, n % 2, hf, rhs, j0 + 16 * part - 8 + 2 * par + hf + 4 * j)
                    phase_end(pe, pe_phase, k0 + part)

            finish("A", N_A, J_FA, 2)

            def sb_quantum(h, par, i, use, bank_, part=None):
                c, hf = divmod(i, 2)
                n = N_FA + 3 * par + c
                quantum(n - 3 * par + 3 * h, n % 2, hf, HT, use, bank_, part)

            for i in range(6):
                sb_quantum(0, 0, i, J_B + i, i % 2)

            def sb_head(h, par, last):
                extra = EXTRA_LAST if last else EXTRA
                use = uses(extra)

                def rounds(some):
                    for kind, r, j, b0, nb in some:
                        pe.wait_ge(b_tr_lo, r + 1 + SB_ROUNDS * h)
                        if kind == "w":
                            pe.wait_ge(w_done, j + 1 + 8 * h)
                        for m in range(nb):
                            src = vT if kind == "v" else T2[:, j % 2, :]
                            mm = t.transpose(trs[r % 2][:, m * P:(m + 1) * P], src[:, (b0 + m) * P:(b0 + m + 1) * P],
                                             ident[:, :])
                        mm.then_inc(b_tr_full, 1)

                def weigh_values(gq):
                    n = use["pv", gq]
                    pe.wait_ge(pj_taken, J_B + 6 + n + 1 + 8 * h)
                    pe.wait_ge(b_tr_lo, (6 if gq == 0 else SB_ROUNDS) + 2 + SB_ROUNDS * h)
                    steps = [(sb, a, c) for sb in range(4 * gq + 4) for a, c in PASSES]
                    for i, (sb, a, c) in enumerate(steps):
                        lo = max(0, sb - 4 * gq) * P
                        mm = t.matmul(pj[n % 2][:, lo:BANK], VS[:, a, sb, :], WT[:, c, sb, lo:BANK], start=i == 0,
                                      stop=i == len(steps) - 1)
                    mm.then_inc(pv_full, 1)

                for i in range(TB + 3):
                    before, after = sb_rounds(i) if i < TB + 2 else ([], [])
                    for e in extra.get(i, []):
                        if e[0] == "pv":
                            weigh_values(e[1])
                    rounds(before)
                    if i < TB:
                        if i == 0:
                            pe.wait_ge(pj_taken, SPARE + J_B + 6 + 8 * h)
                        pe.wait_ge(y_done, i + 1 + 8 * h)
                        for c0, c1 in z_pieces(i):
                            for n, (a, c) in enumerate(PASSES):
                                mm = t.matmul(zs[i % 2][:, c0:c1], QK[:, par, 0, a, i * P:(i + 1) * P],
                                              QK[:, par, 1, c, c0:c1], start=n == 0, stop=n == 2)
                        mm.then_inc(z_full, 1)
                    rounds(after)
                    for e in extra.get(i, []):
                        if e[0] == "q":
                            n = use["q", e[1]]
                            if last:
                                c, hf = divmod(e[1], 2)
                                quantum(N_B + c, (N_B + c) % 2, hf, HT, J_B + 6 + 8 * (SH - 1) + n, n % 2, e[2])
                            else:
                                sb_quantum(h + 1, 1 - par, e[1], J_B + 6 + n + 8 * h, n % 2, e[2])

            with pe.Fori(0, SH // 2 - 1) as j:
                for par in range(2):
                    sb_head(2 * j + par, par, False)
            sb_head(SH - 2, 0, False)
            sb_head(SH - 1, 1, True)
            phase_end(pe, pe_phase, 5)

            finish("B", N_B, J_FB, 6)

            def wide(q, half):
                b = q % TB
                pe.wait_ge(pj_taken, J_D + q + 1)
                product(pj[q % 2][:, :], lambda a, k: HT[:, a, k, b * P:(b + 1) * P],
                        lambda a, k: WD[half % 2][:, :, a, k, :], KD).then_inc(d_full, 1)

            def turn_u(b):
                pe.wait_ge(u_ready, b + 1)
                for r in (2 * b, 2 * b + 1):
                    if r >= 4:
                        pe.wait_ge(ut_lo, r - 3)
                    for j in range(4):
                        k = 4 * (r % 2) + j
                        mm = t.transpose(ring[r % 4][:, j * P:(j + 1) * P], u[:, b % 2, k * P:(k + 1) * P], ident[:, :])
                    mm.then_inc(ut_full, 1)

            pe.wait_ge(fin["B"]["ylo"], 2 * KD)
            for q in range(2 * TB):
                if q % TB == 0:
                    pe.wait_ge(w_ready, N_FB + 4 * (q // TB + 1) + 2)
                wide(q, q // TB)
                if q >= TB + 2:
                    turn_u(q - TB - 2)
            for q in range(2 * TB, 4 * TB):
                if q < 2 * TB + 2:
                    turn_u(q - TB - 2)
                if q % TB == 0:
                    pe.wait_ge(w_ready, N_FB + 4 * (q // TB + 1) + 2)
                if q < 3 * TB:
                    pe.wait_ge(ut_lo, 2 * (q - 2 * TB) + 2)
                wide(q, q // TB)

        @block.scalar
        def _(act):
            s = nc.scalar
            s.preload_act_table_set(EXP_LN)
            s.sem_inc(oT_out, 1)
            s.sem_inc(ob_out[0], 1)
            s.sem_inc(ob_out[1], 1)

            def copy(out_, in_, scale=1.0):
                return s.activation(out_, in_, ACT.Copy, scale=scale)

            def inverse_rms(src, n, i, width, sq, ln, inv, count, junk):
                s.activation(junk, src, ACT.Square, accum_out=ssq[:, i:i + 1]).then_inc(sq, 1)
                act.wait_ge(sq, count)
                s.activation(lnm[:, i:i + 1], ssq[:, i:i + 1], ACT.Ln, bias=epsc[:, 0:1],
                             scale=1.0 / width).then_inc(ln, 1)
                act.wait_ge(ln, count)
                return s.activation(rstd[:, i:i + 1], lnm[:, i:i + 1], ACT.Exp, scale=-0.5).then_inc(inv, 1)

            for r in range(TB // 2):
                act.wait_ge(p_full, r + 1)
                copy(pT[:, HI, :, 2 * r * P:(2 * r + 2) * P],
                     trs[r % 2][:, :].rearrange("p (k n) -> p k n", k=PK)).then_inc(p_hi, 1)

            def take_x(b):
                for r in (2 * b, 2 * b + 1):
                    k = 4 * (r % 2)
                    act.wait_ge(xt_full, r + 1)
                    copy(HT[:, HI, k:k + 4, b * P:(b + 1) * P],
                         ring[r % 4].rearrange("p (k n) -> p k n", k=4)).then_inc(xt_hi, 1)

            act.wait_ge(const_ready, 17)
            for b in range(TB):
                act.wait_ge(x_in[b], 16)
                if b:
                    act.wait_ge(x_sq, b)
                inverse_rms(xin[:, b, :], T, b, D, x_sq, x_ln, x_rstd, b + 1, junk0[:, :])
                for q in (2 * b, 2 * b + 1):
                    act.wait_ge(pe_full, q + 1)
                    if q >= 2:
                        act.wait_ge(pe_out[q % 2], 16 * (q // 2))
                    copy(pes[:, q % 2, :], pj[q % 2][:, :]).then_inc(pj_taken, 1)
                    act.wait_ge(pj_taken, SPARE + J_P + q + 1)
                    act.dma_start(pe_d[b * P:(b + 1) * P, (q % 2) * BANK:(q % 2 + 1) * BANK],
                                  pes[:, q % 2, :]).then_inc(pe_out[q % 2], 16)
                if b:
                    take_x(b - 1)
            take_x(TB - 1)
            act.wait_ge(pe_out[0], 16 * TB)
            act.wait_ge(pe_out[1], 16 * TB)
            phase_end(act, act_phase, 0)

            def quantum_in(q):
                act.wait_ge(q_full, 5 + q)

            for hf in range(NH):
                quantum_in(hf)
                copy(lrT[:, hf * BANK:(hf + 1) * BANK], pj[hf][0:RANK, :]).then_inc(pj_taken, 1)
            act.wait_ge(params_in, 48)
            tmp = [A_ke, A_qd]

            def take_qkv(h, i):
                c, hf = divmod(i, 2)
                quantum_in(2 + i + 8 * h)
                if c >= 2:
                    act.wait_ge(qS_ready, h)
                copy(qkv[:, c, hf * BANK:(hf + 1) * BANK], pj[hf][:, :]).then_inc(pj_taken, 1)

            for h in range(GH):
                for hf in range(NH):
                    r = 2 * h + hf
                    act.wait_ge(y_full, r + 1)
                    if h >= 2 and hf == 0:
                        act.wait_ge(y_ls, h - 1)
                    s.activation(tmp[h % 2][:, hf * BANK:(hf + 1) * BANK], trs[hf][:, :], ACT.Abs,
                                 bias=balp[:, h:h + 1]).then_inc(y_abs, 1)
                act.wait_ge(y_abs, 2 * h + 2)
                s.activation(tmp[h % 2][:, :], tmp[h % 2][:, :], ACT.Exp, scale=-1.0).then_inc(y_exp, 1)
                act.wait_ge(y_exp, h + 1)
                s.activation(tmp[h % 2][:, :], tmp[h % 2][:, :], ACT.Ln, bias=1.0).then_inc(y_ln, 1)
            for i in range(8):
                c, hf = divmod(i, 2)
                quantum_in(2 + i)
                copy(qkv[:, c, hf * BANK:(hf + 1) * BANK], pj[hf][:, :]).then_inc(pj_taken, 1)
            act.wait_ge(y_cum, GH)

            with act.Fori(0, GH) as h:

                def take_round(r, out_):
                    act.wait_ge(g_tr_full, r + 3 + 14 * h)
                    return copy(out_, trs[r % 2][:, :]).then_inc(g_tr_taken, 1)

                for r in range(4):
                    take_round(r, VN[:, 2 * r:2 * r + 2, :].rearrange("p b v -> p (b v)"))
                act.wait_ge(o_full, 2 + 8 * h)
                stand_alone(act)
                yh = Y[:, bass.ds(h, 1), :].rearrange("p a t -> p (a t)")
                s.activation(A_eb[:, :], yh, ACT.Exp, scale=1.0 / TAU).then_inc(e_done, 1)
                s.activation(A_enb[:, :], yh, ACT.Exp, scale=-1.0 / TAU).then_inc(e_done, 1)
                act.wait_ge(dd_done, h + 1)
                s.activation(A_ke[:, :], A_ke[:, :], ACT.Exp, scale=1.0 / TAU).then_inc(ke_done, 1)
                for i in range(4):
                    take_qkv(h + 1, i)
                for r in range(4, 6):
                    take_round(r, KN[:, 4 * (r - 4):4 * (r - 4) + 4, :].rearrange("p b d -> p (b d)"))

                def take_turned(b):
                    r = 6 + b
                    act.wait_ge(g_tr_full, r + 3 + 14 * h)
                    if b == 0:
                        act.wait_ge(oT_out, 1 + 16 * h)
                    stand_alone(act)
                    for v in range(2):
                        i = copy(oT[:, v, b * P:(b + 1) * P], trs[r % 2][:, v * P:(v + 1) * P],
                                 ggla[:, bass.ds(2 * h + v, 1)])
                    i.then_inc(g_tr_taken, 1)

                for b in range(TB):
                    if b % 2 == 1:
                        take_qkv(h + 1, 4 + b // 2)
                    act.wait_ge(o_full, b + 3 + 8 * h)
                    act.wait_ge(on_ready, b + 1 + 8 * h)
                    if b < TB - 1:
                        act.wait_ge(st_ready, b + 2 + 7 * h)
                    i = b % 2
                    c = b + 1 + 8 * h
                    s.activation(junkA[:, :], OBK[i][:, 0:DV], ACT.Square, accum_out=ssq[:, i:i + 1]).then_inc(o_sq, 1)
                    act.wait_ge(o_sq, c)
                    s.activation(lnm[:, i:i + 1], ssq[:, i:i + 1], ACT.Ln, bias=epsc[:, 0:1],
                                 scale=1.0 / DV).then_inc(o_ln, 1)
                    act.wait_ge(o_ln, c)
                    s.activation(rstd[:, i:i + 1], lnm[:, i:i + 1], ACT.Exp, scale=-0.5).then_inc(o_rstd, 1)
                    if b > 0:
                        take_turned(b - 1)
                take_turned(TB - 1)
                act.wait_ge(g_tr_taken, 16 + 14 * h)
                act.dma_start(o_gla_d[bass.ds(DV * h, DV), :].rearrange("(v p) t -> p v t", p=P),
                              oT[:, :, :]).then_inc(oT_out, 16)
            phase_end(act, act_phase, 1)

            def finish(br, n0, j0, k0):
                f = fin[br]
                s.preload_act_table_set(SIGMOID)
                with act.Fori(0, 4) as i:
                    for t in range(4):
                        hf = t % 2
                        if t < 2:
                            act.wait_ge(q_full, 2 * (n0 + 4) + hf + 5 + 2 * i)
                            src = pj[hf][:, :]
                        else:
                            src = early[br][:, bass.ds(i, 1), hf * BANK:(hf + 1) * BANK].rearrange("p a t -> p (a t)")
                        act.wait_ge(f["oa_ready"], t + 3 + 4 * i)
                        stand_alone(act)
                        s.activation(sg[:, hf, :], src, ACT.Sigmoid).then_inc(f["sg_ready"], 1)
                phase_end(act, act_phase, k0)
                with act.Fori(0, KD // 2) as j:
                    for par in range(2):
                        for hf in range(NH):
                            q = 2 * par + hf
                            act.wait_ge(q_full, 2 * (n0 + KD) + q + 5 + 4 * j)
                            stand_alone(act)
                            s.activation(SM[:, bass.ds(2 * j + par, 1), hf * BANK:(hf + 1) * BANK].rearrange(
                                "p a t -> p (a t)"), pj[hf][:, :], ACT.Sigmoid).then_inc(pj_taken, 1)
                s.preload_act_table_set(EXP_LN)
                phase_end(act, act_phase, k0 + 1)
                if br == "A":
                    with act.Fori(0, KD // 2) as j:
                        for par in range(2):
                            for hf in range(NH):
                                act.wait_ge(pj_taken, SPARE + j0 + 24 + 2 * par + hf + 1 + 4 * j)
                                act.dma_start(ya_d[bass.ds(P * (2 * j + par), P), hf * BANK:(hf + 1) * BANK],
                                              ys[:, hf, :]).then_inc(f[f"yio{hf}"], 16)
                phase_end(act, act_phase, k0 + 2)

            finish("A", N_A, J_FA, 2)

            def take_high(h, par, i, bank_):
                c, hf = divmod(i, 2)
                act.wait_ge(q_full, 2 * N_FA + 5 + i + 6 * h)
                copy(QK[:, par, c, HI, hf * BANK:(hf + 1) * BANK], pj[bank_][:, :],
                     Q_SCALE if c == 0 else 1.0).then_inc(b_hi, 1)

            for i in range(4):
                take_high(0, 0, i, i % 2)

            def sb_head(h, par, last):
                extra = EXTRA_LAST if last else EXTRA
                use = uses(extra)

                def take_rounds(some):
                    for kind, r, j, b0, nb in some:
                        act.wait_ge(b_tr_full, r + 1 + SB_ROUNDS * h)
                        src = trs[r % 2][:, 0:nb * P].rearrange("p (b t) -> p b t", b=nb)
                        if kind == "v":
                            copy(VS[:, HI, b0:b0 + nb, :], src).then_inc(b_tr_hi, 1)
                        else:
                            act.wait_ge(pv_full, (2 if j >= 4 else 1) + 2 * h)
                            c0 = (j % 4) * P
                            copy(WT[:, HI, b0:b0 + nb, c0:c0 + P], src).then_inc(b_tr_hi, 1)

                def store_outputs(gq):
                    act.wait_ge(pj_taken, SPARE + J_B + 6 + use["pv", gq] + 1 + 8 * h)
                    act.dma_start(o_sb_d[bass.ds(P * h, P), gq * BANK:(gq + 1) * BANK],
                                  oS[:, gq, :]).then_inc(ob_out[gq], 16)

                for i in range(TB + 3):
                    before, after = sb_rounds(i) if i < TB + 2 else ([], [])
                    w = (i + 1) * P
                    c = i + 1 + 8 * h
                    a = T1[:, i % 2, 0:w] if i < TB else None
                    take_rounds(before)
                    if i < TB:
                        act.wait_ge(z_full, c)
                        s.activation(a, zs[i % 2][:, 0:w], ACT.Abs).then_inc(z_abs, 1)
                    take_rounds(after)
                    if i < TB:
                        act.wait_ge(z_abs, c)
                        s.activation(a, a, ACT.Exp, scale=-1.0).then_inc(z_exp, 1)
                        act.wait_ge(z_exp, c)
                        s.activation(a, a, ACT.Ln, bias=1.0).then_inc(z_ln, 1)
                    if 1 <= i <= TB:
                        act.wait_ge(ym, i + 8 * h)
                        v = T2[:, (i - 1) % 2, 0:i * P]
                        s.activation(v, v, ACT.Exp).then_inc(w_done, 1)
                    for n, e in finished(extra, i):
                        if e[0] == "q" and e[1] < 4 and not last:
                            take_high(h + 1, 1 - par, e[1], n % 2)
                    if i == 7:
                        store_outputs(0)
                store_outputs(1)

            with act.Fori(0, SH // 2 - 1) as j:
                for par in range(2):
                    sb_head(2 * j + par, par, False)
            sb_head(SH - 2, 0, False)
            sb_head(SH - 1, 1, True)
            phase_end(act, act_phase, 5)

            finish("B", N_B, J_FB, 6)

            def u_rms(b):
                act.wait_ge(pj_taken, SPARE + J_D + TB + b + 1)
                if b >= 1:
                    act.wait_ge(u_sq, b)
                inverse_rms(x1[:, b, :], D, b, D, u_sq, u_ln, u_rstd, b + 1, junkD[:, :])

            def take_u(b):
                for r in (2 * b, 2 * b + 1):
                    act.wait_ge(ut_full, r + 1)
                    copy(HT[:, HI, 4 * (r % 2):4 * (r % 2) + 4, b * P:(b + 1) * P],
                         ring[r % 4].rearrange("p (k n) -> p k n", k=4)).then_inc(ut_hi, 1)

            for b in range(TB):
                u_rms(b)
                if b >= 2:
                    take_u(b - 2)
            for b in range(TB - 2, TB):
                take_u(b)

            def final_rms(b):
                act.wait_ge(x2_ready, TB + b + 1)
                if b >= 1:
                    act.wait_ge(f_sq, b)
                inverse_rms(x1[:, b, :], D, b, D, f_sq, f_ln, f_rstd, b + 1, junkD[:, :])

            def store(b):
                act.wait_ge(f_ready, b + 1)
                act.dma_start(out_rows[b * P:(b + 1) * P, :], u[:, b % 2, :]).then_inc(out_done[b % 2], 16)

            act.wait_ge(pj_taken, SPARE + J_D + 2 * TB)
            for q in range(2 * TB):
                if q == 0 or q > TB + 1:
                    s.preload_act_table_set(SIGMOID)
                act.wait_ge(d_full, 2 * TB + q + 1)
                if q >= 2:
                    act.wait_ge(x2_ready, q - 1)
                s.activation(sgD[:, q % 2, :], pj[q % 2][:, :], ACT.Sigmoid).then_inc(pj_taken, 1)
                if q >= TB + 1:
                    s.preload_act_table_set(EXP_LN)
                    final_rms(q - TB - 1)
                    if q >= TB + 2:
                        store(q - TB - 2)
            final_rms(TB - 1)
            store(TB - 2)
            store(TB - 1)
            for i in range(2):
                act.wait_ge(out_done[i], 16 * (TB // 2))

        @block.vector
        def _(dve):
            v = nc.vector
            v.sem_inc(attn_ready, 2)
            v.sem_inc(st_ready, 1)
            v.sem_inc(on_ready, 2)
            v.sem_inc(y_done, 2)
            v.sem_inc(b_tr_lo, 2)
            for br in "AB":
                v.sem_inc(fin[br]["oa_ready"], 4)
                v.sem_inc(fin[br]["ysum"], 2)
            v.sem_inc(fin["A"]["yio0"], 1)
            v.sem_inc(fin["A"]["yio1"], 1)

            def rest(out_, whole, hi):
                return v.tensor_tensor(out_, whole, hi.bitcast(F32), ALU.subtract)

            dve.wait_ge(w_ple_in, 16)
            v.tensor_copy(wpe[:, HI, :, :], wpe_raw[:, :, :]).then_inc(wpe_hi, 1)
            dve.wait_ge(wpe_hi, 1)
            rest(wpe[:, LO, :, :], wpe_raw[:, :, :], wpe[:, HI, :, :]).then_inc(wpe_lo, 1)
            for r in range(TB // 2):
                dve.wait_ge(p_hi, r + 1)
                c = slice(2 * r * P, (2 * r + 2) * P)
                rest(pT[:, LO, :, c], trs[r % 2][:, :].rearrange("p (k n) -> p k n", k=PK),
                     pT[:, HI, :, c]).then_inc(p_lo, 1)
            dve.wait_ge(gain_in, 16)

            def rest_x(b):
                for r in (2 * b, 2 * b + 1):
                    dve.wait_ge(xt_hi, r + 1)
                    k, c = slice(4 * (r % 2), 4 * (r % 2) + 4), slice(b * P, (b + 1) * P)
                    rest(HT[:, LO, k, c], ring[r % 4].rearrange("p (k n) -> p k n", k=4),
                         HT[:, HI, k, c]).then_inc(xt_lo, 1)

            for b in range(TB):
                dve.wait_ge(x_rstd, b + 1)
                v.scalar_tensor_tensor(out=xin[:, b, :], in0=xin[:, b, :], scalar=rstd[:, b:b + 1],
                                       in1=gains[:, 0, :], op0=ALU.mult, op1=ALU.mult).then_inc(x_norm, 1)
                if b:
                    rest_x(b - 1)
            rest_x(TB - 1)
            phase_end(dve, dve_phase, 0)

            v.memset(newchunk[:, :], 1.0).then_inc(chunk_mask, 1)
            v.memset(attn[:, :, :], 0.0).then_inc(chunk_mask, 1)
            dve.wait_ge(chunk_mask, 2)
            v.memset(newchunk[:, :].rearrange("p (c t) -> p c t", t=CHUNK)[:, :, 0:1], 0.0).then_inc(chunk_mask, 1)
            dve.wait_ge(chunk_mask, 3)
            dve.wait_ge(params_in, 48)
            dve.wait_ge(const_ready, 17)
            tmp = [A_ke, A_qd]
            for h in range(GH):
                for hf in range(NH):
                    dve.wait_ge(y_abs, 2 * h + hf + 1)
                    v.tensor_scalar(Y[:, h, hf * BANK:(hf + 1) * BANK], trs[hf][:, :], balp[:, h:h + 1], 0.0,
                                    ALU.add, ALU.min).then_inc(y_min, 1)
                dve.wait_ge(y_min, 2 * h + 2)
                dve.wait_ge(y_ln, h + 1)
                v.tensor_tensor(Y[:, h, :], Y[:, h, :], tmp[h % 2][:, :], ALU.subtract).then_inc(y_ls, 1)
                dve.wait_ge(y_ls, h + 1)
                v.tensor_tensor_scan(Y[:, h, :], newchunk[:, :], Y[:, h, :], 0.0, ALU.mult, ALU.add).then_inc(y_cum, 1)
            dve.wait_ge(y_cum, GH)

            def chunks(a):
                return a.rearrange("p (c t) -> p c t", t=CHUNK)

            with dve.Fori(0, GH) as h:
                dve.wait_ge(o_full, 2 + 8 * h)
                yc = Y[:, bass.ds(h, 1), :].rearrange("p a (c t) -> p (a c) t", t=CHUNK)
                v.tensor_tensor(chunks(A_ke[:, :]), yc[:, :, CHUNK - 1:CHUNK].to_broadcast([P, T // CHUNK, CHUNK]),
                                yc, ALU.subtract).then_inc(dd_done, 1)
                dve.wait_ge(e_done, 1 + 2 * h)
                ends = A_eb[:, :].rearrange("p (b c t) -> p b c t", c=2, t=CHUNK)
                e0, e1 = ends[:, :, 0, CHUNK - 1], ends[:, :, 1, CHUNK - 1]
                v.tensor_copy(two_c[:, :, 1], e0).then_inc(dec_part, 1)
                v.tensor_copy(two_k[:, :, 0], e1).then_inc(dec_part, 1)
                v.tensor_tensor(dec[:, :], e0, e1, ALU.mult).then_inc(dec_part, 1)
                dve.wait_ge(pj_taken, SPARE + J_A + 2 + 8 + 8 * h)
                dve.wait_ge(e_done, 2 + 2 * h)
                q_, k_ = qkv[:, 2, :], qkv[:, 3, :]
                dve.wait_ge(ke_done, h + 1)
                v.tensor_tensor(A_ke[:, :], k_, A_ke[:, :], ALU.mult).then_inc(prep, 1)
                v.scalar_tensor_tensor(out=A_qd[:, :], in0=q_, scalar=Q_SCALE, in1=A_eb[:, :], op0=ALU.mult,
                                       op1=ALU.mult).then_inc(prep, 1)
                v.scalar_tensor_tensor(out=A_qi[:, :], in0=q_, scalar=Q_SCALE, in1=A_enb[:, :], op0=ALU.mult,
                                       op1=ALU.mult).then_inc(prep, 1)
                v.tensor_tensor(A_kd[:, :], k_, A_enb[:, :], ALU.mult).then_inc(prep, 1)
                v.tensor_tensor(A_ki[:, :], k_, A_eb[:, :], ALU.mult).then_inc(prep, 1)
                dve.wait_ge(prep, 5 + 5 * h)
                dve.wait_ge(dec_part, 3 + 3 * h)
                v.tensor_tensor(chunks(A_enb[:, :]), chunks(A_ke[:, :]),
                                two_k[:, :, :].rearrange("p b (c o) -> p (b c) o", o=1).to_broadcast(
                                    [P, T // CHUNK, CHUNK]), ALU.mult).then_inc(kS_ready, 1)
                v.tensor_tensor(chunks(A_eb[:, :]), chunks(A_qd[:, :]),
                                two_c[:, :, :].rearrange("p b (c o) -> p (b c) o", o=1).to_broadcast(
                                    [P, T // CHUNK, CHUNK]), ALU.mult).then_inc(qS_ready, 1)

                def mask(b):
                    dve.wait_ge(s_full, b + 1 + 8 * h)
                    dve.wait_ge(o_full, b + 1 + 8 * h)
                    stand_alone(dve)
                    a, o = attn[:, b % 2, :], SBK[b % 2]
                    c = 2 * b + 16 * h
                    v.copy_predicated(a, m_past[:, :].bitcast(U32), o[:, 0:P]).then_inc(attn_part, 1)
                    dve.wait_ge(attn_part, c + 1)
                    stand_alone(dve)
                    v.copy_predicated(a, m_fut[:, :].bitcast(U32), o[:, P:2 * P]).then_inc(attn_part, 1)
                    dve.wait_ge(attn_part, c + 2)
                    stand_alone(dve)
                    v.copy_predicated(a, m_cross[:, :].bitcast(U32), o[:, 2 * P:3 * P]).then_inc(attn_ready, 1)

                def update_state(b):
                    dve.wait_ge(o_full, b + 3 + 8 * h)
                    dve.wait_ge(st_ready, b + 1 + 7 * h)
                    update = OBK[b % 2][:, DV:2 * DV]
                    if b == 0:
                        v.tensor_copy(St[:, 1, :], update).then_inc(st_ready, 1)
                    else:
                        v.scalar_tensor_tensor(out=St[:, (b + 1) % 2, :], in0=St[:, b % 2, :], scalar=dec[:, b:b + 1],
                                               in1=update, op0=ALU.mult, op1=ALU.add).then_inc(st_ready, 1)

                def norm(b):
                    dve.wait_ge(o_rstd, b + 1 + 8 * h)
                    dve.wait_ge(g_tr_full, (b + 1 if b < 2 else b + 7) + 14 * h)
                    v.tensor_scalar(on[:, b % 2, :], OBK[b % 2][:, 0:DV], rstd[:, b % 2:b % 2 + 1], None,
                                    ALU.mult).then_inc(on_ready, 1)

                mask(0)
                for b in range(TB):
                    if b < TB - 1:
                        mask(b + 1)
                        update_state(b)
                    if b > 0:
                        norm(b - 1)
                norm(TB - 1)
            phase_end(dve, dve_phase, 1)

            def finish(br, n0, j0, k0, stored):
                f = fin[br]
                for e_sem, count in stored:
                    dve.wait_ge(e_sem, count)
                with dve.Fori(0, 4) as i:
                    for t in range(4):
                        hf, slot = t % 2, t // 2
                        c = slice(hf * BANK, (hf + 1) * BANK)
                        g_ = sg[:, hf, :]
                        dve.wait_ge(f["sg_ready"], t + 1 + 4 * i)
                        if slot == 0:
                            v.tensor_tensor(g_, pj[hf][:, :], g_, ALU.mult).then_inc(pj_taken, 1)
                            dve.wait_ge(pj_taken, SPARE + j0 + hf + 1 + 2 * i)
                        else:
                            gate = early[br][:, bass.ds(i, 1), c].rearrange("p a t -> p (a t)")
                            v.tensor_tensor(g_, gate, g_, ALU.mult).then_inc(f["gated"], 1)
                            dve.wait_ge(f["gated"], hf + 1 + 2 * i)
                        dve.wait_ge(f[f"oin{slot}"], 16 + 16 * i)
                        v.tensor_tensor(g_, g_, oin[:, slot, c], ALU.mult).then_inc(f["og"], 1)
                        dve.wait_ge(f["og"], t + 1 + 4 * i)

                        def dst(part):
                            return OA[:, part, bass.ds(i + 4 * (1 - slot), 1), c].rearrange("p a t -> p (a t)")
                        v.tensor_copy(dst(HI), g_).then_inc(f["hi"], 1)
                        dve.wait_ge(f["hi"], t + 1 + 4 * i)
                        rest(dst(LO), g_, dst(HI)).then_inc(f["oa_ready"], 1)
                phase_end(dve, dve_phase, k0)
                phase_end(dve, dve_phase, k0 + 1)
                if br == "B":
                    for hf in range(NH):
                        dve.wait_ge(fin["A"][f"yio{hf}"], 16 * KD + 1)
                with dve.Fori(0, KD // 2) as j:
                    for par in range(2):
                        for hf in range(NH):
                            q = 2 * par + hf
                            e = 2 * j + par
                            c = slice(hf * BANK, (hf + 1) * BANK)
                            dve.wait_ge(q_full, 2 * (n0 + 2 * KD) + q + 5 + 4 * j)
                            y_ = ys[:, hf, :]
                            if br == "A":
                                dve.wait_ge(f[f"yio{hf}"], 1 + 16 * e)
                            m = SM[:, bass.ds(e, 1), c].rearrange("p a t -> p (a t)")
                            v.tensor_tensor(y_, pj[hf][:, :], m, ALU.mult).then_inc(pj_taken, 1)
                            if br == "A":
                                continue
                            dve.wait_ge(pj_taken, SPARE + j0 + 24 + q + 1 + 4 * j)
                            dve.wait_ge(f[f"yio{hf}"], 16 + 16 * e)
                            v.tensor_tensor(y_, y_, yin[:, hf, :], ALU.add).then_inc(f["ysum"], 1)
                            dve.wait_ge(f["ysum"], q + 3 + 4 * j)

                            def dst(part):
                                return HT[:, part, bass.ds(e, 1), c].rearrange("p a t -> p (a t)")
                            v.tensor_copy(dst(HI), y_).then_inc(f["yhi"], 1)
                            dve.wait_ge(f["yhi"], q + 1 + 4 * j)
                            rest(dst(LO), y_, dst(HI)).then_inc(f["ylo"], 1)
                            dve.wait_ge(f["ylo"], q + 1 + 4 * j)
                phase_end(dve, dve_phase, k0 + 2)

            finish("A", N_A, J_FA, 2, [(oT_out, 16 * GH + 1)])

            def take_quantum(h, par, i, bank_):
                c, hf = divmod(i, 2)
                cols = slice(hf * BANK, (hf + 1) * BANK)
                if c == 2:
                    dve.wait_ge(q_full, 2 * N_FA + 5 + i + 6 * h)
                    v.tensor_copy(vT[:, cols], pj[bank_][:, :]).then_inc(pj_taken, 1)
                    return
                dve.wait_ge(b_hi, i + 1 + 4 * h)
                hi, lo = QK[:, par, c, HI, cols], QK[:, par, c, LO, cols]
                v.scalar_tensor_tensor(out=lo, in0=pj[bank_][:, :], scalar=Q_SCALE if c == 0 else 1.0,
                                       in1=hi.bitcast(F32), op0=ALU.mult, op1=ALU.subtract).then_inc(pj_taken, 1)

            for i in range(6):
                take_quantum(0, 0, i, i % 2)

            def sb_head(h, par, last):
                extra = EXTRA_LAST if last else EXTRA

                def take_rounds(some):
                    for kind, r, j, b0, nb in some:
                        dve.wait_ge(b_tr_hi, r + 1 + SB_ROUNDS * h)
                        src = trs[r % 2][:, 0:nb * P].rearrange("p (b t) -> p b t", b=nb)
                        if kind == "v":
                            rest(VS[:, LO, b0:b0 + nb, :], src, VS[:, HI, b0:b0 + nb, :]).then_inc(b_tr_lo, 1)
                        else:
                            c0 = (j % 4) * P
                            rest(WT[:, LO, b0:b0 + nb, c0:c0 + P], src,
                                 WT[:, HI, b0:b0 + nb, c0:c0 + P]).then_inc(b_tr_lo, 1)

                def take_outputs(gq, bank_):
                    dve.wait_ge(pv_full, gq + 2 + 2 * h)
                    dve.wait_ge(ob_out[gq], 1 + 16 * h)
                    v.tensor_copy(oS[:, gq, :], pj[bank_][:, :]).then_inc(pj_taken, 1)

                def take_gate(i, bank_):
                    c, hf = divmod(i, 2)
                    dve.wait_ge(q_full, 2 * N_B + i + 5)
                    v.tensor_copy(graw[:, c, hf * BANK:(hf + 1) * BANK], pj[bank_][:, :]).then_inc(pj_taken, 1)

                for i in range(TB + 3):
                    before, after = sb_rounds(i) if i < TB + 2 else ([], [])
                    take_rounds(before)
                    take_rounds(after)
                    if i < TB:
                        w = (i + 1) * P
                        c = i + 1 + 8 * h
                        z, a, y = zs[i % 2][:, 0:w], T1[:, i % 2, 0:w], T2[:, i % 2, 0:w]
                        dve.wait_ge(z_ln, c)
                        v.scalar_tensor_tensor(out=a, in0=z, scalar=0.0, in1=a, op0=ALU.max,
                                               op1=ALU.add).then_inc(sp, 1)
                        dve.wait_ge(sp, c)
                        v.tensor_tensor(T1[:, i % 2, i * P:w], T1[:, i % 2, i * P:w], before01[:, :],
                                        ALU.mult).then_inc(spm, 1)
                        dve.wait_ge(spm, c)
                        v.tensor_tensor_scan(y[:, ::-1], a[:, ::-1], a[:, ::-1], 0.0, ALU.add,
                                             ALU.bypass).then_inc(cum, 1)
                        dve.wait_ge(cum, c)
                        v.tensor_tensor(y, z, y, ALU.subtract).then_inc(y_done, 1)
                        dve.wait_ge(y_done, c + 2)
                        v.tensor_tensor(T2[:, i % 2, i * P:w], T2[:, i % 2, i * P:w], before_cap[:, :],
                                        ALU.min).then_inc(ym, 1)
                    for n, e in finished(extra, i):
                        if e[0] == "pv":
                            take_outputs(e[1], n % 2)
                        elif last:
                            take_gate(e[1], n % 2)
                        else:
                            take_quantum(h + 1, 1 - par, e[1], n % 2)

            with dve.Fori(0, SH // 2 - 1) as j:
                for par in range(2):
                    sb_head(2 * j + par, par, False)
            sb_head(SH - 2, 0, False)
            sb_head(SH - 1, 1, True)
            phase_end(dve, dve_phase, 5)

            finish("B", N_B, J_FB, 6, [(ob_out[0], 16 * SH + 1), (ob_out[1], 16 * SH + 1)])

            dve.wait_ge(gain2_in, 32)

            def add_x(q):
                ch, b = divmod(q, TB)
                c = slice(ch * BANK, (ch + 1) * BANK)
                dve.wait_ge(d_full, q + 1)
                if ch == 0:
                    dve.wait_ge(x2_in[b], 16)
                v.tensor_tensor(x1[:, b, c], x1[:, b, c], pj[q % 2][:, :], ALU.add).then_inc(pj_taken, 1)

            def norm_u(b):
                dve.wait_ge(u_rstd, b + 1)
                if b >= 2:
                    dve.wait_ge(ut_full, 2 * b - 2)
                v.scalar_tensor_tensor(out=u[:, b % 2, :], in0=x1[:, b, :], scalar=rstd[:, b:b + 1],
                                       in1=gains[:, 0, :], op0=ALU.mult, op1=ALU.mult).then_inc(u_ready, 1)

            def rest_u(b):
                for r in (2 * b, 2 * b + 1):
                    dve.wait_ge(ut_hi, r + 1)
                    k, c = slice(4 * (r % 2), 4 * (r % 2) + 4), slice(b * P, (b + 1) * P)
                    rest(HT[:, LO, k, c], ring[r % 4].rearrange("p (k n) -> p k n", k=4),
                         HT[:, HI, k, c]).then_inc(ut_lo, 1)

            for q in range(2 * TB):
                add_x(q)
                if q >= TB + 1:
                    norm_u(q - TB - 1)
                if q >= TB + 2:
                    rest_u(q - TB - 2)
            norm_u(TB - 1)
            rest_u(TB - 2)
            rest_u(TB - 1)

            def norm_out(b):
                dve.wait_ge(f_rstd, b + 1)
                if b >= 2:
                    dve.wait_ge(out_done[b % 2], 16 * (b // 2))
                v.scalar_tensor_tensor(out=u[:, b % 2, :], in0=x1[:, b, :], scalar=rstd[:, b:b + 1],
                                       in1=gains[:, 1, :], op0=ALU.mult, op1=ALU.mult).then_inc(f_ready, 1)

            for q in range(2 * TB):
                ch, b = divmod(q, TB)
                c = slice(ch * BANK, (ch + 1) * BANK)
                dve.wait_ge(pj_taken, SPARE + J_D + 2 * TB + q + 1)
                dve.wait_ge(pe_in[q % 2], 16 * (q // 2 + 1))
                v.tensor_tensor(sgD[:, q % 2, :], sgD[:, q % 2, :], pin2[:, q % 2, :], ALU.mult).then_inc(gate_used, 1)
                dve.wait_ge(gate_used, q + 1)
                v.tensor_tensor(x1[:, b, c], x1[:, b, c], sgD[:, q % 2, :], ALU.add).then_inc(x2_ready, 1)
                if q >= TB + 2:
                    norm_out(q - TB - 2)
            norm_out(TB - 2)
            norm_out(TB - 1)


_INS = ["x", "p", "g_mix", "w_in", "w_alpha", "b_alpha", "g_gla_out", "w_out_gla", "w_out_sb", "w_out", "g_ple",
        "w_ple_gate", "w_ple", "g_final"]


def kernel(**inputs):
    import numpy as _np
    import concourse.bacc as _bacc
    from concourse import mybir as _mybir
    from concourse.bass_utils import run_bass_kernel_spmd as _run

    nc = _bacc.Bacc("TRN2", target_bir_lowering=False, num_devices=1)
    arrays, args = {}, []
    for name in _INS:
        a = _np.ascontiguousarray(inputs[name])
        arrays[f"in_{name}_dram"] = a
        args.append(nc.dram_tensor(f"in_{name}_dram", a.shape, _mybir.dt.from_np(a.dtype), kind="ExternalInput").ap())
    out = nc.dram_tensor("out_0_dram", inputs["x"].shape, _mybir.dt.from_np(_np.dtype("float32")),
                         kind="ExternalOutput").ap()
    hybrid_block(nc, *args, out)
    r = _run(nc, [arrays], core_ids=[0])
    return r.results[0]["out_0_dram"]
```

```python
from contextlib import ExitStack

import concourse.bass as bass
from concourse import mybir

F32 = mybir.dt.float32
F32R = mybir.dt.float32r
U32 = mybir.dt.uint32
ALU = mybir.AluOpType
ACT = mybir.ActivationFunctionType

P = 128
BANK = 512
CHUNK = 64
EPS = 1e-6
TAU = 16.0
EXP_LN = "natural_log_exp_and_others"
SIGMOID = "sigmoid_and_others"

HI, LO = 0, 1
PASSES = ((HI, HI), (HI, LO), (LO, HI))


def hybrid_block(nc, x, p, g_mix, w_in, w_alpha, b_alpha, g_gla_out, w_out_gla, w_out_sb, w_out, g_ple,
                 w_ple_gate, w_ple, g_final, out):
    T, D = x.shape[1], x.shape[2]
    TB, KD = T // P, D // P
    NH = T // BANK
    RANK, QKW = w_alpha.shape[1], w_alpha.shape[2]
    GH, DV = g_gla_out.shape[1], g_gla_out.shape[2]
    DK = QKW // GH
    SH = D // P
    PK = w_ple.shape[1] // P
    CPB = P // CHUNK
    assert DK == P and DV == 2 * P and CPB == 2 and NH == 2 and TB == 8 and KD == 8 and SH == 8
    Q_SCALE = float(P) ** -0.5

    widths = [QKW, QKW, GH * DV, RANK, GH * DV, D, D, D, D, D, D]
    QA, KA, VA, LR, GA, QB, KB, VB, GB, MA, MB = [sum(widths[:i]) for i in range(len(widths))]

    def by_k(w):
        return w.rearrange("(k p) n -> p k n", p=P)

    w_in_k, w_og_k, w_ob_k = by_k(w_in[0]), by_k(w_out_gla[0]), by_k(w_out_sb[0])
    w_out_k, w_pg_k, w_ple_k = by_k(w_out[0]), by_k(w_ple_gate[0]), by_k(w_ple[0])
    x_rows, p_rows, out_rows = x[0], p[0, 0], out[0]

    o_gla_d = nc.dram_tensor("o_gla_scratch", (D, T), F32, kind="Internal").ap()
    o_sb_d = nc.dram_tensor("o_sb_scratch", (D, T), F32, kind="Internal").ap()
    ya_d = nc.dram_tensor("ya_scratch", (D, T), F32, kind="Internal").ap()
    pe_d = nc.dram_tensor("pe_scratch", (T, D), F32, kind="Internal").ap()

    KB_ = 1024
    base = (nc.sbuf_base + 63) // 64 * 64

    def place(name, shape, dt, at):
        return nc.alloc_sbuf_tensor_at(name, shape, dt, offset=base + at)

    HT = place("HT", [P, 2, KD, T], F32R, 0)
    RAW = place("RAW", [P, 2, KD, P], F32, 64 * KB_)
    WS = place("WS", [P, 2, 2, KD, P], F32R, 72 * KB_)
    AREA = 88 * KB_
    MISC = 184 * KB_
    gains = place("gains", [P, 2, D], F32, MISC)
    ident = place("ident", [P, P], F32, MISC + 8192)
    before01 = place("before01", [P, P], F32, MISC + 8704)
    before_cap = place("before_cap", [P, P], F32, MISC + 9216)
    m_past = place("m_past", [P, P], F32, MISC + 9728)
    m_fut = place("m_fut", [P, P], F32, MISC + 10240)
    m_cross = place("m_cross", [P, P], F32, MISC + 10752)
    balp = place("balp", [P, GH], F32, MISC + 11264)
    ggla = place("ggla", [P, 2 * GH], F32, MISC + 11328)
    ssq = place("ssq", [P, TB], F32, MISC + 11392)
    lnm = place("lnm", [P, TB], F32, MISC + 11456)
    rstd = place("rstd", [P, TB], F32, MISC + 11520)
    two_c = place("two_c", [P, TB, 2], F32, MISC + 11584)
    two_k = place("two_k", [P, TB, 2], F32, MISC + 11648)
    dec = place("dec", [P, TB], F32, MISC + 11712)
    epsc = place("epsc", [P, 1], F32, MISC + 11776)
    lrT = place("lrT", [2 * RANK, T], F32, MISC + 12288)
    walp = place("walp", [2 * RANK, QKW], F32, MISC + 16384)
    wlr = place("wlr", [P, KD, 2, RANK], F32R, MISC + 20480)
    xin = place("xin", [P, TB, D], F32, AREA)
    pin = place("pin", [P, TB, PK * P], F32, AREA + 32 * KB_)
    wpe_raw = place("wpe_raw", [P, PK, D], F32, AREA + 40 * KB_)
    wpe = place("wpe", [P, 2, PK, D], F32R, AREA + 48 * KB_)
    pT = place("pT", [P, 2, PK, T], F32R, AREA + 64 * KB_)
    pes = [place(f"pes{i}", [P, D], F32, AREA + (80, 84, 32, 36)[i] * KB_) for i in range(4)]
    junk0 = place("junk0", [P, D], F32, AREA + 88 * KB_)
    qkv = place("qkv", [P, 4, T], F32, AREA)
    Y = place("Y", [P, GH, T], F32, AREA + 16 * KB_)
    A_ke = place("A_ke", [P, T], F32, AREA + 32 * KB_)
    A_eb = place("A_eb", [P, T], F32, AREA + 36 * KB_)
    A_enb = place("A_enb", [P, T], F32, AREA + 40 * KB_)
    A_qd = place("A_qd", [P, T], F32, AREA + 44 * KB_)
    A_kd = place("A_kd", [P, T], F32, AREA + 48 * KB_)
    A_qi = place("A_qi", [P, T], F32, AREA + 52 * KB_)
    A_ki = place("A_ki", [P, T], F32, AREA + 56 * KB_)
    VN = [place("VN0", [P, TB, DV], F32R, AREA + 60 * KB_), place("VN1", [P, TB, DV], F32R, MISC + 12288)]
    KN = [place("KN0", [P, TB, DK], F32R, AREA + 68 * KB_), place("KN1", [P, TB, DK], F32R, AREA + 86 * KB_)]
    qS = [place("qS0", [P, T], F32R, AREA + 40 * KB_), place("qS1", [P, T], F32R, AREA + 36 * KB_)]
    oT = place("oT", [P, 2, T], F32, AREA + 72 * KB_)
    on = place("on", [P, 2, DV], F32, AREA + 80 * KB_)
    attn = place("attn", [P, 2, P], F32, AREA + 82 * KB_)
    St = place("St", [P, 2, DV], F32, AREA + 83 * KB_)
    junkA = place("junkA", [P, DV], F32, AREA + 85 * KB_)
    attn_s = place("attn_s", [P, 2, 2, P], F32R, AREA + 90 * KB_)
    St_s = place("St_s", [P, 2, 2, DV], F32R, AREA + 92 * KB_)
    newchunk = place("newchunk", [P, T], F32, AREA + 56 * KB_)
    OA = place("OA", [P, 2, KD, T], F32R, AREA + 32 * KB_)
    SM = place("SM", [P, KD, T], F32, AREA)
    graw = place("graw", [P, 4, T], F32, AREA)
    early = {"A": qkv, "B": graw}
    SM_SLOT = [4, 5, 0, 1, 2, 3, 6, 7]
    sg = place("sg", [P, 2, BANK], F32, MISC + 12288)
    oin = place("oin", [P, 2, T], F32, AREA + 24 * KB_)
    ys = place("ys", [P, 2, BANK], F32, MISC + 12288)
    yin = place("yin", [P, 2, BANK], F32, MISC + 16384)
    QK = place("QK", [P, 2, 2, 2, T], F32R, AREA)
    WT = place("WT", [P, 2, TB, BANK], F32R, AREA + 32 * KB_)
    VS = place("VS", [P, 2, TB, P], F32R, AREA + 64 * KB_)
    vT = place("vT", [P, T], F32, AREA + 72 * KB_)
    T1 = place("T1", [P, 2, T], F32, AREA + 76 * KB_)
    T2a = place("T2a", [P, 2, T], F32, AREA + 84 * KB_)
    T2b = place("T2b", [P, 2, T], F32, MISC + 12288)
    T2 = [T2a[:, 0, :], T2a[:, 1, :], T2b[:, 0, :], T2b[:, 1, :]]
    oS = place("oS", [P, 2, BANK], F32, AREA + 92 * KB_)
    WD = [place("WD0", [P, 4, 2, KD, P], F32R, AREA - 8 * KB_), place("WD1", [P, 4, 2, KD, P], F32R, AREA + 32 * KB_)]
    x1 = place("x1", [P, TB, D], F32, AREA + 64 * KB_)
    u = place("u", [P, 2, D], F32, 72 * KB_)
    junkD = place("junkD", [P, D], F32, AREA + 24 * KB_)
    sgD = place("sgD", [P, 2, BANK], F32, AREA + 28 * KB_)
    pin2 = place("pin2", [P, 2, BANK], F32, MISC + 12288)

    with ExitStack() as ctx:
        def sem(name):
            return ctx.enter_context(nc.semaphore(name))

        def bank(name, n=1):
            return ctx.enter_context(nc.psum_tensor(name, [P, n * BANK], F32))

        pj = [bank("pj0"), bank("pj1")]
        z0 = bank("z0", 2)
        z1 = bank("z1", 2)
        trs = [bank("tr0"), bank("tr1")]
        zs = [z0, z1]
        SBK = [z0[:, 0:BANK], z0[:, BANK:2 * BANK]]
        OBK = [z1[:, 0:BANK], z1[:, BANK:2 * BANK]]
        ring = [trs[0][:, :], trs[1][:, :]] + SBK

        def vk_bank(r):
            return SBK[r] if r < 2 else trs[r % 2][:, :]

        pe_phase, act_phase, dve_phase = sem("pe_phase"), sem("act_phase"), sem("dve_phase")
        pj_taken = sem("pj_taken")
        const_ready = sem("const_ready")
        params_in = sem("params_in")
        waits_passed = sem("waits_passed")
        gain_in, gain2_in, w_ple_in = sem("gain_in"), sem("gain2_in"), [sem("w_ple_in0"), sem("w_ple_in1")]
        p_in, x_in = sem("p_in"), [sem(f"x_in{i}") for i in range(TB)]
        w_in_s = [sem("w_raw0"), sem("w_raw1")]
        w_hi, w_ready, wlr_part = sem("w_hi"), sem("w_ready"), sem("wlr_part")
        q_full = sem("q_full")

        def phase_over(eng, own):
            eng.drain().then_inc(own, 1)

        def phase_end(eng, own, k):
            phase_over(eng, own)
            if own is not pe_phase:
                area_free(eng, k)

        def area_free(eng, k):
            for s_ in (pe_phase, act_phase, dve_phase):
                eng.wait_ge(s_, k + 1)

        def stand_alone(eng):
            eng.sem_inc(waits_passed, 1)

        def product(out_, lhs, rhs, blocks):
            steps = [(k, a, b) for k in range(blocks) for a, b in PASSES]
            for i, (k, a, b) in enumerate(steps):
                mm = nc.tensor.matmul(out_, lhs(a, k), rhs(b, k), start=i == 0, stop=i == len(steps) - 1)
            return mm

        N_A0, N_A = 1, 1 + 4 * GH
        N_FA = N_A + 3 * KD
        N_B = N_FA + 3 * SH
        N_FB = N_B + 3 * KD
        N_D = N_FB + 2 * KD
        WIDE_ORDER = [3, 1, 2, 0, 4, 5, 6, 7]
        GLA_SLICES = [(VA, DV), (VA + P, DV), (QA, P), (KA, P)]
        SB_SLICES = [(QB, P), (KB, P), (VB, P)]

        J_A = 0
        J_FA = J_A + 2 + 8 * GH + 8
        FIN_USES = 8 + 16 + 16
        J_B = J_FA + FIN_USES
        J_FB = J_B + 6 + 8 * (SH - 1) + 10
        J_D = J_FB + FIN_USES
        SPARE = 2

        def col(off, step, i):
            return bass.ds(off + step * i, P)

        p_full, p_hi, p_lo = sem("p_full"), sem("p_hi"), sem("p_lo")
        wpe_hi, wpe_lo = sem("wpe_hi"), [sem("wpe_lo0"), sem("wpe_lo1")]
        pe_full, pe_taken = [sem("pe_full0"), sem("pe_full1")], [sem("pe_taken0"), sem("pe_taken1")]
        pe_out = [sem(f"pe_out{i}") for i in range(4)]
        x_sq, x_ln, x_rstd, x_norm = sem("x_sq"), sem("x_ln"), sem("x_rstd"), sem("x_norm")
        xt_full, xt_hi, xt_lo = sem("xt_full"), sem("xt_hi"), sem("xt_lo")
        y_full, y_abs, y_min, y_exp, y_ln, y_ls, y_cum = [sem(n) for n in (
            "y_full", "y_abs", "y_min", "y_exp", "y_ln", "y_ls", "y_cum")]
        chunk_mask = sem("chunk_mask")
        e_done, dd_done, ke_done, dec_part, dec_done, prep, kS_ready, qS_part, qS_ready = [sem(n) for n in (
            "e_done", "dd_done", "ke_done", "dec_part", "dec_done", "prep", "kS_ready", "qS_part", "qS_ready")]
        g_tr_full, g_tr_taken = sem("g_tr_full"), sem("g_tr_taken")
        vk_hi, vk_taken = sem("vk_hi"), sem("vk_taken")
        s_full, attn_part, attn_ready = sem("s_full"), sem("attn_part"), sem("attn_ready")
        st_part, st_ready = sem("st_part"), sem("st_ready")
        o_full, o_sq, o_ln, o_rstd, on_ready = [sem(n) for n in ("o_full", "o_sq", "o_ln", "o_rstd", "on_ready")]
        oT_out = sem("oT_out")
        b_hi = sem("b_hi")
        z_full, z_abs, z_exp, z_ln, sp, spm, cum, y_done, ym, w_done = [sem(n) for n in (
            "z_full", "z_abs", "z_exp", "z_ln", "sp", "spm", "cum", "y_done", "ym", "w_done")]
        b_tr_full, b_tr_hi, b_tr_lo = sem("b_tr_full"), sem("b_tr_hi"), sem("b_tr_lo")
        pv_full, ob_out = sem("pv_full"), [sem("ob_out0"), sem("ob_out1")]
        fin = {}
        for br in "AB":
            fin[br] = {n: sem(f"f{br}_{n}") for n in (
                "sg_ready", "gated", "og", "hi", "oa_ready", "oin0", "oin1", "ysum",
                "yhi", "ylo", "yio0", "yio1")}
        x2_in = [sem(f"x2_in{i}") for i in range(TB)]
        d_full = sem("d_full")
        u_sq, u_ln, u_rstd, u_ready = sem("u_sq"), sem("u_ln"), sem("u_rstd"), sem("u_ready")
        ut_full, ut_hi, ut_lo = sem("ut_full"), sem("ut_hi"), sem("ut_lo")
        pe_in, gate_used, x2_ready = [sem("pe_in0"), sem("pe_in1")], sem("gate_used"), sem("x2_ready")
        f_sq, f_ln, f_rstd, f_ready, out_done = sem("f_sq"), sem("f_ln"), sem("f_rstd"), sem("f_ready"), [
            sem("out_done0"), sem("out_done1")]

        def sb_rounds(i):
            if i < 2:
                return [("v", i, None, 4 * i, 4)]
            j = i - 2
            if j < 4:
                return [("w", 2 + j, j, 0, j + 1)]
            if j < TB:
                return [("w", 6 + 2 * (j - 4), j, 0, 4), ("w", 7 + 2 * (j - 4), j, 4, j - 3)]
            return []

        SB_ROUNDS = 14
        SB_STEPS = TB + 3
        TAKE_EARLY, ROUNDS_EARLY = (6,), (7,)
        EXTRA = {0: [], 1: [("q", 0, 0)], 2: [("q", 0, 1)], 3: [("q", 1, 0), ("q", 1, 1)], 4: [("q", 2, 0)],
                 5: [("q", 2, 1), ("q", 3, 0)], 6: [("q", 3, 1), ("pv", 0)], 7: [("q", 4, 0)], 8: [("q", 4, 1)],
                 9: [("q", 5, 0)], 10: [("q", 5, 1), ("pv", 1)]}
        EXTRA_LAST = {0: [("q", 0, 0), ("q", 0, 1)], 1: [("q", 1, 0), ("q", 1, 1)], 2: [("q", 2, 0)],
                      3: [("q", 2, 1)], 4: [("q", 3, 0), ("q", 3, 1)], 5: [("q", 4, 0), ("q", 4, 1)],
                      6: [("pv", 0)], 7: [("q", 5, 0), ("q", 5, 1)], 8: [("q", 6, 0), ("q", 6, 1)],
                      9: [("q", 7, 0)], 10: [("q", 7, 1), ("pv", 1)]}

        def uses(extra):
            order = []
            for i in sorted(extra):
                for e in extra[i]:
                    if e[:2] not in order:
                        order.append(e[:2])
            return {e: n for n, e in enumerate(order)}

        def finished(extra, i):
            return [(uses(extra)["q", e[1]], e[1]) for e in extra[i] if e[0] == "q" and e[2] == 1]

        def z_pieces(i):
            w = (i + 1) * P
            first = (0, min(BANK, max(w, 2 * P)))
            return [first] + ([(BANK, max(w, BANK + 2 * P))] if w > BANK else [])

        block = ctx.enter_context(nc.Block())

        @block.sync
        def _(sp_eng):
            sy = sp_eng
            sy.dma_start(pin[:, :, :], p_rows.rearrange("(b t) d -> t b d", t=P)).then_inc(p_in, 16)
            for ch in range(NH):
                c = slice(ch * BANK, (ch + 1) * BANK)
                sy.dma_start(wpe_raw[:, :, c], w_ple_k[:, :, c]).then_inc(w_ple_in[ch], 16)
            for b in range(TB):
                sy.dma_start(xin[:, b, :], x_rows[b * P:(b + 1) * P, :]).then_inc(x_in[b], 16)
                if b == 0:
                    sy.dma_start(gains[:, 0, :], g_mix[0].partition_broadcast(P)).then_inc(gain_in, 16)

            def load(n, slot, src):
                sy.wait_ge(w_ready, n + 1)
                sy.dma_start(RAW[:, slot, :, :], src).then_inc(w_in_s[slot], 16)

            load(0, 0, w_in_k[:, :, LR:LR + P])
            for part in range(2):
                sy.dma_start(walp[part * RANK:(part + 1) * RANK, :], w_alpha[0]).then_inc(params_in, 16)
            with nc.allow_non_contiguous_dma(reason="two small per-channel vectors"):
                sy.dma_start(balp[:, :], b_alpha[0].rearrange("(h d) -> d h", d=P)).then_inc(params_in, 16)
                sy.dma_start(ggla[:, :], g_gla_out[0].rearrange("h (v d) -> d (h v)", d=P)).then_inc(params_in, 16)
            with sy.Fori(0, GH) as h:
                for c, (off, step) in enumerate(GLA_SLICES):
                    load(N_A0 + c + 4 * h, (N_A0 + c) % 2, w_in_k[:, :, col(off, step, h)])

            def finish(br, n0, k0, gate_off, m_off, wo_k, o_d, stored):
                s = fin[br]

                def load_gate(e):
                    load(n0 + e, (n0 + e) % 2, w_in_k[:, :, gate_off + P * e:gate_off + P * e + P])

                for e in range(6):
                    load_gate(e)
                for e_sem, v in stored:
                    sy.wait_ge(e_sem, v)
                area_free(sy, k0 - 1)
                for i in range(4):
                    for slot, e in enumerate((4 + i, i)):
                        sy.wait_ge(s["oa_ready"], 4 * i + 2 + 2 * slot)
                        sy.dma_start(oin[:, slot, :], o_d[P * e:P * e + P, :]).then_inc(s[f"oin{slot}"], 16)
                    if i < 2:
                        load_gate(6 + i)
                    else:
                        load(n0 + KD + i - 2, (n0 + i) % 2, w_in_k[:, :, m_off + P * (i - 2):m_off + P * (i - 1)])
                with sy.Fori(1, KD // 2) as j:
                    for par in range(2):
                        load(n0 + KD + par + 2 * j, (n0 + par) % 2, w_in_k[:, :, col(m_off, P, 2 * j + par)])
                with sy.Fori(0, KD // 2) as j:
                    for par in range(2):
                        load(n0 + 2 * KD + par + 2 * j, (n0 + par) % 2, wo_k[:, :, col(0, P, 2 * j + par)])

            area_free(sy, 0)
            sy.dma_start(gains[:, 0, :], g_ple[0].partition_broadcast(P)).then_inc(gain2_in, 16)
            sy.dma_start(gains[:, 1, :], g_final.partition_broadcast(P)).then_inc(gain2_in, 16)
            finish("A", N_A, 2, GA, MA, w_og_k, o_gla_d, [(oT_out, 16 * GH + 1)])
            with sy.Fori(0, SH // 2) as j:
                for par in range(2):
                    for c, (off, step) in enumerate(SB_SLICES):
                        n = N_FA + 3 * par + c
                        load(n + 6 * j, n % 2, w_in_k[:, :, col(off, step, 2 * j + par)])
            finish("B", N_B, 6, GB, MB, w_ob_k, o_sb_d, [(ob_out[0], 16 * SH + 1), (ob_out[1], 16 * SH + 1)])

            for m in range(2 * KD):
                w, c = (w_out_k, WIDE_ORDER[m]) if m < KD else (w_pg_k, m - KD)
                load(N_FB + m, (N_FB + m) % 2, w[:, :, c * P:(c + 1) * P])
                if m == 3:
                    area_free(sy, 8)
                    for b in range(TB):
                        sy.dma_start(x1[:, b, :], x_rows[b * P:(b + 1) * P, :]).then_inc(x2_in[b], 16)
            for q in range(2 * TB):
                ch, b = divmod(q, TB)
                if q >= 2:
                    sy.wait_ge(gate_used, q - 1)
                sy.dma_start(pin2[:, q % 2, :], pe_d[b * P:(b + 1) * P, ch * BANK:(ch + 1) * BANK]
                             ).then_inc(pe_in[q % 2], 16)

        @block.gpsimd
        def _(pool):
            g = nc.gpsimd
            g.sem_inc(w_ready, 2)
            steps = []

            def one(ins):
                steps.append(ins)
                ins.then_inc(const_ready, 1)
                pool.wait_ge(const_ready, len(steps))

            one(g.memset(ident[:, :], 0.0))
            one(g.affine_select(out=ident[:, :], in_=ident[:, :], compare_op=ALU.not_equal, fill=1.0, base=0,
                                pattern=[[-1, P]], channel_multiplier=1))
            one(g.memset(before01[:, :], 1.0))
            one(g.affine_select(out=before01[:, :], in_=before01[:, :], compare_op=ALU.is_gt, fill=0.0, base=0,
                                pattern=[[-1, P]], channel_multiplier=1))
            one(g.memset(before_cap[:, :], 3e38))
            one(g.affine_select(out=before_cap[:, :], in_=before_cap[:, :], compare_op=ALU.is_gt, fill=-1e30, base=0,
                                pattern=[[-1, P]], channel_multiplier=1))
            one(g.memset(m_past[:, :], 1.0))
            one(g.affine_select(out=m_past[:, :], in_=m_past[:, :], compare_op=ALU.is_ge, fill=0.0, base=0,
                                pattern=[[1, P]], channel_multiplier=-1))
            one(g.memset(m_past[0:CHUNK, CHUNK:P], 0.0))
            one(g.memset(m_fut[:, :], 1.0))
            one(g.affine_select(out=m_fut[:, :], in_=m_fut[:, :], compare_op=ALU.is_gt, fill=0.0, base=0,
                                pattern=[[-1, P]], channel_multiplier=1))
            one(g.memset(m_fut[CHUNK:P, 0:CHUNK], 0.0))
            one(g.memset(m_cross[:, :], 0.0))
            one(g.memset(m_cross[0:CHUNK, CHUNK:P], 1.0))
            one(g.memset(two_c[:, :, :], 1.0))
            one(g.memset(two_k[:, :, :], 1.0))
            one(g.memset(epsc[:, :], EPS))

            for ch in range(NH):
                c = slice(ch * BANK, (ch + 1) * BANK)
                pool.wait_ge(w_ple_in[ch], 16)
                g.tensor_scalar(wpe[:, HI, :, c], wpe_raw[:, :, c], 1.0, 1.0, ALU.mult, ALU.mult).then_inc(wpe_hi, 1)
                pool.wait_ge(wpe_hi, ch + 1)
                for k in range(1, PK):
                    g.tensor_tensor(wpe[:, LO, k, c], wpe_raw[:, k, c], wpe[:, HI, k, c].bitcast(F32),
                                    ALU.subtract).then_inc(wpe_lo[ch], 1)

            pool.wait_ge(w_in_s[0], 16)
            raw = RAW[:, 0, :, 0:RANK]
            g.tensor_scalar(wlr[:, :, HI, :], raw, 1.0, 1.0, ALU.mult, ALU.mult).then_inc(wlr_part, 1)
            pool.wait_ge(wlr_part, 1)
            g.tensor_tensor(wlr[:, :, LO, :], raw, wlr[:, :, HI, :].bitcast(F32), ALU.subtract).then_inc(wlr_part, 1)

            def split(n, half_n, slot, hi, lo):
                pool.wait_ge(w_in_s[slot], 16 * half_n + 16)
                stand_alone(pool)
                g.tensor_scalar(hi, RAW[:, slot, :, :], 1.0, 1.0, ALU.mult, ALU.mult).then_inc(w_hi, 1)
                pool.wait_ge(w_hi, n + 1)
                g.tensor_tensor(lo, RAW[:, slot, :, :], hi.bitcast(F32), ALU.subtract).then_inc(w_ready, 1)

            def split_ring(n, half_n, slot):
                pool.wait_ge(q_full, 2 * n + 2)
                split(n, half_n, slot, WS[:, slot, HI, :, :], WS[:, slot, LO, :, :])

            with pool.Fori(0, N_FB // 2) as j:
                for par in range(2):
                    split_ring(2 * j + par, j, par)
            if N_FB % 2:
                split_ring(N_FB - 1, N_FB // 2, 0)
            for m in range(2 * KD):
                n, half = N_FB + m, m // 4
                c = (WIDE_ORDER[m] if m < KD else m) % 4
                if m < 3:
                    pool.wait_ge(pj_taken, SPARE + J_FB + 24 + 4 * (m + 1))
                elif m == 3:
                    pool.wait_ge(q_full, 4 + 2 * (N_FB - 1))
                elif m == 4:
                    area_free(pool, 8)
                elif half >= 2:
                    pool.wait_ge(d_full, TB * (half - 1))
                split(n, n // 2, n % 2, WD[half % 2][:, c, HI, :, :], WD[half % 2][:, c, LO, :, :])

        @block.tensor
        def _(pe):
            t = nc.tensor
            pe.sem_inc(pj_taken, 2)
            pe.sem_inc(q_full, 4)
            pe.sem_inc(o_full, 2)
            pe.sem_inc(g_tr_full, 2)
            pe.sem_inc(pv_full, 1)

            pe.wait_ge(const_ready, 2)
            pe.wait_ge(p_in, 16)
            for r in range(TB // 2):
                for j in range(4):
                    k, b = j // 2, 2 * r + j % 2
                    mm = t.transpose(ring[r][:, j * P:(j + 1) * P], pin[:, b, k * P:(k + 1) * P], ident[:, :])
                mm.then_inc(p_full, 1)

            def turn_x(b):
                pe.wait_ge(x_norm, b + 1)
                for r in (2 * b, 2 * b + 1):
                    if r >= 4:
                        pe.wait_ge(xt_lo, r - 3)
                    else:
                        pe.wait_ge(p_lo, r + 1)
                    for j in range(4):
                        k = 4 * (r % 2) + j
                        mm = t.transpose(ring[r % 4][:, j * P:(j + 1) * P], xin[:, b, k * P:(k + 1) * P], ident[:, :])
                    mm.then_inc(xt_full, 1)


            def embed(b):
                pe.wait_ge(p_lo, b // 2 + 1)
                for ch in range(NH):
                    if b > 0:
                        pe.wait_ge(pe_taken[ch], b)
                    else:
                        pe.wait_ge(wpe_lo[ch], PK)
                    product(pj[ch][:, :], lambda a, k: pT[:, a, k, b * P:(b + 1) * P],
                            lambda a, k: wpe[:, a, k, ch * BANK:(ch + 1) * BANK], PK).then_inc(pe_full[ch], 1)

            embed(0)
            for b in range(TB):
                turn_x(b)
                if b < TB - 1:
                    embed(b + 1)
            phase_end(pe, pe_phase, 0)

            def quantum(n, slot, hf, rhs, use, bank_=None, part=None):
                if hf == 0 and part != 1:
                    pe.wait_ge(w_ready, n + 3)
                if part != 1:
                    pe.wait_ge(pj_taken, use + 1)
                o = pj[hf if bank_ is None else bank_][:, :]
                steps = [(k, a, b) for k in range(KD) for a, b in PASSES]
                half = len(steps) // 2
                mine = range(len(steps)) if part is None else range(part * half, (part + 1) * half)
                for i in mine:
                    k, a, b = steps[i]
                    mm = t.matmul(o, WS[:, slot, a, k, :], rhs[:, b, k, hf * BANK:(hf + 1) * BANK], start=i == 0,
                                  stop=i == len(steps) - 1)
                if part != 0:
                    mm.then_inc(q_full, 1)

            pe.sem_inc(g_tr_taken, 2)
            for hf in range(NH):
                pe.wait_ge(xt_lo, TB * (hf + 1))
                pe.wait_ge(pe_taken[hf], TB)
                pe.wait_ge(pj_taken, J_A + hf + 1)
                if hf == 0:
                    pe.wait_ge(wlr_part, 2)
                for i in range(2 * KD):
                    k, b = divmod(i, 2)
                    mm = t.matmul(pj[hf][0:2 * RANK, :], wlr[:, k, :, :].rearrange("p a r -> p (a r)"),
                                  HT[:, b, k, hf * BANK:(hf + 1) * BANK], start=i == 0, stop=i == 2 * KD - 1)
                mm.then_inc(q_full, 1)

            def gla_quantum(h, i, part=None):
                c, hf = divmod(i, 2)
                quantum(N_A0 + c + 4 * h, (N_A0 + c) % 2, hf, HT, J_A + 2 + i + 8 * h, part=part)

            gla_quantum(0, 0)
            pe.wait_ge(params_in, 64)
            pe.wait_ge(pj_taken, SPARE + J_A + 2)
            for r in range(2 * GH):
                h, hf = divmod(r, 2)
                if r >= 2:
                    pe.wait_ge(y_min, r - 1)
                t.matmul(trs[hf][:, :], walp[:, h * P:(h + 1) * P], lrT[:, hf * BANK:(hf + 1) * BANK],
                         start=True, stop=True).then_inc(y_full, 1)
                if hf:
                    for i in range(r, min(r + 2, 8)):
                        gla_quantum(0, i)
            pe.wait_ge(y_min, 2 * GH)

            with pe.Fori(0, GH) as h:

                pe.wait_ge(pj_taken, SPARE + J_A + 6 + 8 * h)
                for r in range(4):
                    if r < 2:
                        pe.wait_ge(attn_ready, 2 + 8 * h)
                    else:
                        pe.wait_ge(g_tr_taken, r - 1 + 8 * h)
                    for j in range(4):
                        b, v = 2 * r + j // 2, j % 2
                        mm = t.transpose(vk_bank(r)[:, j * P:(j + 1) * P], qkv[:, v, b * P:(b + 1) * P], ident[:, :])
                    mm.then_inc(g_tr_full, 1)
                for i in range(3):
                    gla_quantum(h + 1, i)
                pe.wait_ge(kS_ready, h + 1)
                for r in range(4, 6):
                    pe.wait_ge(vk_taken, r - 1 + 6 * h)
                    for j in range(4):
                        b = 4 * (r - 4) + j
                        mm = t.transpose(vk_bank(r)[:, j * P:(j + 1) * P], A_enb[:, b * P:(b + 1) * P], ident[:, :])
                    mm.then_inc(g_tr_full, 1)

                def scores(b):
                    cols = slice(b * P, (b + 1) * P)
                    pe.wait_ge(attn_ready, b + 1 + 8 * h)
                    o = SBK[b % 2]
                    t.matmul(o[:, 0:P], A_kd[:, cols], A_qd[:, cols], start=True, stop=True)
                    t.matmul(o[:, P:2 * P], A_ki[:, cols], A_qi[:, cols], start=True, stop=True)
                    t.matmul(o[:, 2 * P:3 * P], A_ke[:, cols], A_qd[:, cols], start=True, stop=True).then_inc(s_full, 1)

                def turn(b):
                    pe.wait_ge(g_tr_taken, b + 1 + 8 * h)
                    pe.wait_ge(on_ready, b + 3 + 8 * h)
                    for v in range(2):
                        mm = t.transpose(trs[b % 2][:, v * P:(v + 1) * P], on[:, b % 2, v * P:(v + 1) * P], ident[:, :])
                    mm.then_inc(g_tr_full, 1)

                gla_quantum(h + 1, 3, part=0)
                pe.wait_ge(prep, 5 + 5 * h)
                scores(0)
                for b in range(TB):
                    cols = slice(b * P, (b + 1) * P)
                    if b < TB - 1:
                        scores(b + 1)
                    gla_quantum(h + 1, 3 + (b + 1) // 2, part=(b + 1) % 2)
                    if b == 0:
                        pe.wait_ge(vk_taken, 6 + 6 * h)
                    pe.wait_ge(attn_ready, b + 3 + 8 * h)
                    pe.wait_ge(on_ready, b + 1 + 8 * h)
                    o = OBK[b % 2]
                    for n, (a, c) in enumerate(PASSES):
                        mm = t.matmul(o[:, 0:DV], attn_s[:, b % 2, a, :], VN[c][:, b, :], start=n == 0,
                                      stop=b == 0 and n == 2)
                    if b > 0:
                        if b == 1:
                            pe.wait_ge(qS_ready, h + 1)
                        pe.wait_ge(st_ready, b + 1 + 7 * h)
                        for n, (a, c) in enumerate(PASSES):
                            mm = t.matmul(o[:, 0:DV], qS[a][:, cols], St_s[:, b % 2, c, :], start=False, stop=n == 2)
                    if b < TB - 1:
                        mm = product(o[:, DV:2 * DV], lambda a, k: KN[a][:, b, :], lambda a, k: VN[a][:, b, :], 1)
                    mm.then_inc(o_full, 1)
                    if b > 0:
                        turn(b - 1)
                gla_quantum(h + 1, 7, part=1)
                turn(TB - 1)
            phase_end(pe, pe_phase, 1)

            def finish(br, n0, j0, k0):
                s = fin[br]
                with pe.Fori(0, 2) as j:
                    for par in range(2):
                        for hf in range(NH):
                            quantum(n0 + 4 + par + 2 * j, (n0 + par) % 2, hf, HT, j0 + 2 * par + hf + 4 * j)
                phase_end(pe, pe_phase, k0)
                for part, rhs in ((1, HT), (2, OA)):
                    if part == 2:
                        pe.wait_ge(s["oa_ready"], 4 + 2 * KD)
                    with pe.Fori(0, KD // 2) as j:
                        for par in range(2):
                            n = n0 + part * KD + par
                            for hf in range(NH):
                                quantum(n + 2 * j, n % 2, hf, rhs, j0 + 16 * part - 8 + 2 * par + hf + 4 * j)
                    phase_end(pe, pe_phase, k0 + part)

            finish("A", N_A, J_FA, 2)

            def sb_quantum(h, par, i, use, bank_, part=None):
                c, hf = divmod(i, 2)
                n = N_FA + 3 * par + c
                quantum(n - 3 * par + 3 * h, n % 2, hf, HT, use, bank_, part)

            for i in range(6):
                sb_quantum(0, 0, i, J_B + i, i % 2)

            def scores(h, par, i):
                pe.wait_ge(y_done, i + 1 + 8 * h)
                for c0, c1 in z_pieces(i):
                    for n, (a, c) in enumerate(PASSES):
                        mm = t.matmul(zs[i % 2][:, c0:c1], QK[:, par, 0, a, i * P:(i + 1) * P],
                                      QK[:, par, 1, c, c0:c1], start=n == 0, stop=n == 2)
                mm.then_inc(z_full, 1)

            def sb_head(h, par, last):
                extra = EXTRA_LAST if last else EXTRA
                use = uses(extra)

                def rounds(some):
                    for kind, r, j, b0, nb in some:
                        if kind == "v":
                            pe.wait_ge(pj_taken, SPARE + J_B + 5 + r + 8 * h)
                        else:
                            pe.wait_ge(w_done, j + 1 + 8 * h)
                        pe.wait_ge(b_tr_lo, r + 1 + SB_ROUNDS * h)
                        for m in range(nb):
                            src = vT if kind == "v" else T2[j % 4]
                            mm = t.transpose(trs[r % 2][:, m * P:(m + 1) * P], src[:, (b0 + m) * P:(b0 + m + 1) * P],
                                             ident[:, :])
                        mm.then_inc(b_tr_full, 1)

                def weigh_values(gq):
                    n = use["pv", gq]
                    pe.wait_ge(pj_taken, J_B + 6 + n + 1 + 8 * h)
                    pe.wait_ge(b_tr_lo, (6 if gq == 0 else SB_ROUNDS) + 2 + SB_ROUNDS * h)
                    steps = [(sb, a, c) for sb in range(4 * gq + 4) for a, c in PASSES]
                    for i, (sb, a, c) in enumerate(steps):
                        lo = max(0, sb - 4 * gq) * P
                        mm = t.matmul(pj[n % 2][:, lo:BANK], VS[:, a, sb, :], WT[:, c, sb, lo:BANK], start=i == 0,
                                      stop=i == len(steps) - 1)
                    mm.then_inc(pv_full, 1)

                for i in range(SB_STEPS):
                    if 2 <= i < TB:
                        scores(h, par, i)
                    elif i > TB and not last:
                        if i == TB + 1:
                            pe.wait_ge(pj_taken, SPARE + J_B + 6 + use["q", 3] + 1 + 8 * h)
                        scores(h + 1, 1 - par, i - TB - 1)
                    for e in extra[i]:
                        if e[0] == "q":
                            n = use["q", e[1]]
                            if last:
                                c, hf = divmod(e[1], 2)
                                quantum(N_B + c, (N_B + c) % 2, hf, HT, J_B + 6 + 8 * (SH - 1) + n, n % 2, e[2])
                            else:
                                sb_quantum(h + 1, 1 - par, e[1], J_B + 6 + n + 8 * h, n % 2, e[2])
                        else:
                            weigh_values(e[1])
                    rounds(sb_rounds(i))

            pe.wait_ge(pj_taken, SPARE + J_B + 4)
            for i in range(2):
                scores(0, 0, i)
            with pe.Fori(0, SH // 2 - 1) as j:
                for par in range(2):
                    sb_head(2 * j + par, par, False)
            sb_head(SH - 2, 0, False)
            sb_head(SH - 1, 1, True)
            phase_end(pe, pe_phase, 5)

            finish("B", N_B, J_FB, 6)

            def wide(q, half):
                b = q % TB
                pe.wait_ge(pj_taken, J_D + q + 1)
                for k in range(KD):
                    if q == 0:
                        pe.wait_ge(fin["B"]["ylo"], 2 * k + 2)
                    for n, (a, c) in enumerate(PASSES):
                        mm = t.matmul(pj[q % 2][:, :], HT[:, a, k, b * P:(b + 1) * P], WD[half % 2][:, :, c, k, :],
                                      start=k == n == 0, stop=k == KD - 1 and n == 2)
                mm.then_inc(d_full, 1)

            def turn_u(b):
                pe.wait_ge(u_ready, b + 1)
                for r in (2 * b, 2 * b + 1):
                    if r >= 4:
                        pe.wait_ge(ut_lo, r - 3)
                    for j in range(4):
                        k = 4 * (r % 2) + j
                        mm = t.transpose(ring[r % 4][:, j * P:(j + 1) * P], u[:, b % 2, k * P:(k + 1) * P], ident[:, :])
                    mm.then_inc(ut_full, 1)

            for q in range(2 * TB):
                if q % TB == 0:
                    pe.wait_ge(w_ready, N_FB + 4 * (q // TB + 1) + 2)
                wide(q, q // TB)
                if q >= TB + 2:
                    turn_u(q - TB - 2)
            for q in range(2 * TB, 4 * TB):
                if q < 2 * TB + 2:
                    turn_u(q - TB - 2)
                if q % TB == 0:
                    pe.wait_ge(w_ready, N_FB + 4 * (q // TB + 1) + 2)
                if q < 3 * TB:
                    pe.wait_ge(ut_lo, 2 * (q - 2 * TB) + 2)
                wide(q, q // TB)

        @block.scalar
        def _(act):
            s = nc.scalar
            s.preload_act_table_set(EXP_LN)
            s.sem_inc(oT_out, 1)
            s.sem_inc(ob_out[0], 1)
            s.sem_inc(ob_out[1], 1)

            def copy(out_, in_, scale=1.0):
                return s.activation(out_, in_, ACT.Copy, scale=scale)

            def inverse_rms(src, n, i, width, sq, ln, inv, count, junk):
                s.activation(junk, src, ACT.Square, accum_out=ssq[:, i:i + 1]).then_inc(sq, 1)
                act.wait_ge(sq, count)
                s.activation(lnm[:, i:i + 1], ssq[:, i:i + 1], ACT.Ln, bias=epsc[:, 0:1],
                             scale=1.0 / width).then_inc(ln, 1)
                act.wait_ge(ln, count)
                return s.activation(rstd[:, i:i + 1], lnm[:, i:i + 1], ACT.Exp, scale=-0.5).then_inc(inv, 1)

            for r in range(TB // 2):
                act.wait_ge(p_full, r + 1)
                copy(pT[:, HI, :, 2 * r * P:(2 * r + 2) * P],
                     ring[r].rearrange("p (k n) -> p k n", k=PK)).then_inc(p_hi, 1)

            def take_x(b):
                for r in (2 * b, 2 * b + 1):
                    k = 4 * (r % 2)
                    act.wait_ge(xt_full, r + 1)
                    copy(HT[:, HI, k:k + 4, b * P:(b + 1) * P],
                         ring[r % 4].rearrange("p (k n) -> p k n", k=4)).then_inc(xt_hi, 1)

            act.wait_ge(const_ready, 17)

            def x_rms(b):
                act.wait_ge(x_in[b], 16)
                if b:
                    act.wait_ge(x_sq, b)
                inverse_rms(xin[:, b, :], T, b, D, x_sq, x_ln, x_rstd, b + 1, junk0[:, :])

            def store_embedded(b):
                for ch in range(NH):
                    act.wait_ge(pe_taken[ch], b + 1)
                act.dma_start(pe_d[b * P:(b + 1) * P, :], pes[b % 4][:, :]).then_inc(pe_out[b % 4], 16)

            x_rms(0)
            x_rms(1)
            for b in range(TB):
                act.wait_ge(pe_full[0], b + 1)
                if b >= 4:
                    act.wait_ge(pe_out[b % 4], 16 * (b // 4))
                copy(pes[b % 4][:, 0:BANK], pj[0][:, :]).then_inc(pe_taken[0], 1)
                take_x(b)
                if b < TB - 2:
                    x_rms(b + 2)
                store_embedded(b)
            phase_end(act, act_phase, 0)

            def quantum_in(q):
                act.wait_ge(q_full, 5 + q)

            for hf in range(NH):
                quantum_in(hf)
                copy(lrT[:, hf * BANK:(hf + 1) * BANK], pj[hf][0:2 * RANK, :]).then_inc(pj_taken, 1)
            act.wait_ge(params_in, 64)
            tmp = [A_ke, A_qd]

            def take_qkv(h, i):
                c, hf = divmod(i, 2)
                quantum_in(2 + i + 8 * h)
                if c >= 2:
                    act.wait_ge(prep, 5 * h)
                copy(qkv[:, c, hf * BANK:(hf + 1) * BANK], pj[hf][:, :]).then_inc(pj_taken, 1)

            def take_first(i):
                c, hf = divmod(i, 2)
                quantum_in(2 + i)
                copy(qkv[:, c, hf * BANK:(hf + 1) * BANK], pj[hf][:, :]).then_inc(pj_taken, 1)

            take_first(0)
            for i in range(4):
                act.wait_ge(pe_out[i], 4 * TB)
            for h in range(GH):
                for hf in range(NH):
                    r = 2 * h + hf
                    act.wait_ge(y_full, r + 1)
                    if h >= 2 and hf == 0:
                        act.wait_ge(y_ls, h - 1)
                    s.activation(tmp[h % 2][:, hf * BANK:(hf + 1) * BANK], trs[hf][:, :], ACT.Abs,
                                 bias=balp[:, h:h + 1]).then_inc(y_abs, 1)
                act.wait_ge(y_abs, 2 * h + 2)
                s.activation(tmp[h % 2][:, :], tmp[h % 2][:, :], ACT.Exp, scale=-1.0).then_inc(y_exp, 1)
                act.wait_ge(y_exp, h + 1)
                s.activation(tmp[h % 2][:, :], tmp[h % 2][:, :], ACT.Ln, bias=1.0).then_inc(y_ln, 1)
                for i in range(2 * h + 1, min(2 * h + 3, 8)):
                    take_first(i)
            act.wait_ge(y_cum, GH)

            with act.Fori(0, GH) as h:

                def take_round(r, out_):
                    act.wait_ge(g_tr_full, r + 3 + 14 * h)
                    return copy(out_, vk_bank(r)).then_inc(vk_hi, 1)

                for r in range(4):
                    take_round(r, VN[HI][:, 2 * r:2 * r + 2, :].rearrange("p b v -> p (b v)"))
                act.wait_ge(o_full, 2 + 8 * h)
                stand_alone(act)
                yh = Y[:, bass.ds(h, 1), :].rearrange("p a t -> p (a t)")
                s.activation(A_eb[:, :], yh, ACT.Exp, scale=1.0 / TAU).then_inc(e_done, 1)
                s.activation(A_enb[:, :], yh, ACT.Exp, scale=-1.0 / TAU).then_inc(e_done, 1)
                act.wait_ge(dd_done, h + 1)
                s.activation(A_ke[:, :], A_ke[:, :], ACT.Exp, scale=1.0 / TAU).then_inc(ke_done, 1)
                for i in range(3):
                    take_qkv(h + 1, i)
                for r in range(4, 6):
                    take_round(r, KN[HI][:, 4 * (r - 4):4 * (r - 4) + 4, :].rearrange("p b d -> p (b d)"))

                def take_turned(b):
                    r = 6 + b
                    act.wait_ge(g_tr_full, r + 3 + 14 * h)
                    if b == 0:
                        act.wait_ge(oT_out, 1 + 16 * h)
                    stand_alone(act)
                    for v in range(2):
                        i = copy(oT[:, v, b * P:(b + 1) * P], trs[r % 2][:, v * P:(v + 1) * P],
                                 ggla[:, bass.ds(2 * h + v, 1)])
                    i.then_inc(g_tr_taken, 1)

                for b in range(TB):
                    if b % 2 == 0:
                        take_qkv(h + 1, 3 + b // 2)
                    act.wait_ge(o_full, b + 3 + 8 * h)
                    act.wait_ge(on_ready, b + 1 + 8 * h)
                    if b < TB - 1:
                        act.wait_ge(st_part, 2 * b + 1 + 14 * h)
                    i = b % 2
                    c = b + 1 + 8 * h
                    s.activation(junkA[:, :], OBK[i][:, 0:DV], ACT.Square, accum_out=ssq[:, i:i + 1]).then_inc(o_sq, 1)
                    act.wait_ge(o_sq, c)
                    s.activation(lnm[:, i:i + 1], ssq[:, i:i + 1], ACT.Ln, bias=epsc[:, 0:1],
                                 scale=1.0 / DV).then_inc(o_ln, 1)
                    act.wait_ge(o_ln, c)
                    s.activation(rstd[:, i:i + 1], lnm[:, i:i + 1], ACT.Exp, scale=-0.5).then_inc(o_rstd, 1)
                    if b > 0:
                        take_turned(b - 1)
                take_qkv(h + 1, 7)
                take_turned(TB - 1)
                act.wait_ge(g_tr_taken, 10 + 8 * h)
                act.dma_start(o_gla_d[bass.ds(DV * h, DV), :].rearrange("(v p) t -> p v t", p=P),
                              oT[:, :, :]).then_inc(oT_out, 16)
            phase_end(act, act_phase, 1)

            def finish(br, n0, j0, k0):
                f = fin[br]
                s.preload_act_table_set(SIGMOID)
                with act.Fori(0, 4) as i:
                    for t in range(4):
                        hf = t % 2
                        if t < 2:
                            act.wait_ge(q_full, 2 * (n0 + 4) + hf + 5 + 2 * i)
                            src = pj[hf][:, :]
                        else:
                            src = early[br][:, bass.ds(i, 1), hf * BANK:(hf + 1) * BANK].rearrange("p a t -> p (a t)")
                        act.wait_ge(f["oa_ready"], t + 3 + 4 * i)
                        stand_alone(act)
                        s.activation(sg[:, hf, :], src, ACT.Sigmoid).then_inc(f["sg_ready"], 1)

                def take_merge_gate(e, slot):
                    for hf in range(NH):
                        act.wait_ge(q_full, 2 * (n0 + KD) + hf + 5 + 2 * e)
                        stand_alone(act)
                        s.activation(SM[:, bass.ds(slot, 1), hf * BANK:(hf + 1) * BANK].rearrange(
                            "p a t -> p (a t)"), pj[hf][:, :], ACT.Sigmoid).then_inc(pj_taken, 1)

                act.wait_ge(pj_taken, SPARE + j0 + 8)
                for e in (0, 1):
                    take_merge_gate(e, SM_SLOT[e])
                phase_end(act, act_phase, k0)
                with act.Fori(0, 2) as j:
                    for par in range(2):
                        take_merge_gate(2 * j + par + 2, 2 * j + par)
                for e in (6, 7):
                    take_merge_gate(e, SM_SLOT[e])
                s.preload_act_table_set(EXP_LN)
                phase_over(act, act_phase)
                with act.Fori(0, KD // 2) as j:
                    for par in range(2):
                        for hf in range(NH):
                            rows = ya_d[bass.ds(P * (2 * j + par), P), hf * BANK:(hf + 1) * BANK]
                            if br == "A":
                                act.wait_ge(pj_taken, SPARE + j0 + 24 + 2 * par + hf + 1 + 4 * j)
                                act.dma_start(rows, ys[:, hf, :]).then_inc(f[f"yio{hf}"], 16)
                            else:
                                act.wait_ge(f["ysum"], 2 * par + hf + 1 + 4 * j)
                                act.dma_start(yin[:, hf, :], rows).then_inc(f[f"yio{hf}"], 16)
                phase_end(act, act_phase, k0 + 2)

            finish("A", N_A, J_FA, 2)

            def take_high(h, par, i, bank_):
                c, hf = divmod(i, 2)
                act.wait_ge(q_full, 2 * N_FA + 5 + i + 6 * h)
                copy(QK[:, par, c, HI, hf * BANK:(hf + 1) * BANK], pj[bank_][:, :],
                     Q_SCALE if c == 0 else 1.0).then_inc(b_hi, 1)

            for i in range(4):
                take_high(0, 0, i, i % 2)

            def scores_ln(h, i):
                a = T1[:, i % 2, 0:(i + 1) * P]
                act.wait_ge(z_full, i + 1 + 8 * h)
                s.activation(a, zs[i % 2][:, 0:(i + 1) * P], ACT.Abs).then_inc(z_abs, 1)
                act.wait_ge(z_abs, i + 1 + 8 * h)
                s.activation(a, a, ACT.Exp, scale=-1.0).then_inc(z_exp, 1)
                act.wait_ge(z_exp, i + 1 + 8 * h)
                s.activation(a, a, ACT.Ln, bias=1.0).then_inc(z_ln, 1)

            def weights(h, i):
                act.wait_ge(ym, i + 1 + 8 * h)
                v = T2[i % 4][:, 0:(i + 1) * P]
                s.activation(v, v, ACT.Exp).then_inc(w_done, 1)

            def sb_head(h, par, last):
                extra = EXTRA_LAST if last else EXTRA
                use = uses(extra)

                def take_rounds(some):
                    for kind, r, j, b0, nb in some:
                        act.wait_ge(b_tr_full, r + 1 + SB_ROUNDS * h)
                        src = trs[r % 2][:, 0:nb * P].rearrange("p (b t) -> p b t", b=nb)
                        if kind == "v":
                            copy(VS[:, HI, b0:b0 + nb, :], src).then_inc(b_tr_hi, 1)
                        else:
                            act.wait_ge(pv_full, (2 if j >= 4 else 1) + 2 * h)
                            c0 = (j % 4) * P
                            copy(WT[:, HI, b0:b0 + nb, c0:c0 + P], src).then_inc(b_tr_hi, 1)

                def store_outputs(gq):
                    act.wait_ge(pj_taken, SPARE + J_B + 6 + use["pv", gq] + 1 + 8 * h)
                    act.dma_start(o_sb_d[bass.ds(P * h, P), gq * BANK:(gq + 1) * BANK],
                                  oS[:, gq, :]).then_inc(ob_out[gq], 16)

                for i in range(SB_STEPS):
                    if 2 <= i < TB:
                        scores_ln(h, i)
                    elif i > TB and not last:
                        scores_ln(h + 1, i - TB - 1)
                    if i == TB:
                        take_rounds(sb_rounds(i))
                    if i == 0:
                        weights(h, 1)
                    elif 3 <= i <= TB:
                        weights(h, i - 1)
                    elif i == TB + 2 and not last:
                        weights(h + 1, 0)
                    for n, q in finished(extra, i):
                        if q < 4 and not last:
                            take_high(h + 1, 1 - par, q, n % 2)
                    if i != TB:
                        take_rounds(sb_rounds(i))
                    if i == 7:
                        store_outputs(0)
                store_outputs(1)

            for i in range(2):
                scores_ln(0, i)
            weights(0, 0)
            with act.Fori(0, SH // 2 - 1) as j:
                for par in range(2):
                    sb_head(2 * j + par, par, False)
            sb_head(SH - 2, 0, False)
            sb_head(SH - 1, 1, True)
            phase_end(act, act_phase, 5)

            for hf in range(NH):
                act.wait_ge(fin["A"][f"yio{hf}"], 16 * KD + 1)
            finish("B", N_B, J_FB, 6)

            def u_rms(b):
                act.wait_ge(pj_taken, SPARE + J_D + TB + b + 1)
                if b >= 1:
                    act.wait_ge(u_sq, b)
                inverse_rms(x1[:, b, :], D, b, D, u_sq, u_ln, u_rstd, b + 1, junkD[:, :])

            def take_u(b):
                for r in (2 * b, 2 * b + 1):
                    act.wait_ge(ut_full, r + 1)
                    copy(HT[:, HI, 4 * (r % 2):4 * (r % 2) + 4, b * P:(b + 1) * P],
                         ring[r % 4].rearrange("p (k n) -> p k n", k=4)).then_inc(ut_hi, 1)

            for b in range(TB):
                u_rms(b)
                if b >= 2:
                    take_u(b - 2)
            for b in range(TB - 2, TB):
                take_u(b)

            def final_rms(b):
                act.wait_ge(x2_ready, TB + b + 1)
                if b >= 1:
                    act.wait_ge(f_sq, b)
                inverse_rms(x1[:, b, :], D, b, D, f_sq, f_ln, f_rstd, b + 1, junkD[:, :])

            def store(b):
                act.wait_ge(f_ready, b + 1)
                act.dma_start(out_rows[b * P:(b + 1) * P, :], x1[:, b, :]).then_inc(out_done[0], 16)

            act.wait_ge(pj_taken, SPARE + J_D + 2 * TB)
            for q in range(2 * TB):
                if q >= TB + 1:
                    s.preload_act_table_set(EXP_LN)
                    final_rms(q - TB - 1)
                    if q >= TB + 2:
                        store(q - TB - 2)
                if q == 0 or q >= TB + 1:
                    s.preload_act_table_set(SIGMOID)
                act.wait_ge(d_full, 2 * TB + q + 1)
                if q >= 2:
                    act.wait_ge(x2_ready, q - 1)
                s.activation(sgD[:, q % 2, :], pj[q % 2][:, :], ACT.Sigmoid).then_inc(pj_taken, 1)
            s.preload_act_table_set(EXP_LN)
            store(TB - 2)
            final_rms(TB - 1)
            for ch in range(NH):
                c = slice(ch * BANK, (ch + 1) * BANK)
                act.wait_ge(f_ready, TB + ch)
                act.dma_start(out_rows[(TB - 1) * P:TB * P, c], x1[:, TB - 1, c]).then_inc(out_done[1], 16)
            act.wait_ge(out_done[0], 16 * (TB - 1))
            act.wait_ge(out_done[1], 16 * NH)

        @block.vector
        def _(dve):
            v = nc.vector
            v.sem_inc(attn_ready, 2)
            v.sem_inc(st_ready, 1)
            v.sem_inc(on_ready, 2)
            v.sem_inc(y_done, 2)
            v.sem_inc(b_tr_lo, 2)
            for br in "AB":
                v.sem_inc(fin[br]["oa_ready"], 4)
                v.sem_inc(fin[br]["ysum"], 2)
            v.sem_inc(fin["A"]["yio0"], 1)
            v.sem_inc(fin["A"]["yio1"], 1)

            def rest(out_, whole, hi):
                return v.tensor_tensor(out_, whole, hi.bitcast(F32), ALU.subtract)

            for r in range(TB // 2):
                dve.wait_ge(p_hi, r + 1)
                c = slice(2 * r * P, (2 * r + 2) * P)
                rest(pT[:, LO, :, c], ring[r].rearrange("p (k n) -> p k n", k=PK),
                     pT[:, HI, :, c]).then_inc(p_lo, 1)
                if r % 2:
                    ch = r // 2
                    c = slice(ch * BANK, (ch + 1) * BANK)
                    dve.wait_ge(wpe_hi, ch + 1)
                    rest(wpe[:, LO, 0, c], wpe_raw[:, 0, c], wpe[:, HI, 0, c]).then_inc(wpe_lo[ch], 1)
            dve.wait_ge(gain_in, 16)

            def rest_x(b):
                for r in (2 * b, 2 * b + 1):
                    dve.wait_ge(xt_hi, r + 1)
                    k, c = slice(4 * (r % 2), 4 * (r % 2) + 4), slice(b * P, (b + 1) * P)
                    rest(HT[:, LO, k, c], ring[r % 4].rearrange("p (k n) -> p k n", k=4),
                         HT[:, HI, k, c]).then_inc(xt_lo, 1)

            def norm_x(b):
                dve.wait_ge(x_rstd, b + 1)
                v.scalar_tensor_tensor(out=xin[:, b, :], in0=xin[:, b, :], scalar=rstd[:, b:b + 1],
                                       in1=gains[:, 0, :], op0=ALU.mult, op1=ALU.mult).then_inc(x_norm, 1)

            norm_x(0)
            for b in range(TB):
                if b < TB - 1:
                    norm_x(b + 1)
                dve.wait_ge(pe_full[1], b + 1)
                if b >= 4:
                    dve.wait_ge(pe_out[b % 4], 16 * (b // 4))
                v.tensor_copy(pes[b % 4][:, BANK:D], pj[1][:, :]).then_inc(pe_taken[1], 1)
                rest_x(b)
            phase_end(dve, dve_phase, 0)

            for i in range(4):
                dve.wait_ge(pe_out[i], 4 * TB)
            v.memset(newchunk[:, :], 1.0).then_inc(chunk_mask, 1)
            v.memset(attn[:, :, :], 0.0).then_inc(chunk_mask, 1)
            dve.wait_ge(chunk_mask, 2)
            v.memset(newchunk[:, :].rearrange("p (c t) -> p c t", t=CHUNK)[:, :, 0:1], 0.0).then_inc(chunk_mask, 1)
            dve.wait_ge(chunk_mask, 3)
            dve.wait_ge(params_in, 64)
            dve.wait_ge(const_ready, 17)
            tmp = [A_ke, A_qd]
            for h in range(GH):
                for hf in range(NH):
                    dve.wait_ge(y_abs, 2 * h + hf + 1)
                    v.tensor_scalar(Y[:, h, hf * BANK:(hf + 1) * BANK], trs[hf][:, :], balp[:, h:h + 1], 0.0,
                                    ALU.add, ALU.min).then_inc(y_min, 1)
                dve.wait_ge(y_min, 2 * h + 2)
                dve.wait_ge(y_ln, h + 1)
                v.tensor_tensor(Y[:, h, :], Y[:, h, :], tmp[h % 2][:, :], ALU.subtract).then_inc(y_ls, 1)
                dve.wait_ge(y_ls, h + 1)
                v.tensor_tensor_scan(Y[:, h, :], newchunk[:, :], Y[:, h, :], 0.0, ALU.mult, ALU.add).then_inc(y_cum, 1)
            dve.wait_ge(y_cum, GH)

            def chunks(a):
                return a.rearrange("p (c t) -> p c t", t=CHUNK)

            with dve.Fori(0, GH) as h:
                dve.wait_ge(o_full, 2 + 8 * h)
                yc = Y[:, bass.ds(h, 1), :].rearrange("p a (c t) -> p (a c) t", t=CHUNK)
                v.tensor_tensor(chunks(A_ke[:, :]), yc[:, :, CHUNK - 1:CHUNK].to_broadcast([P, T // CHUNK, CHUNK]),
                                yc, ALU.subtract).then_inc(dd_done, 1)

                def take_round(r, out_, hi):
                    dve.wait_ge(vk_hi, r + 1 + 6 * h)
                    rest(out_, vk_bank(r), hi).then_inc(vk_taken, 1)

                for r in range(4):
                    take_round(r, *[VN[a][:, 2 * r:2 * r + 2, :].rearrange("p b v -> p (b v)") for a in (LO, HI)])
                dve.wait_ge(e_done, 1 + 2 * h)
                ends = A_eb[:, :].rearrange("p (b c t) -> p b c t", c=2, t=CHUNK)
                e0, e1 = ends[:, :, 0, CHUNK - 1], ends[:, :, 1, CHUNK - 1]
                v.tensor_copy(two_c[:, :, 1], e0).then_inc(dec_part, 1)
                v.tensor_copy(two_k[:, :, 0], e1).then_inc(dec_part, 1)
                v.tensor_tensor(dec[:, :], e0, e1, ALU.mult).then_inc(dec_part, 1)
                dve.wait_ge(pj_taken, SPARE + J_A + 2 + 8 + 8 * h)
                dve.wait_ge(e_done, 2 + 2 * h)
                q_, k_ = qkv[:, 2, :], qkv[:, 3, :]
                dve.wait_ge(ke_done, h + 1)
                v.tensor_tensor(A_ke[:, :], k_, A_ke[:, :], ALU.mult).then_inc(prep, 1)
                v.scalar_tensor_tensor(out=A_qi[:, :], in0=q_, scalar=Q_SCALE, in1=A_enb[:, :], op0=ALU.mult,
                                       op1=ALU.mult).then_inc(prep, 1)
                v.tensor_tensor(A_kd[:, :], k_, A_enb[:, :], ALU.mult).then_inc(prep, 1)
                dve.wait_ge(prep, 3 + 5 * h)
                dve.wait_ge(dec_part, 3 + 3 * h)
                v.tensor_tensor(chunks(A_enb[:, :]), chunks(A_ke[:, :]),
                                two_k[:, :, :].rearrange("p b (c o) -> p (b c) o", o=1).to_broadcast(
                                    [P, T // CHUNK, CHUNK]), ALU.mult).then_inc(kS_ready, 1)
                v.scalar_tensor_tensor(out=A_qd[:, :], in0=q_, scalar=Q_SCALE, in1=A_eb[:, :], op0=ALU.mult,
                                       op1=ALU.mult).then_inc(prep, 1)
                v.tensor_tensor(A_ki[:, :], k_, A_eb[:, :], ALU.mult).then_inc(prep, 1)
                dve.wait_ge(prep, 5 + 5 * h)
                v.tensor_tensor(chunks(A_eb[:, :]), chunks(A_qd[:, :]),
                                two_c[:, :, :].rearrange("p b (c o) -> p (b c) o", o=1).to_broadcast(
                                    [P, T // CHUNK, CHUNK]), ALU.mult).then_inc(qS_part, 1)
                for r in range(4, 6):
                    take_round(r, *[KN[a][:, 4 * (r - 4):4 * (r - 4) + 4, :].rearrange("p b d -> p (b d)")
                                    for a in (LO, HI)])
                dve.wait_ge(qS_part, 1 + 2 * h)
                v.tensor_copy(qS[HI][:, :], A_eb[:, :]).then_inc(qS_part, 1)
                dve.wait_ge(qS_part, 2 + 2 * h)
                rest(qS[LO][:, :], A_eb[:, :], qS[HI][:, :]).then_inc(qS_ready, 1)

                def mask(b):
                    dve.wait_ge(s_full, b + 1 + 8 * h)
                    dve.wait_ge(o_full, b + 1 + 8 * h)
                    dve.wait_ge(attn_ready, b + 1 + 8 * h)
                    stand_alone(dve)
                    a, o = attn[:, b % 2, :], SBK[b % 2]
                    c = 4 * b + 32 * h
                    v.copy_predicated(a, m_past[:, :].bitcast(U32), o[:, 0:P]).then_inc(attn_part, 1)
                    dve.wait_ge(attn_part, c + 1)
                    stand_alone(dve)
                    v.copy_predicated(a, m_fut[:, :].bitcast(U32), o[:, P:2 * P]).then_inc(attn_part, 1)
                    dve.wait_ge(attn_part, c + 2)
                    stand_alone(dve)
                    v.copy_predicated(a, m_cross[:, :].bitcast(U32), o[:, 2 * P:3 * P]).then_inc(attn_part, 1)
                    dve.wait_ge(attn_part, c + 3)
                    v.tensor_copy(attn_s[:, b % 2, HI, :], a).then_inc(attn_part, 1)
                    dve.wait_ge(attn_part, c + 4)
                    rest(attn_s[:, b % 2, LO, :], a, attn_s[:, b % 2, HI, :]).then_inc(attn_ready, 1)

                def update_state(b):
                    dve.wait_ge(o_full, b + 3 + 8 * h)
                    dve.wait_ge(st_ready, b + 1 + 7 * h)
                    update = OBK[b % 2][:, DV:2 * DV]
                    if b == 0:
                        v.tensor_copy(St[:, 1, :], update).then_inc(st_part, 1)
                    else:
                        v.scalar_tensor_tensor(out=St[:, (b + 1) % 2, :], in0=St[:, b % 2, :], scalar=dec[:, b:b + 1],
                                               in1=update, op0=ALU.mult, op1=ALU.add).then_inc(st_part, 1)
                    i = (b + 1) % 2
                    dve.wait_ge(st_part, 2 * b + 1 + 14 * h)
                    v.tensor_copy(St_s[:, i, HI, :], St[:, i, :]).then_inc(st_part, 1)
                    dve.wait_ge(st_part, 2 * b + 2 + 14 * h)
                    rest(St_s[:, i, LO, :], St[:, i, :], St_s[:, i, HI, :]).then_inc(st_ready, 1)

                def norm(b):
                    dve.wait_ge(o_rstd, b + 1 + 8 * h)
                    dve.wait_ge(g_tr_full, (b + 1 if b < 2 else b + 7) + 14 * h)
                    v.tensor_scalar(on[:, b % 2, :], OBK[b % 2][:, 0:DV], rstd[:, b % 2:b % 2 + 1], None,
                                    ALU.mult).then_inc(on_ready, 1)

                mask(0)
                for b in range(TB):
                    if b < TB - 1:
                        mask(b + 1)
                    if b > 0:
                        norm(b - 1)
                    if b < TB - 1:
                        update_state(b)
                norm(TB - 1)
            phase_end(dve, dve_phase, 1)

            def finish(br, n0, j0, k0, stored):
                f = fin[br]
                for e_sem, count in stored:
                    dve.wait_ge(e_sem, count)
                with dve.Fori(0, 4) as i:
                    for t in range(4):
                        hf, slot = t % 2, t // 2
                        c = slice(hf * BANK, (hf + 1) * BANK)
                        g_ = sg[:, hf, :]
                        dve.wait_ge(f["sg_ready"], t + 1 + 4 * i)
                        if slot == 0:
                            v.tensor_tensor(g_, pj[hf][:, :], g_, ALU.mult).then_inc(pj_taken, 1)
                            dve.wait_ge(pj_taken, SPARE + j0 + hf + 1 + 2 * i)
                        else:
                            gate = early[br][:, bass.ds(i, 1), c].rearrange("p a t -> p (a t)")
                            v.tensor_tensor(g_, gate, g_, ALU.mult).then_inc(f["gated"], 1)
                            dve.wait_ge(f["gated"], hf + 1 + 2 * i)
                        dve.wait_ge(f[f"oin{slot}"], 16 + 16 * i)
                        v.tensor_tensor(g_, g_, oin[:, slot, c], ALU.mult).then_inc(f["og"], 1)
                        dve.wait_ge(f["og"], t + 1 + 4 * i)

                        def dst(part):
                            return OA[:, part, bass.ds(i + 4 * (1 - slot), 1), c].rearrange("p a t -> p (a t)")
                        v.tensor_copy(dst(HI), g_).then_inc(f["hi"], 1)
                        dve.wait_ge(f["hi"], t + 1 + 4 * i)
                        rest(dst(LO), g_, dst(HI)).then_inc(f["oa_ready"], 1)
                phase_end(dve, dve_phase, k0)
                phase_end(dve, dve_phase, k0 + 1)

                def merge(e, slot):
                    for hf in range(NH):
                        q = hf + 2 * e
                        c = slice(hf * BANK, (hf + 1) * BANK)
                        dve.wait_ge(q_full, 2 * (n0 + 2 * KD) + 5 + q)
                        y_ = ys[:, hf, :]
                        if br == "A":
                            dve.wait_ge(f[f"yio{hf}"], 1 + 16 * e)
                        m = SM[:, bass.ds(slot, 1), c].rearrange("p a t -> p (a t)")
                        v.tensor_tensor(y_, pj[hf][:, :], m, ALU.mult).then_inc(pj_taken, 1)
                        if br == "A":
                            continue
                        dve.wait_ge(pj_taken, SPARE + j0 + 24 + 1 + q)
                        dve.wait_ge(f[f"yio{hf}"], 16 + 16 * e)
                        v.tensor_tensor(y_, y_, yin[:, hf, :], ALU.add).then_inc(f["ysum"], 1)
                        dve.wait_ge(f["ysum"], 3 + q)

                        def dst(part):
                            return HT[:, part, bass.ds(e, 1), c].rearrange("p a t -> p (a t)")
                        v.tensor_copy(dst(HI), y_).then_inc(f["yhi"], 1)
                        dve.wait_ge(f["yhi"], 1 + q)
                        rest(dst(LO), y_, dst(HI)).then_inc(f["ylo"], 1)
                        dve.wait_ge(f["ylo"], 1 + q)

                for e in (0, 1):
                    merge(e, SM_SLOT[e])
                with dve.Fori(0, 2) as j:
                    for par in range(2):
                        merge(2 * j + par + 2, 2 * j + par)
                for e in (6, 7):
                    merge(e, SM_SLOT[e])
                phase_end(dve, dve_phase, k0 + 2)

            finish("A", N_A, J_FA, 2, [(oT_out, 16 * GH + 1)])

            def take_quantum(h, par, i, bank_):
                c, hf = divmod(i, 2)
                cols = slice(hf * BANK, (hf + 1) * BANK)
                if c == 2:
                    dve.wait_ge(q_full, 2 * N_FA + 5 + i + 6 * h)
                    v.tensor_copy(vT[:, cols], pj[bank_][:, :]).then_inc(pj_taken, 1)
                    return
                dve.wait_ge(b_hi, i + 1 + 4 * h)
                hi, lo = QK[:, par, c, HI, cols], QK[:, par, c, LO, cols]
                v.scalar_tensor_tensor(out=lo, in0=pj[bank_][:, :], scalar=Q_SCALE if c == 0 else 1.0,
                                       in1=hi.bitcast(F32), op0=ALU.mult, op1=ALU.subtract).then_inc(pj_taken, 1)

            for i in range(6):
                take_quantum(0, 0, i, i % 2)

            def softplus(h, i):
                w = (i + 1) * P
                c = i + 1 + 8 * h
                z, a = zs[i % 2][:, 0:w], T1[:, i % 2, 0:w]
                dve.wait_ge(z_ln, c)
                v.scalar_tensor_tensor(out=a, in0=z, scalar=0.0, in1=a, op0=ALU.max, op1=ALU.add).then_inc(sp, 1)
                dve.wait_ge(sp, c)
                v.tensor_tensor(T1[:, i % 2, i * P:w], T1[:, i % 2, i * P:w], before01[:, :],
                                ALU.mult).then_inc(spm, 1)

            def log_weights(h, i):
                w = (i + 1) * P
                c = i + 1 + 8 * h
                z, a, y = zs[i % 2][:, 0:w], T1[:, i % 2, 0:w], T2[i % 4][:, 0:w]
                dve.wait_ge(spm, c)
                v.tensor_tensor_scan(y[:, ::-1], a[:, ::-1], a[:, ::-1], 0.0, ALU.add, ALU.bypass).then_inc(cum, 1)
                dve.wait_ge(cum, c)
                v.tensor_tensor(y, z, y, ALU.subtract).then_inc(y_done, 1)
                dve.wait_ge(y_done, c + 2)
                v.tensor_tensor(y[:, i * P:w], y[:, i * P:w], before_cap[:, :], ALU.min).then_inc(ym, 1)

            def sb_head(h, par, last):
                extra = EXTRA_LAST if last else EXTRA

                def take_rounds(some):
                    for kind, r, j, b0, nb in some:
                        dve.wait_ge(b_tr_hi, r + 1 + SB_ROUNDS * h)
                        src = trs[r % 2][:, 0:nb * P].rearrange("p (b t) -> p b t", b=nb)
                        if kind == "v":
                            rest(VS[:, LO, b0:b0 + nb, :], src, VS[:, HI, b0:b0 + nb, :]).then_inc(b_tr_lo, 1)
                        else:
                            c0 = (j % 4) * P
                            rest(WT[:, LO, b0:b0 + nb, c0:c0 + P], src,
                                 WT[:, HI, b0:b0 + nb, c0:c0 + P]).then_inc(b_tr_lo, 1)

                def take_outputs(gq, bank_):
                    dve.wait_ge(pv_full, gq + 2 + 2 * h)
                    dve.wait_ge(ob_out[gq], 1 + 16 * h)
                    v.tensor_copy(oS[:, gq, :], pj[bank_][:, :]).then_inc(pj_taken, 1)

                def take_gate(i, bank_):
                    c, hf = divmod(i, 2)
                    dve.wait_ge(q_full, 2 * N_B + i + 5)
                    v.tensor_copy(graw[:, c, hf * BANK:(hf + 1) * BANK], pj[bank_][:, :]).then_inc(pj_taken, 1)

                for i in range(SB_STEPS):
                    scored = (h, i) if 2 <= i < TB else (h + 1, i - TB - 1) if i > TB and not last else None
                    if scored:
                        softplus(*scored)
                        if i in ROUNDS_EARLY:
                            take_rounds(sb_rounds(i))
                        if i not in TAKE_EARLY:
                            log_weights(*scored)
                    for n, q in finished(extra, i):
                        if last:
                            take_gate(q, n % 2)
                        else:
                            take_quantum(h + 1, 1 - par, q, n % 2)
                    if scored and i in TAKE_EARLY:
                        log_weights(*scored)
                    if ("pv", 0) in extra[i]:
                        take_outputs(0, uses(extra)["pv", 0] % 2)
                    if i not in ROUNDS_EARLY:
                        take_rounds(sb_rounds(i))
                take_outputs(1, uses(extra)["pv", 1] % 2)

            for hf in range(NH):
                dve.wait_ge(fin["A"][f"yio{hf}"], 16 * KD + 1)
            for i in range(2):
                softplus(0, i)
                log_weights(0, i)
            with dve.Fori(0, SH // 2 - 1) as j:
                for par in range(2):
                    sb_head(2 * j + par, par, False)
            sb_head(SH - 2, 0, False)
            sb_head(SH - 1, 1, True)
            phase_end(dve, dve_phase, 5)

            finish("B", N_B, J_FB, 6, [(ob_out[0], 16 * SH + 1), (ob_out[1], 16 * SH + 1)])

            dve.wait_ge(gain2_in, 32)

            def add_x(q):
                ch, b = divmod(q, TB)
                c = slice(ch * BANK, (ch + 1) * BANK)
                dve.wait_ge(d_full, q + 1)
                if ch == 0:
                    dve.wait_ge(x2_in[b], 16)
                v.tensor_tensor(x1[:, b, c], x1[:, b, c], pj[q % 2][:, :], ALU.add).then_inc(pj_taken, 1)

            def norm_u(b):
                dve.wait_ge(u_rstd, b + 1)
                if b >= 2:
                    dve.wait_ge(ut_full, 2 * b - 2)
                v.scalar_tensor_tensor(out=u[:, b % 2, :], in0=x1[:, b, :], scalar=rstd[:, b:b + 1],
                                       in1=gains[:, 0, :], op0=ALU.mult, op1=ALU.mult).then_inc(u_ready, 1)

            def rest_u(b):
                for r in (2 * b, 2 * b + 1):
                    dve.wait_ge(ut_hi, r + 1)
                    k, c = slice(4 * (r % 2), 4 * (r % 2) + 4), slice(b * P, (b + 1) * P)
                    rest(HT[:, LO, k, c], ring[r % 4].rearrange("p (k n) -> p k n", k=4),
                         HT[:, HI, k, c]).then_inc(ut_lo, 1)

            for q in range(2 * TB):
                add_x(q)
                if q >= TB + 1:
                    norm_u(q - TB - 1)
                if q >= TB + 2:
                    rest_u(q - TB - 2)
            norm_u(TB - 1)
            rest_u(TB - 2)
            rest_u(TB - 1)

            def norm_out(b, c):
                dve.wait_ge(f_rstd, b + 1)
                v.scalar_tensor_tensor(out=x1[:, b, c], in0=x1[:, b, c], scalar=rstd[:, b:b + 1],
                                       in1=gains[:, 1, c], op0=ALU.mult, op1=ALU.mult).then_inc(f_ready, 1)

            for q in range(2 * TB):
                ch, b = divmod(q, TB)
                c = slice(ch * BANK, (ch + 1) * BANK)
                if q >= TB + 1:
                    norm_out(q - TB - 1, slice(0, D))
                dve.wait_ge(pj_taken, SPARE + J_D + 2 * TB + q + 1)
                dve.wait_ge(pe_in[q % 2], 16 * (q // 2 + 1))
                v.tensor_tensor(sgD[:, q % 2, :], sgD[:, q % 2, :], pin2[:, q % 2, :], ALU.mult).then_inc(gate_used, 1)
                dve.wait_ge(gate_used, q + 1)
                v.tensor_tensor(x1[:, b, c], x1[:, b, c], sgD[:, q % 2, :], ALU.add).then_inc(x2_ready, 1)
            for ch in range(NH):
                norm_out(TB - 1, slice(ch * BANK, (ch + 1) * BANK))


_INS = ["x", "p", "g_mix", "w_in", "w_alpha", "b_alpha", "g_gla_out", "w_out_gla", "w_out_sb", "w_out", "g_ple",
        "w_ple_gate", "w_ple", "g_final"]


def kernel(**inputs):
    import numpy as _np
    import concourse.bacc as _bacc
    from concourse import mybir as _mybir
    from concourse.bass_utils import run_bass_kernel_spmd as _run

    nc = _bacc.Bacc("TRN2", target_bir_lowering=False, num_devices=1)
    arrays, args = {}, []
    for name in _INS:
        a = _np.ascontiguousarray(inputs[name])
        arrays[f"in_{name}_dram"] = a
        args.append(nc.dram_tensor(f"in_{name}_dram", a.shape, _mybir.dt.from_np(a.dtype), kind="ExternalInput").ap())
    out = nc.dram_tensor("out_0_dram", inputs["x"].shape, _mybir.dt.from_np(_np.dtype("float32")),
                         kind="ExternalOutput").ap()
    hybrid_block(nc, *args, out)
    r = _run(nc, [arrays], core_ids=[0])
    return r.results[0]["out_0_dram"]
```
